# Optimizing a Trainium2 kernel written in Bass

```python
import jax, jax.numpy as jnp
from jax import lax
import numpy as np
import math

D_MODEL = 2048
BATCH = 1
SEQ = 256
DEPTH = 1

LRU_WIDTH = D_MODEL
LRU_BLOCKS = 16
LRU_BLOCK_DIM = LRU_WIDTH // LRU_BLOCKS
LRU_C = 8.0
CONV_WIDTH = 4
CONV_LEFT = 2
N_HEADS = 16
N_KV_HEADS = 4
HEAD_DIM = 128
GROUP = N_HEADS // N_KV_HEADS
ATTN_WIDTH = N_HEADS * HEAD_DIM
KV_WIDTH = N_KV_HEADS * HEAD_DIM
WINDOW = 128
BLOCK = 128
ROPE_THETA = 500000.0
ROT_DIM = HEAD_DIM // 4
NORM_EPS = 1e-6
IN_SPLITS = (LRU_WIDTH, LRU_WIDTH, ATTN_WIDTH, KV_WIDTH, KV_WIDTH, ATTN_WIDTH, D_MODEL, D_MODEL)
IN_WIDTH = sum(IN_SPLITS)


def rms_norm(x, w):
    xf = x.astype(jnp.float32)
    y = xf * lax.rsqrt(jnp.mean(xf * xf, axis=-1, keepdims=True) + NORM_EPS)
    return (y * w.astype(jnp.float32)).astype(x.dtype)

def centred_depthwise_conv(u, w, b):
    s = u.shape[1]
    up = jnp.pad(u, ((0, 0), (CONV_LEFT, CONV_WIDTH - 1 - CONV_LEFT), (0, 0)))
    y = b
    for tap in range(CONV_WIDTH):
        y = y + up[:, tap:tap + s] * w[tap]
    return y

def _linear_combine(e1, e2):
    a1, b1 = e1
    a2, b2 = e2
    return a1 * a2, a2 * b1 + b2

def rg_lru(u, w_r, b_r, w_i, b_i, lam, reverse):
    bsz, s, _ = u.shape
    ub = u.reshape(bsz, s, LRU_BLOCKS, LRU_BLOCK_DIM)
    gate_r = jax.nn.sigmoid(jnp.einsum('bsni,nij->bsnj', ub, w_r).reshape(bsz, s, LRU_WIDTH) + b_r)
    gate_i = jax.nn.sigmoid(jnp.einsum('bsni,nij->bsnj', ub, w_i).reshape(bsz, s, LRU_WIDTH) + b_i)
    log_a = -LRU_C * gate_r.astype(jnp.float32) * jax.nn.softplus(-lam.astype(jnp.float32))
    a = jnp.exp(log_a)
    in_scale = jnp.sqrt(-jnp.expm1(2.0 * log_a))
    b = in_scale * (gate_i * u).astype(jnp.float32)
    _, h = lax.associative_scan(_linear_combine, (a, b), axis=1, reverse=reverse)
    return h

def partial_rope(t, cos, sin):
    half = ROT_DIM // 2
    tf = t[..., :ROT_DIM].astype(jnp.float32)
    t1, t2 = tf[..., :half], tf[..., half:]
    c = cos[None, :, None, :]
    sn = sin[None, :, None, :]
    rot = jnp.concatenate([t1 * c - t2 * sn, t2 * c + t1 * sn], axis=-1).astype(t.dtype)
    return jnp.concatenate([rot, t[..., ROT_DIM:]], axis=-1)

def windowed_gqa(q, k, v, sink):
    bsz, s = q.shape[:2]
    nb = s // BLOCK
    qb = q.reshape(bsz, nb, BLOCK, N_KV_HEADS, GROUP, HEAD_DIM)

    def band(t):
        tp = jnp.pad(t, ((0, 0), (BLOCK, BLOCK), (0, 0), (0, 0)))
        tp = tp.reshape(bsz, nb + 2, BLOCK, N_KV_HEADS, HEAD_DIM)
        return jnp.concatenate([tp[:, :-2], tp[:, 1:-1], tp[:, 2:]], axis=2)

    kw, vw = band(k), band(v)
    scores = jnp.einsum('bnqkgd,bnskd->bnkgqs', qb, kw).astype(jnp.float32) * (HEAD_DIM ** -0.5)
    q_idx = jnp.arange(BLOCK)[:, None]
    s_idx = jnp.arange(3 * BLOCK)[None, :]
    band_ok = jnp.abs(s_idx - BLOCK - q_idx) <= WINDOW
    key_pos = (jnp.arange(nb)[:, None] - 1) * BLOCK + jnp.arange(3 * BLOCK)[None, :]
    in_range = (key_pos >= 0) & (key_pos < s)
    mask = band_ok[None] & in_range[:, None, :]
    scores = jnp.where(mask[None, :, None, None], scores, -1e30)
    sink_l = sink.astype(jnp.float32).reshape(1, 1, N_KV_HEADS, GROUP, 1, 1)
    m = jnp.maximum(scores.max(axis=-1, keepdims=True), sink_l)
    e = jnp.exp(scores - m)
    p = e / (e.sum(axis=-1, keepdims=True) + jnp.exp(sink_l - m))
    out = jnp.einsum('bnkgqs,bnskd->bnqkgd', p.astype(v.dtype), vw)
    return out.reshape(bsz, s, ATTN_WIDTH)

def first_inputs(seed: int = 0) -> dict:
    key = jax.random.key(seed)
    ks = jax.random.split(key, 16)

    def nrm(k, shape, fan_in):
        return jax.random.normal(k, shape, jnp.float32) * (fan_in ** -0.5)

    L = DEPTH
    x = jax.random.normal(ks[0], (BATCH, SEQ, D_MODEL), jnp.float32)
    norm_pre_w = 1.0 + 0.02 * jax.random.normal(ks[1], (L, D_MODEL), jnp.float32)
    w_in = nrm(ks[2], (L, D_MODEL, IN_WIDTH), D_MODEL)
    conv_w = nrm(ks[3], (L, CONV_WIDTH, LRU_WIDTH), CONV_WIDTH)
    conv_b = 0.01 * jax.random.normal(ks[4], (L, LRU_WIDTH), jnp.float32)
    lru_w_r = nrm(ks[5], (L, 2, LRU_BLOCKS, LRU_BLOCK_DIM, LRU_BLOCK_DIM), LRU_BLOCK_DIM)
    lru_b_r = 0.01 * jax.random.normal(ks[6], (L, 2, LRU_WIDTH), jnp.float32)
    lru_w_i = nrm(ks[7], (L, 2, LRU_BLOCKS, LRU_BLOCK_DIM, LRU_BLOCK_DIM), LRU_BLOCK_DIM)
    lru_b_i = 0.01 * jax.random.normal(ks[8], (L, 2, LRU_WIDTH), jnp.float32)
    a_c = jax.random.uniform(ks[9], (L, 2, LRU_WIDTH), jnp.float32, minval=0.9, maxval=0.999)
    sig = a_c ** (1.0 / LRU_C)
    lru_lambda = jnp.log(sig) - jnp.log1p(-sig)
    attn_sink = jax.random.normal(ks[10], (L, N_HEADS), jnp.float32)
    w_proj_a = nrm(ks[11], (L, LRU_WIDTH, D_MODEL), LRU_WIDTH)
    w_proj_b = nrm(ks[12], (L, ATTN_WIDTH, D_MODEL), ATTN_WIDTH)
    w_out = nrm(ks[13], (L, D_MODEL, D_MODEL), D_MODEL)
    norm_post_w = 1.0 + 0.02 * jax.random.normal(ks[14], (L, D_MODEL), jnp.float32)
    return {'x': x, 'norm_pre_w': norm_pre_w, 'w_in': w_in, 'conv_w': conv_w, 'conv_b': conv_b,
            'lru_w_r': lru_w_r, 'lru_b_r': lru_b_r, 'lru_w_i': lru_w_i, 'lru_b_i': lru_b_i,
            'lru_lambda': lru_lambda, 'attn_sink': attn_sink, 'w_proj_a': w_proj_a,
            'w_proj_b': w_proj_b, 'w_out': w_out, 'norm_post_w': norm_post_w}

def first_block(x, norm_pre_w, w_in, conv_w, conv_b, lru_w_r, lru_b_r, lru_w_i, lru_b_i,
              lru_lambda, attn_sink, w_proj_a, w_proj_b, w_out, norm_post_w):
    bsz, s, _ = x.shape
    pos = jnp.arange(s, dtype=jnp.float32)
    inv_freq = ROPE_THETA ** (-jnp.arange(0, ROT_DIM, 2, dtype=jnp.float32) / ROT_DIM)
    ang = pos[:, None] * inv_freq[None, :]
    cos, sin = jnp.cos(ang), jnp.sin(ang)
    split_at = np.cumsum(IN_SPLITS)[:-1].tolist()
    for l in range(DEPTH):
        xn = rms_norm(x, norm_pre_w[l])
        z = xn @ w_in[l]
        u_lru, g_lru, q, k, v, g_attn, m_lru, m_attn = jnp.split(z, split_at, axis=-1)
        u = centred_depthwise_conv(u_lru, conv_w[l], conv_b[l])
        h = (rg_lru(u, lru_w_r[l, 0], lru_b_r[l, 0], lru_w_i[l, 0], lru_b_i[l, 0], lru_lambda[l, 0], False)
             + rg_lru(u, lru_w_r[l, 1], lru_b_r[l, 1], lru_w_i[l, 1], lru_b_i[l, 1], lru_lambda[l, 1], True))
        y_a = h.astype(x.dtype) * jax.nn.silu(g_lru)
        q = partial_rope(q.reshape(bsz, s, N_HEADS, HEAD_DIM), cos, sin)
        k = partial_rope(k.reshape(bsz, s, N_KV_HEADS, HEAD_DIM), cos, sin)
        v = v.reshape(bsz, s, N_KV_HEADS, HEAD_DIM)
        y_b = windowed_gqa(q, k, v, attn_sink[l]) * jax.nn.silu(g_attn)
        merged = (jax.nn.sigmoid(m_lru) * (y_a @ w_proj_a[l])
                  + jax.nn.sigmoid(m_attn) * (y_b @ w_proj_b[l]))
        x = x + rms_norm(merged @ w_out[l], norm_post_w[l])
    return x


DEPTH_2 = 2

MIX_WIDTH = D_MODEL
A_HEAD_DIM = 64
A_WIDTH = 3 * D_MODEL // 8
A_Q_HEADS = A_WIDTH // A_HEAD_DIM
A_KV_HEADS = A_Q_HEADS // 3
A_GROUP = A_Q_HEADS // A_KV_HEADS
A_KV_WIDTH = A_KV_HEADS * A_HEAD_DIM
ATTN_BLOCK = 128
ROT_DIM_2 = A_HEAD_DIM // 4
B_WIDTH = D_MODEL // 4
B_CONV_WIDTH = 31
C_HEAD_DIM = 128
C_HEADS = (MIX_WIDTH - A_WIDTH - B_WIDTH) // C_HEAD_DIM
C_WIDTH = C_HEADS * C_HEAD_DIM
C_CONV_WIDTH = 4
CHUNK = 64

EPS = 1e-6
MAX_POS_OFFSET = 4096

COL_SPLITS = (A_WIDTH, A_KV_WIDTH, A_KV_WIDTH, A_WIDTH,
              2 * B_WIDTH, B_WIDTH,
              3 * C_WIDTH, C_HEADS, C_HEADS, C_WIDTH)
IN_COLS = sum(COL_SPLITS)


def _split_cols(p):
    idx = []
    s = 0
    for n in COL_SPLITS[:-1]:
        s += n
        idx.append(s)
    return jnp.split(p, idx, axis=-1)

def rms_norm_2(x, w):
    x32 = x.astype(jnp.float32)
    y = x32 * lax.rsqrt(jnp.mean(x32 * x32, axis=-1, keepdims=True) + EPS)
    return (y * w.astype(jnp.float32)).astype(x.dtype)

def layer_norm(x, w, b):
    x32 = x.astype(jnp.float32)
    mu = jnp.mean(x32, axis=-1, keepdims=True)
    var = jnp.mean(jnp.square(x32 - mu), axis=-1, keepdims=True)
    y = (x32 - mu) * lax.rsqrt(var + EPS)
    return (y * w.astype(jnp.float32) + b.astype(jnp.float32)).astype(x.dtype)

def l2_norm(x):
    return x * lax.rsqrt(jnp.sum(x * x, axis=-1, keepdims=True) + EPS)

def causal_depthwise_conv(x, w):
    K, C = w.shape
    return lax.conv_general_dilated(
        x, w[:, None, :].astype(x.dtype), window_strides=(1,), padding=[(K - 1, 0)],
        dimension_numbers=('NWC', 'WIO', 'NWC'), feature_group_count=C)

def rope_tables(positions):
    inv_freq = ROPE_THETA ** (-jnp.arange(0, ROT_DIM_2, 2, dtype=jnp.float32) / ROT_DIM_2)
    ang = positions.astype(jnp.float32)[..., None] * inv_freq
    return jnp.cos(ang)[:, :, None, :], jnp.sin(ang)[:, :, None, :]

def apply_partial_rope(x, cos, sin):
    half = ROT_DIM_2 // 2
    x1 = x[..., :half].astype(jnp.float32)
    x2 = x[..., half:ROT_DIM_2].astype(jnp.float32)
    rot = jnp.concatenate([x1 * cos - x2 * sin, x2 * cos + x1 * sin], axis=-1)
    return jnp.concatenate([rot.astype(x.dtype), x[..., ROT_DIM_2:]], axis=-1)

def sliding_window_sink_attention(q, k, v, sinks):
    bsz, T = q.shape[0], q.shape[1]
    nb = T // ATTN_BLOCK
    qb = q.reshape(bsz, nb, ATTN_BLOCK, A_KV_HEADS, A_GROUP, A_HEAD_DIM)
    kb = k.reshape(bsz, nb, ATTN_BLOCK, A_KV_HEADS, A_HEAD_DIM)
    vb = v.reshape(bsz, nb, ATTN_BLOCK, A_KV_HEADS, A_HEAD_DIM)
    prev = lambda t: jnp.concatenate([jnp.zeros_like(t[:, :1]), t[:, :-1]], axis=1)
    kk = jnp.concatenate([prev(kb), kb], axis=2)
    vv = jnp.concatenate([prev(vb), vb], axis=2)
    s = jnp.einsum('bnqhgd,bnkhd->bnhgqk', qb, kk).astype(jnp.float32) * (A_HEAD_DIM ** -0.5)
    qi = jnp.arange(ATTN_BLOCK)[:, None]
    kj = jnp.arange(2 * ATTN_BLOCK)[None, :]
    dist = qi + ATTN_BLOCK - kj
    band = (dist >= 0) & (dist < WINDOW)
    not_pad = (jnp.arange(nb)[:, None, None] > 0) | (kj[None] >= ATTN_BLOCK)
    valid = band[None] & not_pad
    s = jnp.where(valid[None, :, None, None], s, -jnp.inf)
    sink = sinks.reshape(A_KV_HEADS, A_GROUP).astype(jnp.float32)[None, None, :, :, None, None]
    sink = jnp.broadcast_to(sink, s.shape[:-1] + (1,))
    p = jax.nn.softmax(jnp.concatenate([s, sink], axis=-1), axis=-1)[..., :-1]
    o = jnp.einsum('bnhgqk,bnkhd->bnqhgd', p.astype(v.dtype), vv)
    return o.reshape(bsz, T, A_Q_HEADS * A_HEAD_DIM)

def conformer_conv_module(u, conv_w, conv_b, ln_w, ln_b, pw_w, pw_b):
    a, gt = jnp.split(u, 2, axis=-1)
    h = a * jax.nn.sigmoid(gt)
    h = causal_depthwise_conv(h, conv_w) + conv_b.astype(h.dtype)
    h = jax.nn.silu(layer_norm(h, ln_w, ln_b))
    return h @ pw_w + pw_b

def gated_delta_rule_chunked(q, k, v, g, beta):
    bsz, T, H, Dk = q.shape
    Dv = v.shape[-1]
    n = T // CHUNK
    q = q * (Dk ** -0.5)

    def to_chunks(t):
        return t.reshape(bsz, n, CHUNK, H, t.shape[-1]).transpose(0, 1, 3, 2, 4)

    qc, kc, vc = to_chunks(q), to_chunks(k), to_chunks(v)
    bc = beta.reshape(bsz, n, CHUNK, H).transpose(0, 1, 3, 2)
    gc = jnp.cumsum(g.reshape(bsz, n, CHUNK, H).transpose(0, 1, 3, 2), axis=-1)
    idx = jnp.arange(CHUNK)
    incl = idx[:, None] >= idx[None, :]
    strict = idx[:, None] > idx[None, :]
    decay = jnp.exp(jnp.where(incl, gc[..., :, None] - gc[..., None, :], -jnp.inf))
    kb = kc * bc[..., None]
    lower = jnp.where(strict, jnp.einsum('bnhid,bnhjd->bnhij', kb, kc) * decay, 0.0)
    eye = jnp.eye(CHUNK, dtype=lower.dtype)
    rhs = jnp.concatenate([vc * bc[..., None], kb * jnp.exp(gc)[..., None]], axis=-1)
    sol = lax.linalg.triangular_solve(lower + eye, rhs, left_side=True, lower=True,
                                      unit_diagonal=True)
    u, w = sol[..., :Dv], sol[..., Dv:]
    intra = jnp.where(incl, jnp.einsum('bnhid,bnhjd->bnhij', qc, kc) * decay, 0.0)

    def step(S, xs):
        q_i, k_i, u_i, w_i, g_i, a_i = xs
        v_new = u_i - jnp.einsum('bhck,bhkv->bhcv', w_i, S)
        o_i = (jnp.einsum('bhck,bhkv->bhcv', q_i * jnp.exp(g_i)[..., None], S)
               + jnp.einsum('bhij,bhjv->bhiv', a_i, v_new))
        g_last = g_i[..., -1:]
        S = (S * jnp.exp(g_last)[..., None]
             + jnp.einsum('bhck,bhcv->bhkv', k_i * jnp.exp(g_last - g_i)[..., None], v_new))
        return S, o_i

    S0 = jnp.zeros((bsz, H, Dk, Dv), q.dtype)
    xs = tuple(jnp.moveaxis(t, 1, 0) for t in (qc, kc, u, w, gc, intra))
    _, o = lax.scan(step, S0, xs)
    return o.transpose(1, 0, 3, 2, 4).reshape(bsz, T, H, Dv)

def gated_deltanet(qkv_raw, b_raw, a_raw, conv_w, a_log, dt_bias):
    bsz, T = qkv_raw.shape[0], qkv_raw.shape[1]
    qkv = jax.nn.silu(causal_depthwise_conv(qkv_raw, conv_w)).astype(jnp.float32)
    q, k, v = jnp.split(qkv, 3, axis=-1)
    q = l2_norm(q.reshape(bsz, T, C_HEADS, C_HEAD_DIM))
    k = l2_norm(k.reshape(bsz, T, C_HEADS, C_HEAD_DIM))
    v = v.reshape(bsz, T, C_HEADS, C_HEAD_DIM)
    beta = jax.nn.sigmoid(b_raw.astype(jnp.float32))
    g = -jnp.exp(a_log.astype(jnp.float32)) * jax.nn.softplus(
        a_raw.astype(jnp.float32) + dt_bias.astype(jnp.float32))
    return gated_delta_rule_chunked(q, k, v, g, beta)

def second_inputs(seed: int = 0) -> dict:
    key = jax.random.key(seed)
    ks = jax.random.split(key, 24)
    nrm = jax.random.normal
    x = nrm(ks[0], (BATCH, SEQ, D_MODEL), jnp.float32)
    offset = jax.random.randint(ks[1], (BATCH, 1), 0, MAX_POS_OFFSET, dtype=jnp.int32)
    positions = (offset + jnp.arange(SEQ, dtype=jnp.int32)[None, :]).astype(jnp.int32)
    norm_w = 1.0 + 0.02 * nrm(ks[2], (DEPTH_2, D_MODEL))
    w_in = nrm(ks[3], (DEPTH_2, D_MODEL, IN_COLS)) * D_MODEL ** -0.5
    q_norm_w = 1.0 + 0.02 * nrm(ks[4], (DEPTH_2, A_HEAD_DIM))
    k_norm_w = 1.0 + 0.02 * nrm(ks[5], (DEPTH_2, A_HEAD_DIM))
    sinks = nrm(ks[6], (DEPTH_2, A_Q_HEADS))
    b_conv_w = nrm(ks[7], (DEPTH_2, B_CONV_WIDTH, B_WIDTH)) * B_CONV_WIDTH ** -0.5
    b_conv_b = 0.02 * nrm(ks[8], (DEPTH_2, B_WIDTH))
    b_ln_w = 1.0 + 0.02 * nrm(ks[9], (DEPTH_2, B_WIDTH))
    b_ln_b = 0.02 * nrm(ks[10], (DEPTH_2, B_WIDTH))
    b_pw_w = nrm(ks[11], (DEPTH_2, B_WIDTH, B_WIDTH)) * B_WIDTH ** -0.5
    b_pw_b = 0.02 * nrm(ks[12], (DEPTH_2, B_WIDTH))
    c_conv_w = nrm(ks[13], (DEPTH_2, C_CONV_WIDTH, 3 * C_WIDTH)) * C_CONV_WIDTH ** -0.5
    c_a_log = jnp.log(jax.random.uniform(ks[14], (DEPTH_2, C_HEADS), minval=1.0, maxval=16.0))
    dt = jnp.exp(jax.random.uniform(ks[15], (DEPTH_2, C_HEADS),
                                    minval=math.log(1e-3), maxval=math.log(1e-1)))
    c_dt_bias = dt + jnp.log(-jnp.expm1(-dt))
    c_onorm_w = 1.0 + 0.02 * nrm(ks[16], (DEPTH_2, C_HEAD_DIM))
    w_out = nrm(ks[17], (DEPTH_2, MIX_WIDTH, D_MODEL)) * MIX_WIDTH ** -0.5
    return {"x": x, "positions": positions, "norm_w": norm_w, "w_in": w_in,
            "q_norm_w": q_norm_w, "k_norm_w": k_norm_w, "sinks": sinks,
            "b_conv_w": b_conv_w, "b_conv_b": b_conv_b, "b_ln_w": b_ln_w,
            "b_ln_b": b_ln_b, "b_pw_w": b_pw_w, "b_pw_b": b_pw_b,
            "c_conv_w": c_conv_w, "c_a_log": c_a_log, "c_dt_bias": c_dt_bias,
            "c_onorm_w": c_onorm_w, "w_out": w_out}

def second_block(x, positions, norm_w, w_in, q_norm_w, k_norm_w, sinks, b_conv_w, b_conv_b,
              b_ln_w, b_ln_b, b_pw_w, b_pw_b, c_conv_w, c_a_log, c_dt_bias, c_onorm_w,
              w_out):
    bsz, T = x.shape[0], x.shape[1]
    cos, sin = rope_tables(positions)
    for l in range(DEPTH_2):
        h = rms_norm_2(x, norm_w[l])
        p = h @ w_in[l]
        qa, ka, va, za, ub, zb, qkv_c, b_c, a_c, zc = _split_cols(p)
        qa = apply_partial_rope(rms_norm_2(qa.reshape(bsz, T, A_Q_HEADS, A_HEAD_DIM), q_norm_w[l]), cos, sin)
        ka = apply_partial_rope(rms_norm_2(ka.reshape(bsz, T, A_KV_HEADS, A_HEAD_DIM), k_norm_w[l]), cos, sin)
        va = va.reshape(bsz, T, A_KV_HEADS, A_HEAD_DIM)
        oa = sliding_window_sink_attention(qa, ka, va, sinks[l]) * jax.nn.silu(za)
        ob = conformer_conv_module(ub, b_conv_w[l], b_conv_b[l], b_ln_w[l], b_ln_b[l],
                                   b_pw_w[l], b_pw_b[l]) * jax.nn.silu(zb)
        oc = gated_deltanet(qkv_c, b_c, a_c, c_conv_w[l], c_a_log[l], c_dt_bias[l]).astype(x.dtype)
        oc = rms_norm_2(oc, c_onorm_w[l]) * jax.nn.silu(zc.reshape(bsz, T, C_HEADS, C_HEAD_DIM))
        oc = oc.reshape(bsz, T, C_WIDTH)
        y = jnp.concatenate([oa, ob, oc], axis=-1)
        x = x + y @ w_out[l]
    return x


def setup_inputs(seed=0):
    out = dict(first_inputs(seed))
    for name, value in second_inputs(seed + 1).items():
        if name != "x":
            out[name + "_2"] = value
    return out


def reference(
    x, norm_pre_w, w_in, conv_w, conv_b, lru_w_r, lru_b_r, lru_w_i, lru_b_i, lru_lambda,
    attn_sink, w_proj_a, w_proj_b, w_out, norm_post_w, positions_2, norm_w_2, w_in_2,
    q_norm_w_2, k_norm_w_2, sinks_2, b_conv_w_2, b_conv_b_2, b_ln_w_2, b_ln_b_2, b_pw_w_2,
    b_pw_b_2, c_conv_w_2, c_a_log_2, c_dt_bias_2, c_onorm_w_2, w_out_2,
):
    x = first_block(
        x, norm_pre_w, w_in, conv_w, conv_b, lru_w_r, lru_b_r, lru_w_i, lru_b_i, lru_lambda,
        attn_sink, w_proj_a, w_proj_b, w_out, norm_post_w,
    )
    return second_block(
        x, positions_2, norm_w_2, w_in_2, q_norm_w_2, k_norm_w_2, sinks_2, b_conv_w_2,
        b_conv_b_2, b_ln_w_2, b_ln_b_2, b_pw_w_2, b_pw_b_2, c_conv_w_2, c_a_log_2, c_dt_bias_2,
        c_onorm_w_2, w_out_2,
    )


_drawn_inputs = setup_inputs


def setup_inputs(seed=0):
    import zlib

    import numpy as np

    out = dict(_drawn_inputs(seed))
    spreads = {}
    factors = {'lru_b_r': 8.0,
     'lru_b_i': 8.0,
     'attn_sink': 8.0,
     'norm_post_w': 3.465,
     'norm_w_2': 4.269,
     'q_norm_w_2': 8.0,
     'k_norm_w_2': 8.0,
     'sinks_2': 5.041,
     'b_conv_b_2': 7.038,
     'b_ln_w_2': 8.0,
     'b_ln_b_2': 8.0,
     'b_pw_b_2': 8.0,
     'c_onorm_w_2': 7.333}
    for name, (base, spread) in spreads.items():
        noise = np.random.default_rng([zlib.crc32(name.encode()), seed]).standard_normal(out[name].shape)
        drawn = base * np.exp(spread * noise) if base else spread * noise
        out[name] = __import__('jax').numpy.asarray(drawn.astype(out[name].dtype))
    for name, factor in factors.items():
        out[name] = (out[name] * factor).astype(out[name].dtype)
    return out
```

```python
import math
from collections import namedtuple
from contextlib import ExitStack, contextmanager

import numpy as np

import concourse.bass as bass
from concourse import mybir

F32 = mybir.dt.float32
F32R = mybir.dt.float32r
I32 = mybir.dt.int32
ACT = mybir.ActivationFunctionType
ALU = mybir.AluOpType
AX_X = mybir.AxisListType.X

P = 128
D = 2048
T = 256
KT = D // P
CHUNK_COLS = 256
SLOT_K = KT // 2
SLOTS = 4
RAW = 2
NORM_EPS = 1e-6
NEG = -1e30
ROPE_THETA = 500000.0

LRU_PASSES = KT // 2
KV_HEADS_1, HEAD_DIM_1, ROT_1 = 4, 128, 32
LAYERS = 2
HEAD_DIM_2, HEADS_2, ROT_2 = 64, 12, 16
B_TILES = 4
TAPS_B = 31
C_HEADS, C_DIM, CHUNK = 6, 128, 64
TAPS_C = 4

SLOT_LRU = 0
SLOT_MERGE_A = SLOT_LRU + 4 * LRU_PASSES
SLOT_ATT_1 = SLOT_MERGE_A + 4 * (KT // 2)
SLOT_MERGE_B = SLOT_ATT_1 + 4 * 2 + 4 * (KT // 2)
SLOT_OUT_1 = SLOT_MERGE_B + 4 * (KT // 2)
SLOTS_1 = SLOT_OUT_1 + 2 * (KT // 2)
SLOT_ATT_2 = 0
SLOT_CONV_2 = SLOT_ATT_2 + 4 + 4 * 3
SLOT_DELTA_2 = SLOT_CONV_2 + 4 * 3
SLOT_OUT_2 = SLOT_DELTA_2 + 4 * C_HEADS
SLOTS_2 = SLOT_OUT_2 + 2 * (KT // 2)

P1_NORM, P1_CONV, P1_CONVB = 0, 16, 80
P1_BR, P1_BI, P1_LAM, P1_POST = 96, 128, 160, 192
P1_COLS = 208
P2_NORM, P2_QN, P2_KN, P2_ONORM = 0, 16, 17, 18
P2_BCONV, P2_BCONVB, P2_LNW, P2_LNB, P2_PWB = 19, 19 + 124, 147, 151, 155
P2_CCONV = 159
P2_COLS = P2_CCONV + TAPS_C * 3 * C_HEADS


def constant_columns():
    cols, parts, at = {}, [], 0

    def put(name, a):
        nonlocal at
        a = np.asarray(a, np.float32).reshape(P, -1)
        cols[name] = (at, a.shape[1])
        parts.append(a)
        at += a.shape[1]

    i, j = np.arange(P)[:, None], np.arange(P)[None, :]
    same = i // CHUNK == j // CHUNK
    put("ident", i == j)
    put("ones", np.ones((P, P)))
    put("blocks", same)
    put("cumulate", same & (i <= j))
    put("not_after", np.where(same & (j <= i), 0.0, NEG))
    put("not_before", np.where(same & (j >= i), 0.0, NEG))
    put("strict", same & (j < i))
    for name, flip in (("levels", False), ("levels_t", True)):
        masks = []
        for level in range(6):
            b = 1 << level
            m = -1.0 * ((i // (2 * b) == j // (2 * b)) & (i // b % 2 == 1) & (j // b % 2 == 0))
            masks.append(m.T if flip else m)
        put(name, np.stack(masks, 1))
    q = np.arange(P)[:, None, None] + P * np.arange(2)[None, :, None]
    s = np.arange(T)[None, None, :]
    put("window_1", np.where(np.abs(q - s) <= 128, 0.0, NEG))
    put("window_2", np.where((q - s >= 0) & (q - s < 128), 0.0, NEG))
    for name, rot, head in (("1", ROT_1, HEAD_DIM_1), ("2", ROT_2, HEAD_DIM_2)):
        half = rot // 2
        freq = ROPE_THETA ** (-np.arange(0, rot, 2, dtype=np.float64) / rot)
        column, turn = np.zeros(P), np.zeros((P, P))
        for base in range(0, P, head):
            for d in range(rot):
                column[base + d] = freq[d % half]
            for d in range(half):
                turn[base + d + half, base + d] = -1.0
                turn[base + d, base + d + half] = 1.0
        put("freq_" + name, np.stack([column, column], 1))
        put("turn_" + name, turn)
    return cols, np.concatenate(parts, 1)


CONST_COLS, CONSTANTS = constant_columns()


def record(**fields):
    return namedtuple("Record", fields.keys())(*fields.values())


@contextmanager
def phase(nc, name, sems):
    with ExitStack() as stack:
        def sbuf(n, shape, dt=F32):
            return stack.enter_context(nc.sbuf_tensor(f"{name}_{n}", shape, dt))
        named = {n: stack.enter_context(nc.semaphore(f"{name}_{n}")) for n in sems.split()}
        s = record(**named, sbuf=sbuf, all=list(named.values()))
        yield s
        with nc.Block() as block:
            @block.sync
            def _(sp):
                for sem in s.all:
                    sp.sem_clear(sem)


STREAM = "loaded0 loaded1 rounded split used "


class Stream:

    def __init__(self, k, s, source, first):
        self.k, self.s, self.source, self.first = k, s, source, first
        self.loaded = (s.loaded0, s.loaded1)

    def open_dve(self, dve):
        dve.sem_inc(self.s.split, RAW)

    def open_pe(self, pe):
        pe.sem_inc(self.s.used, SLOTS)

    def load(self, sp, i, s):
        sp.wait_ge(self.s.split, 4 * i + s + 1)
        src = self.source[bass.ds(self.first + 4 * i + s, 1)].rearrange("a p n -> p (a n)")
        dst = self.k.w_raw[:, s % RAW].rearrange("p k n -> p (k n)")
        sp.dma_start(dst, src).then_inc(self.loaded[s % RAW], 16)

    def round(self, act, i, s):
        act.wait_ge(self.loaded[s % RAW], 16 * (2 * i + s // RAW + 1))
        act.wait_ge(self.s.used, 4 * i + s + 1)
        act.activation(self.k.w_hi[:, s], self.k.w_raw[:, s % RAW], ACT.Copy).then_inc(self.s.rounded, 1)

    def residual(self, dve, i, s):
        dve.wait_ge(self.s.rounded, 4 * i + s + 1)
        dve.tensor_tensor(self.k.w_lo[:, s], self.k.w_raw[:, s % RAW], self.k.w_hi[:, s].bitcast(F32),
                          ALU.subtract).then_inc(self.s.split, 1)

    def multiply(self, pe, i, s, hi, lo, tokens_out=False):
        k = self.k
        pe.wait_ge(self.s.split, 4 * i + s + 1 + RAW)
        for m in range(2):
            out = k.z[2 * (s // 2) + m][:, 0:T]
            for kk in range(SLOT_K):
                row = SLOT_K * (s % 2) + kk
                first, last = row == 0, row == KT - 1
                if tokens_out:
                    w_hi, w_lo = k.w_hi[:, s, kk], k.w_lo[:, s, kk]
                    x_hi, x_lo = hi[:, row, P * m:P * m + P], lo[:, row, P * m:P * m + P]
                    pairs = ((x_hi, w_hi), (x_hi, w_lo), (x_lo, w_hi))
                else:
                    w_hi, w_lo = k.w_hi[:, s, kk, P * m:P * m + P], k.w_lo[:, s, kk, P * m:P * m + P]
                    pairs = ((w_hi, hi[:, row]), (w_hi, lo[:, row]), (w_lo, hi[:, row]))
                for n, (a, b) in enumerate(pairs):
                    ins = pe.matmul(out, a, b, start=first and n == 0, stop=last and n == 2)
        ins.then_inc(self.s.used, 1)

    def done(self, i, s):
        return SLOTS + 4 * i + s + 1


def pipelined(engine, count, steps):
    low = min(lag for lag, _ in steps)
    full, end = max(lag for lag, _ in steps), count + low
    for i in range(low, full):
        for lag, fn in steps:
            if 0 <= i - lag < count:
                fn(i - lag)
    if end - full > 1:
        with engine.Fori(full, end) as i:
            for lag, fn in steps:
                fn(i - lag)
    elif end - full == 1:
        for lag, fn in steps:
            fn(full - lag)
    for i in range(max(end, full), count + full):
        for lag, fn in steps:
            if 0 <= i - lag < count:
                fn(i - lag)


def stream_steps(engine, act):
    def step(i):
        for s in range(SLOTS):
            act(engine, i, s)
    return step


def constant(k, name, p=P):
    at, n = CONST_COLS[name]
    return k.constants[0:p, at:at + n]


def setup_phase(k):
    nc = k.nc
    with phase(nc, "setup", "loaded") as s:
        with nc.Block() as block:
            @block.sync
            def _(sp):
                sp.dma_start(k.ident[:], constant(k, "ident")).then_inc(s.loaded, 16)
                sp.dma_start(k.ones[:], constant(k, "ones")).then_inc(s.loaded, 16)
                sp.dma_start(k.blocks[:], constant(k, "blocks")).then_inc(s.loaded, 16)
                sp.wait_ge(s.loaded, 48)

            @block.gpsimd
            def _(pool):
                pool.memset(k.eps[:], NORM_EPS)


def norm_phase(k, name, weight, source, keep):
    nc = k.nc
    with phase(nc, name, "x0 x1 x2 x3 weight squared summed std rstd scaled rounded split kept") as s:
        squares = s.sbuf("squares", [P, KT, T])
        std, rstd = s.sbuf("std", [P, T]), s.sbuf("rstd", [P, T])
        w = s.sbuf("w", [P, KT])
        x_loaded = (s.x0, s.x1, s.x2, s.x3)
        q4 = [slice(4 * q, 4 * q + 4) for q in range(4)]
        with nc.Block() as block:
            @block.sync
            def _(sp):
                if source is not None:
                    for q in range(4):
                        sp.dma_start(k.feat[:, q4[q]], source[:, q4[q]]).then_inc(x_loaded[q], 16)
                sp.dma_start(w[:], weight).then_inc(s.weight, 16)
                if keep is not None:
                    sp.dma_start(keep, k.feat[:]).then_inc(s.kept, 16)
                    sp.wait_ge(s.kept, 16)

            @block.scalar
            def _(act):
                for q in range(4):
                    if source is not None:
                        act.wait_ge(x_loaded[q], 16)
                    act.activation(squares[:, q4[q]], k.feat[:, q4[q]], ACT.Square).then_inc(s.squared, 1)
                act.wait_ge(s.summed, 1)
                act.activation(std[:], k.aux[0][:, 0:T], ACT.Sqrt, bias=k.eps[:], scale=1.0 / D).then_inc(s.std, 1)
                for q in range(4):
                    act.wait_ge(s.scaled, 4 * q + 4)
                    act.activation(k.xn_hi[:, q4[q]], squares[:, q4[q]], ACT.Copy).then_inc(s.rounded, 1)

            @block.tensor
            def _(pe):
                for t in range(KT):
                    if t % 4 == 0:
                        pe.wait_ge(s.squared, t // 4 + 1)
                    ins = pe.matmul(k.aux[0][:, 0:T], k.ones[:], squares[:, t], start=t == 0, stop=t == KT - 1)
                ins.then_inc(s.summed, 1)

            @block.vector
            def _(dve):
                dve.wait_ge(s.weight, 16)
                dve.wait_ge(s.std, 1)
                dve.reciprocal(rstd[:], std[:]).then_inc(s.rstd, 1)
                dve.wait_ge(s.rstd, 1)
                for t in range(KT):
                    dve.scalar_tensor_tensor(out=squares[:, t], in0=k.feat[:, t], scalar=w[:, t:t + 1], in1=rstd[:],
                                             op0=ALU.mult, op1=ALU.mult).then_inc(s.scaled, 1)
                for q in range(4):
                    dve.wait_ge(s.rounded, q + 1)
                    dve.tensor_tensor(k.xn_lo[:, q4[q]], squares[:, q4[q]], k.xn_hi[:, q4[q]].bitcast(F32),
                                      ALU.subtract).then_inc(s.split, 1)


def softplus_tail(link, dve, x, w, z, acc):
    link(lambda: dve.tensor_scalar(z, w, 2.0, None, ALU.add))
    link(lambda: dve.reciprocal(acc, z))
    link(lambda: dve.tensor_tensor(w, w, acc, ALU.mult))
    link(lambda: dve.tensor_tensor(z, w, w, ALU.mult))
    link(lambda: dve.tensor_scalar(acc, z, 1.0 / 17, 1.0 / 15, ALU.mult, ALU.add))
    for n in range(13, 0, -2):
        link(lambda: dve.tensor_tensor(acc, acc, z, ALU.mult))
        link(lambda: dve.tensor_scalar(acc, acc, 1.0 / n, None, ALU.add))
    link(lambda: dve.tensor_tensor(acc, acc, w, ALU.mult))
    link(lambda: dve.tensor_scalar(x, x, 0.0, None, ALU.max))
    link(lambda: dve.scalar_tensor_tensor(out=x, in0=acc, scalar=2.0, in1=x, op0=ALU.mult, op1=ALU.add))


def after(engine, sem, value):
    if not (isinstance(value, int) and value == 0):
        engine.wait_ge(sem, value)


def chain(engine, sem):
    count = [0]

    def link(make):
        count[0] += 1
        make().then_inc(sem, 1)
        engine.wait_ge(sem, count[0])
    return link


def lru_phase(k):
    nc = k.nc
    CONV = 8
    with phase(nc, "lru", STREAM + "weights params exped chain cleared ucopied conv gsig zcopied gates0 gates taken "
               "decay dsteps rounded_y ydone") as s:
        stream = Stream(k, s, k.w1, SLOT_LRU)
        params = s.sbuf("params", [P, P1_COLS])
        gate_w = s.sbuf("gate_w", [P, 2, 4, P])
        padded = s.sbuf("padded", [P, 2, T + 4])
        g_all = s.sbuf("g_all", [P, KT, T])
        gsig = s.sbuf("gsig", [P, 2, T])
        gate_r, gate_i, decay, tau = (s.sbuf(n, [P, 2, 2, T]) for n in ("gate_r", "gate_i", "decay", "tau"))
        y = s.sbuf("y", [P, 2, T])
        scale_a, scale_t = s.sbuf("scale_a", [P, 32]), s.sbuf("scale_t", [P, 32])
        tmp = [s.sbuf(f"tmp{n}", [P, 32]) for n in range(3)]
        rate = s.sbuf("rate", [P, 32])

        def col(at, i=0):
            return params[:, bass.ds(at + i, 1)]

        with nc.Block() as block:
            @block.sync
            def _(sp):
                sp.dma_start(params[:], k.p1).then_inc(s.params, 16)

                def gates_in(i):
                    sp.wait_ge(s.gates, i + 1)
                    sp.dma_start(gate_w[:].rearrange("p b g n -> p (b g n)"),
                                 k.lru_w[bass.ds(i, 1)].rearrange("a p n -> p (a n)")).then_inc(s.weights, 16)
                pipelined(sp, LRU_PASSES, [(0, stream_steps(sp, stream.load)), (0, gates_in)])

            @block.scalar
            def _(act):
                act.wait_ge(s.chain, 2)
                act.activation(tmp[1][:], tmp[0][:], ACT.Exp).then_inc(s.exped, 1)
                act.wait_ge(s.cleared, 1)

                def inputs(i):
                    act.wait_ge(s.conv, CONV * i + 1)
                    act.wait_ge(s.used, stream.done(i, 1))
                    for b in range(2):
                        act.activation(padded[:, b, 2:2 + T], k.z[b][:, 0:T], ACT.Copy).then_inc(s.ucopied, 1)
                    act.wait_ge(s.used, stream.done(i, 3))
                    for b in range(2):
                        act.activation(gsig[:, b], k.z[2 + b][:, 0:T], ACT.Sigmoid).then_inc(s.gsig, 1)

                def gates(i):
                    act.wait_ge(s.gates, i + 2)
                    for b in range(2):
                        for d in range(2):
                            act.activation(gate_r[:, b, d], k.aux[2 * b + d][:, 0:T], ACT.Sigmoid,
                                           bias=col(P1_BR + 16 * d + b, 2 * i)).then_inc(s.taken, 1)
                            act.activation(gate_i[:, b, d], k.aux[2 * b + d][:, T:2 * T], ACT.Sigmoid,
                                           bias=col(P1_BI + 16 * d + b, 2 * i)).then_inc(s.taken, 1)
                    act.wait_ge(s.taken, 8 * i + 9)
                    for b in range(2):
                        for d in range(2):
                            act.activation(tau[:, b, d], gate_r[:, b, d], ACT.Tanh,
                                           scale=scale_t[:, bass.ds(16 * d + b + 2 * i, 1)]).then_inc(s.decay, 1)
                    for b in range(2):
                        for d in range(2):
                            act.activation(decay[:, b, d], gate_r[:, b, d], ACT.Exp,
                                           scale=scale_a[:, bass.ds(16 * d + b + 2 * i, 1)]).then_inc(s.decay, 1)
                    act.wait_ge(s.decay, 9 * i + 8)
                    act.activation(tau[:], tau[:], ACT.Sqrt).then_inc(s.decay, 1)

                def round_y(i):
                    act.wait_ge(s.dsteps, 10 * i + 10)
                    act.activation(k.y_hi[:, bass.ds(2 * i, 2)], y[:], ACT.Copy).then_inc(s.rounded_y, 1)

                pipelined(act, LRU_PASSES, [(0, stream_steps(act, stream.round)), (1, inputs), (2, gates), (2, round_y)])

            @block.vector
            def _(dve):
                stream.open_dve(dve)
                dve.sem_inc(s.conv, 1)
                dve.memset(padded[:], 0.0).then_inc(s.cleared, 1)
                link = chain(dve, s.chain)
                dve.wait_ge(s.params, 16)
                link(lambda: dve.tensor_scalar(rate[:], params[:, P1_LAM:P1_LAM + 32], -1.0, None, ALU.mult))

                link(lambda: dve.tensor_tensor(tmp[0][:], rate[:], params[:, P1_LAM:P1_LAM + 32], ALU.min))
                dve.wait_ge(s.exped, 1)
                softplus_tail(link, dve, rate[:], tmp[1][:], tmp[0][:], tmp[2][:])
                link(lambda: dve.tensor_scalar(scale_a[:], rate[:], -8.0, None, ALU.mult))
                link(lambda: dve.tensor_scalar(scale_t[:], rate[:], 4.0, None, ALU.mult))

                def convolve(i):
                    dve.wait_ge(s.ucopied, 2 * i + 4)
                    for tap in range(4):
                        for b in range(2):
                            if tap:
                                dve.wait_ge(s.conv, CONV * i + 1 + 2 * (tap - 1) + b + 1)
                            u, x = k.feat[:, bass.ds(2 * i + b, 1)], padded[:, b, tap:tap + T]
                            if tap == 0:
                                ins = dve.tensor_scalar(u, x[:, None], col(P1_CONV + b, 2 * i), col(P1_CONVB + b, 2 * i),
                                                        ALU.mult, ALU.add)
                            else:
                                ins = dve.scalar_tensor_tensor(out=u, in0=x[:, None], scalar=col(P1_CONV + 16 * tap + b, 2 * i),
                                                               in1=u, op0=ALU.mult, op1=ALU.add)
                            ins.then_inc(s.conv, 1)
                    dve.wait_ge(s.gsig, 2 * i + 2)
                    for b in range(2):
                        dve.tensor_tensor(g_all[:, bass.ds(2 * i + b, 1)], k.z[2 + b][:, None, 0:T], gsig[:, b:b + 1],
                                          ALU.mult).then_inc(s.zcopied, 1)

                def scan(i):
                    def step(n):
                        dve.wait_ge(s.dsteps, 10 * i + n)
                    dve.wait_ge(s.decay, 9 * i + 9)
                    dve.scalar_tensor_tensor(out=tau[:], in0=decay[:], scalar=1.0, in1=tau[:], op0=ALU.add,
                                             op1=ALU.mult).then_inc(s.dsteps, 1)
                    for b in range(2):
                        u = k.feat[:, bass.ds(2 * i + b, 1)].to_broadcast([P, 2, T])
                        dve.tensor_tensor(gate_i[:, b], gate_i[:, b], u, ALU.mult).then_inc(s.dsteps, 1)
                    step(3)
                    dve.tensor_tensor(tau[:], tau[:], gate_i[:], ALU.mult).then_inc(s.dsteps, 1)
                    step(4)
                    for b in range(2):
                        dve.tensor_tensor_scan(gate_r[:, b, 0], decay[:, b, 0], tau[:, b, 0], 0.0, ALU.mult,
                                               ALU.add).then_inc(s.dsteps, 1)
                        dve.tensor_tensor_scan(gate_r[:, b, 1, ::-1], decay[:, b, 1, ::-1], tau[:, b, 1, ::-1], 0.0,
                                               ALU.mult, ALU.add).then_inc(s.dsteps, 1)
                    step(8)
                    dve.tensor_tensor(gate_i[:, :, 0], gate_r[:, :, 0], gate_r[:, :, 1], ALU.add).then_inc(s.dsteps, 1)
                    step(9)
                    dve.tensor_tensor(y[:], gate_i[:, :, 0], g_all[:, bass.ds(2 * i, 2)], ALU.mult).then_inc(s.dsteps, 1)
                    dve.wait_ge(s.rounded_y, i + 1)
                    dve.tensor_tensor(k.y_lo[:, bass.ds(2 * i, 2)], y[:], k.y_hi[:, bass.ds(2 * i, 2)].bitcast(F32),
                                      ALU.subtract).then_inc(s.ydone, 1)

                pipelined(dve, LRU_PASSES, [(0, stream_steps(dve, stream.residual)), (1, convolve), (2, scan)])

            @block.tensor
            def _(pe):
                stream.open_pe(pe)
                pe.sem_inc(s.gates, 1)
                pe.sem_inc(s.ucopied, 2)
                pe.sem_inc(s.zcopied, 2)
                pe.sem_inc(s.taken, 1)

                def products(i):
                    pe.wait_ge(s.ucopied, 2 * i + 2)
                    for sl in (0, 1):
                        stream.multiply(pe, i, sl, k.xn_hi, k.xn_lo)
                    pe.wait_ge(s.zcopied, 2 * i + 2)
                    for sl in (2, 3):
                        stream.multiply(pe, i, sl, k.xn_hi, k.xn_lo)

                def gates(i):
                    pe.wait_ge(s.conv, CONV * i + 1 + CONV)
                    pe.wait_ge(s.weights, 16 * i + 16)
                    pe.wait_ge(s.taken, 8 * i + 1)
                    for b in range(2):
                        for d in range(2):
                            for g in range(2):
                                ins = pe.matmul(k.aux[2 * b + d][:, g * T:g * T + T], gate_w[:, b, 2 * d + g],
                                                k.feat[:, bass.ds(2 * i + b, 1)], start=True, stop=True)
                    ins.then_inc(s.gates, 1)

                pipelined(pe, LRU_PASSES, [(0, products), (1, gates)])


def merge_phase(k, name, first_slot, y_first):
    nc = k.nc
    with phase(nc, name, STREAM + "gsig taken steps") as s:
        stream = Stream(k, s, k.w1, first_slot)
        gate, part = s.sbuf("gate", [P, 2, T]), s.sbuf("part", [P, 2, T])
        with nc.Block() as block:
            @block.sync
            def _(sp):
                pipelined(sp, KT // 2, [(0, stream_steps(sp, stream.load))])

            @block.scalar
            def _(act):
                def gates(i):
                    act.wait_ge(s.used, stream.done(i, 1))
                    act.wait_ge(s.taken, 2 * i + 2)
                    for b in range(2):
                        act.activation(gate[:, b], k.z[b][:, 0:T], ACT.Sigmoid).then_inc(s.gsig, 1)
                pipelined(act, KT // 2, [(0, stream_steps(act, stream.round)), (1, gates)])

            @block.vector
            def _(dve):
                stream.open_dve(dve)
                dve.sem_inc(s.taken, 2)

                def merge(i):
                    dve.wait_ge(s.gsig, 2 * i + 4)
                    dve.wait_ge(s.used, stream.done(i, 3))
                    out = k.feat[:, bass.ds(2 * i, 2)] if y_first else part[:]
                    for b in range(2):
                        o = k.feat[:, bass.ds(2 * i + b, 1)] if y_first else part[:, b:b + 1]
                        dve.tensor_tensor(o, k.z[2 + b][:, None, 0:T], gate[:, b:b + 1], ALU.mult).then_inc(s.taken, 1)
                    if not y_first:
                        dve.wait_ge(s.taken, 2 * i + 4)
                        f = k.feat[:, bass.ds(2 * i, 2)]
                        dve.tensor_tensor(f, f, part[:], ALU.add).then_inc(s.steps, 1)
                        dve.wait_ge(s.steps, i + 1)
                pipelined(dve, KT // 2, [(0, stream_steps(dve, stream.residual)), (1, merge)])

            @block.tensor
            def _(pe):
                stream.open_pe(pe)
                pe.sem_inc(s.gsig, 2)

                def products(i):
                    pe.wait_ge(s.gsig, 2 * i + 2)
                    for sl in (0, 1):
                        stream.multiply(pe, i, sl, k.xn_hi, k.xn_lo)
                    pe.wait_ge(s.taken, 2 * i + 2)
                    for sl in (2, 3):
                        stream.multiply(pe, i, sl, k.y_hi, k.y_lo)
                pipelined(pe, KT // 2, [(0, products)])


def rope_tables(k, name, positions, freq):
    nc = k.nc
    turn_parts = (6.28125, 0.0019350051879882812, 3.019916e-07)
    turn_parts = turn_parts[:2] + (2 * math.pi - sum(turn_parts[:2]),)
    magic = 1.5 * 2.0 ** 23
    with phase(nc, name, "loaded counted chain looked") as s:
        pos_i = s.sbuf("pos_i", [P, T], I32)
        angle, turns, rest = (s.sbuf(n, [P, T]) for n in ("angle", "turns", "rest"))
        f = s.sbuf("f", [P, 2])
        with nc.Block() as block:
            @block.sync
            def _(sp):
                sp.dma_start(f[:], constant(k, freq)).then_inc(s.loaded, 16)
                if positions is not None:
                    sp.dma_start(pos_i[:], positions.to_broadcast([P, T])).then_inc(s.loaded, 16)

            @block.gpsimd
            def _(pool):
                if positions is None:
                    pool.iota(pos_i[:], [[1, T]], base=0, channel_multiplier=0).then_inc(s.counted, 1)

            @block.vector
            def _(dve):
                link = chain(dve, s.chain)
                if positions is None:
                    dve.wait_ge(s.counted, 1)
                    dve.wait_ge(s.loaded, 16)
                else:
                    dve.wait_ge(s.loaded, 32)
                link(lambda: dve.tensor_copy(angle[:], pos_i[:]))
                link(lambda: dve.tensor_scalar(angle[:], angle[:], f[:, 0:1], None, ALU.mult))
                for n, (table, quarter) in enumerate(((k.sin_t, 0.0), (k.cos_t, 0.25))):
                    if n:
                        dve.wait_ge(s.looked, 1)
                    link(lambda: dve.tensor_scalar(turns[:], angle[:], 0.5 / math.pi, quarter, ALU.mult, ALU.add))
                    link(lambda: dve.tensor_scalar(turns[:], turns[:], magic, None, ALU.add))
                    link(lambda: dve.tensor_scalar(turns[:], turns[:], -magic, None, ALU.add))
                    for m, part in enumerate(turn_parts):
                        link(lambda: dve.scalar_tensor_tensor(out=rest[:], in0=turns[:], scalar=-part,
                                                              in1=rest[:] if m else angle[:], op0=ALU.mult, op1=ALU.add))
                    link(lambda: dve.tensor_scalar(rest[:], rest[:], quarter * 2 * math.pi, 3.1415925, ALU.add, ALU.min))
                    link(lambda: dve.tensor_scalar(rest[:], rest[:], -3.1415925, None, ALU.max))

            @block.scalar
            def _(act):
                for n, table in enumerate((k.sin_t, k.cos_t)):
                    act.wait_ge(s.chain, 2 + 8 * (n + 1))
                    act.activation(table[:], rest[:], ACT.Sin).then_inc(s.looked, 1)


def attention_phase(k, name, a):
    nc = k.nc
    heads = a.heads_per_tile
    pairs = heads
    M = 12
    R = 5 if heads == 2 else 3
    C = 4 if heads == 2 else 2
    KV_PASSES = 2 // heads
    G0 = 2 if heads == 1 else 1
    K_STEPS = 6 if heads == 1 else R + 8
    MIXED = 1 if heads == 1 else 0
    with phase(nc, name, STREAM + "consts ready kcopied kturned ksteps kdone kdup vcopied vcur qcopied turned rope "
               "qstd gsig gmul scores soft exped flipped fcopied mixed ysteps yrounded") as s:
        stream = Stream(k, s, a.weights, a.first_slot)
        turn = s.sbuf("turn", [P, P])
        mask = s.sbuf("mask", [P, 2, T])
        sinks, sink_row = s.sbuf("sinks", [P, a.n_heads, 2]), s.sbuf("sink_row", [P, a.n_heads])
        norms = s.sbuf("norms", [P, 2])
        kt_n = 4 // heads
        keys = s.sbuf("keys", [P, 4, T])
        values = s.sbuf("values", [P, 2, a.kv_width])
        values_now = s.sbuf("values_now", [P, 2, P]) if heads == 1 else None
        q_raw, q_sq, q_rot, part = (s.sbuf(n, [P, 2, T]) for n in ("q_raw", "q_sq", "q_rot", "part"))
        k_raw = s.sbuf("k_raw", [P, 4, T]) if heads == 1 else q_raw
        std, rstd = (s.sbuf(n, [P, 2, T]) for n in ("std", "rstd")) if heads == 2 else (None, None)
        gsig, gate = s.sbuf("gsig", [P, 2, T]), s.sbuf("gate", [P, 2, T])
        S = [s.sbuf(f"S{p}", [P, 2, 2, T]) for p in range(pairs)]
        W = [s.sbuf(f"W{p}", [P, 2, 2, T]) for p in range(pairs)]
        small = [s.sbuf(f"small{p}", [P, 6, 4]) for p in range(pairs)]
        y = s.sbuf("y", [P, 2, T])
        cos_b = k.cos_t[:, None, :].to_broadcast([P, 2, T])
        sin_b = k.sin_t[:, None, :].to_broadcast([P, 2, T])

        def both(bank):
            return bank[:, 0:2 * T].rearrange("p (b t) -> p b t", b=2)

        def kv_of(i, p, h):
            return i // 2 if heads == 1 else (4 * i + 2 * p + h) // 3

        with nc.Block() as block:
            @block.sync
            def _(sp):
                sp.dma_start(turn[:], constant(k, a.turn)).then_inc(s.consts, 16)
                sp.dma_start(mask[:].rearrange("p b t -> p (b t)"), constant(k, a.mask)).then_inc(s.consts, 16)
                sp.dma_start(sink_row[:], a.sinks.to_broadcast([P, a.n_heads])).then_inc(s.consts, 16)
                if a.norms is not None:
                    sp.dma_start(norms[:], a.norms).then_inc(s.consts, 16)
                pipelined(sp, G0 + a.passes, [(0, stream_steps(sp, stream.load))])

            consts_in = 48 if a.norms is None else 64

            @block.gpsimd
            def _(pool):
                if heads == 1:
                    pool.wait_ge(s.vcopied, 4)

                    def values_here(i):
                        pool.wait_ge(s.mixed, i + 1)
                        pool.tensor_copy(values_now[:], values[:, :, bass.ds((i // 2) * P, P)]).then_inc(s.vcur, 1)
                    pipelined(pool, a.passes, [(0, values_here)])

            @block.scalar
            def _(act):
                for g in range(G0):
                    stream_steps(act, stream.round)(g)
                if heads == 1:
                    for t in range(4):
                        act.wait_ge(s.used, stream.done(0, 2 * (t // 2) + 1))
                        act.activation(k_raw[:, t], k.z[t][:, 0:T], ACT.Copy).then_inc(s.kcopied, 1)
                    v_pass, v_bank = 1, 0
                else:
                    act.wait_ge(s.consts, consts_in)
                    act.wait_ge(s.used, stream.done(0, 1))
                    for t in range(2):
                        act.activation(k_raw[:, t], k.z[t][:, 0:T], ACT.Copy, scale=norms[:, 1:2]).then_inc(s.kcopied, 1)
                        act.activation(q_sq[:, t], k.z[t][:, 0:T], ACT.Square).then_inc(s.kcopied, 1)
                    v_pass, v_bank = 0, 2
                if heads == 2:
                    act.wait_ge(s.kturned, 2)
                    act.activation(std[:], both(k.z[1]), ACT.Sqrt, bias=k.eps[:], scale=1.0 / HEAD_DIM_2).then_inc(s.qstd, 1)
                stream_steps(act, stream.round)(G0)
                for n in range(4 // heads):
                    bank = v_bank + n
                    act.wait_ge(s.used, stream.done(v_pass, 2 * (bank // 2) + 1))
                    at = T * (n // 2)
                    act.activation(values[:, n % 2, at:at + T], k.z[bank][:, 0:T], ACT.Copy).then_inc(s.vcopied, 1)

                def exps(i, p):
                    u = pairs * i + p
                    act.wait_ge(s.soft, M * u + 5)
                    for h in range(2):
                        for b in range(2):
                            c = 2 * h + b
                            act.activation(S[p][:, h, b], S[p][:, h, b], ACT.Exp, bias=small[p][:, 1, c:c + 1],
                                           accum_out=small[p][:, 3, c:c + 1]).then_inc(s.exped, 1)
                    act.wait_ge(s.soft, M * u + 6)
                    act.activation(small[p][:, 4], small[p][:, 2], ACT.Exp).then_inc(s.exped, 1)

                def copy_weights(i, p):
                    u = pairs * i + p
                    act.wait_ge(s.flipped, u + 1)
                    for h in range(2):
                        act.activation(W[p][:, h], both(k.aux[2 * p + h]), ACT.Copy).then_inc(s.fcopied, 1)

                def round_y(i, p):
                    u = pairs * i + p
                    act.wait_ge(s.ysteps, 2 * u + 1)
                    if heads == 1:
                        act.activation(k.y_hi[:, bass.ds(2 * i, 2)], y[:], ACT.Copy).then_inc(s.yrounded, 1)
                    else:
                        act.activation(k.y_hi[:, 2 * i + p], y[:, 0], ACT.Copy).then_inc(s.yrounded, 1)

                def body(i, prev, nxt):
                    g = i + G0
                    if prev:
                        act.wait_ge(s.used, stream.done(g - 1, 3))
                        for b in range(2):
                            act.activation(gsig[:, b], k.z[2 + b][:, 0:T], ACT.Sigmoid).then_inc(s.gsig, 1)
                        exps(i - 1, 0)
                    if nxt:
                        stream.round(act, g + 1, 0)
                    if prev and pairs == 2:
                        exps(i - 1, 1)
                    if nxt:
                        stream.round(act, g + 1, 1)
                    act.wait_ge(s.used, stream.done(g, 1))
                    if prev:
                        act.wait_ge(s.rope, R * i)
                    elif heads == 2:
                        act.wait_ge(s.ksteps, K_STEPS)
                    for t in range(2):
                        if heads == 2:
                            act.activation(q_raw[:, t], k.z[t][:, 0:T], ACT.Copy, scale=norms[:, 0:1]).then_inc(s.qcopied, 1)
                            act.activation(q_sq[:, t], k.z[t][:, 0:T], ACT.Square).then_inc(s.qcopied, 1)
                        else:
                            act.activation(q_raw[:, t], k.z[t][:, 0:T], ACT.Copy).then_inc(s.qcopied, 1)
                    if prev:
                        copy_weights(i - 1, 0)
                    if nxt:
                        stream.round(act, g + 1, 2)
                    if heads == 2:
                        act.wait_ge(s.turned, i + 1)
                        act.activation(std[:], both(k.z[1]), ACT.Sqrt, bias=k.eps[:], scale=1.0 / HEAD_DIM_2).then_inc(s.qstd, 1)
                    if prev:
                        round_y(i - 1, 0)
                    if prev and pairs == 2:
                        copy_weights(i - 1, 1)
                    if nxt:
                        stream.round(act, g + 1, 3)
                    if prev and pairs == 2:
                        round_y(i - 1, 1)

                def tail(i):
                    act.wait_ge(s.used, stream.done(i + G0, 3))
                    for b in range(2):
                        act.activation(gsig[:, b], k.z[2 + b][:, 0:T], ACT.Sigmoid).then_inc(s.gsig, 1)
                    for p in range(pairs):
                        exps(i, p)
                    for p in range(pairs):
                        copy_weights(i, p)
                        round_y(i, p)
                run_passes(act, a.passes, body, tail)

            @block.vector
            def _(dve):
                stream.open_dve(dve)
                for g in range(G0):
                    stream_steps(dve, stream.residual)(g)
                dve.wait_ge(s.consts, consts_in)
                for b in range(2):
                    dve.tensor_copy(sinks[:, :, b], sink_row[:]).then_inc(s.ready, 1)

                def rotate(i, p, wait, sem, base, raw, out):
                    wait(0)
                    after(dve, sem, base)
                    dve.tensor_tensor(part[:], raw, cos_b, ALU.mult).then_inc(sem, 1)
                    dve.tensor_tensor(out, both(p), sin_b, ALU.mult).then_inc(sem, 1)
                    dve.wait_ge(sem, base + 2)
                    dve.tensor_tensor(out, out, part[:], ALU.add).then_inc(sem, 1)
                    if heads == 2:
                        wait(1)
                        dve.reciprocal(rstd[:], std[:]).then_inc(sem, 1)
                        dve.wait_ge(sem, base + 4)
                        dve.tensor_tensor(out, out, rstd[:], ALU.mult).then_inc(sem, 1)

                if heads == 1:
                    for h in range(2):
                        rotate(0, k.aux[h], lambda n: dve.wait_ge(s.kturned, h + 1), s.ksteps, R * h,
                               k_raw[:, 2 * h:2 * h + 2], keys[:, 2 * h:2 * h + 2])
                else:
                    rotate(0, k.z[0], lambda n: dve.wait_ge(s.qstd if n else s.kturned, 1), s.ksteps, 0, k_raw[:], q_rot[:])
                    dve.wait_ge(s.ksteps, R)
                    for kv in range(4):
                        half = (kv % 2) * 64
                        for to in (0, 64):
                            dve.tensor_copy(keys[to:to + 64, kv], q_rot[half:half + 64, kv // 2]).then_inc(s.ksteps, 1)
                stream_steps(dve, stream.residual)(G0)

                def soften(i, p):
                    u = pairs * i + p
                    dve.wait_ge(s.scores, u + 1)
                    for h in range(2):
                        dve.scalar_tensor_tensor(out=S[p][:, h], in0=both(k.aux[2 * p + h]), scalar=a.scale, in1=mask[:],
                                                 op0=ALU.mult, op1=ALU.add).then_inc(s.soft, 1)
                    dve.wait_ge(s.soft, M * u + 2)
                    m = small[p]
                    dve.tensor_reduce(m[:, 0], S[p][:].rearrange("p h b t -> p (h b) t"), AX_X, ALU.max).then_inc(s.soft, 1)
                    dve.wait_ge(s.soft, M * u + 3)
                    sink = sinks[:, bass.ds(2 * u, 2)].rearrange("p h b -> p (h b)")
                    dve.tensor_tensor(m[:, 0], m[:, 0], sink, ALU.max).then_inc(s.soft, 1)
                    dve.wait_ge(s.soft, M * u + 4)
                    dve.tensor_scalar(m[:, 1], m[:, 0], -1.0, None, ALU.mult).then_inc(s.soft, 1)
                    dve.wait_ge(s.soft, M * u + 5)
                    dve.tensor_tensor(m[:, 2], m[:, 1], sink, ALU.add).then_inc(s.soft, 1)

                def normalise(i, p):
                    u = pairs * i + p
                    m = small[p]
                    dve.wait_ge(s.exped, 5 * u + 5)
                    dve.tensor_tensor(m[:, 5], m[:, 3], m[:, 4], ALU.add).then_inc(s.soft, 1)
                    dve.wait_ge(s.soft, M * u + 7)
                    dve.reciprocal(m[:, 0], m[:, 5]).then_inc(s.soft, 1)
                    dve.wait_ge(s.soft, M * u + 8)
                    for h in range(2):
                        for b in range(2):
                            c = 2 * h + b
                            dve.tensor_scalar(S[p][:, h, b], S[p][:, h, b], m[:, 0, c:c + 1], None, ALU.mult)\
                               .then_inc(s.soft, 1)

                def open_gates(i):
                    dve.wait_ge(s.gsig, 2 * i + 2)
                    for b in range(2):
                        dve.tensor_tensor(gate[:, b], k.z[2 + b][:, 0:T], gsig[:, b], ALU.mult).then_inc(s.gmul, 1)

                def finish(i, p):
                    u = pairs * i + p
                    dve.wait_ge(s.mixed, u + 1 + MIXED)
                    dve.wait_ge(s.gmul, 2 * i + 2)
                    if heads == 1:
                        dve.tensor_tensor(y[:], both(k.aux[0]), gate[:], ALU.mult).then_inc(s.ysteps, 1)
                        hi, lo, v = k.y_hi[:, bass.ds(2 * i, 2)], k.y_lo[:, bass.ds(2 * i, 2)], y[:]
                    else:
                        dve.tensor_tensor(y[:, 0], k.aux[2 * p][:, 0:T], gate[:, p], ALU.mult).then_inc(s.ysteps, 1)
                        hi, lo, v = k.y_hi[:, 2 * i + p], k.y_lo[:, 2 * i + p], y[:, 0]
                    dve.wait_ge(s.yrounded, u + 1)
                    dve.tensor_tensor(lo, v, hi.bitcast(F32), ALU.subtract).then_inc(s.ysteps, 1)
                    dve.wait_ge(s.ysteps, 2 * u + 2)

                def body(i, prev, nxt):
                    g = i + G0
                    if prev:
                        open_gates(i - 1)
                        soften(i - 1, 0)
                    if nxt:
                        stream.residual(dve, g + 1, 0)
                    if prev:
                        normalise(i - 1, 0)
                        if pairs == 2:
                            soften(i - 1, 1)
                    if nxt:
                        stream.residual(dve, g + 1, 1)
                    if prev and pairs == 2:
                        normalise(i - 1, 1)
                    if nxt:
                        stream.residual(dve, g + 1, 2)
                    rotate(i, k.z[0], lambda n: dve.wait_ge(s.qstd, i + 2) if n else dve.wait_ge(s.turned, i + 1), s.rope, R * i,
                           q_raw[:], q_rot[:])
                    if prev:
                        finish(i - 1, 0)
                    if nxt:
                        stream.residual(dve, g + 1, 3)
                    if prev and pairs == 2:
                        finish(i - 1, 1)

                def tail(i):
                    open_gates(i)
                    for p in range(pairs):
                        soften(i, p)
                        normalise(i, p)
                    for p in range(pairs):
                        finish(i, p)
                run_passes(dve, a.passes, body, tail)

            @block.tensor
            def _(pe):
                stream.open_pe(pe)
                if heads == 1:
                    pe.sem_inc(s.mixed, 1)
                for sl in range(4):
                    stream.multiply(pe, 0, sl, k.xn_hi, k.xn_lo, tokens_out=heads == 2 and sl >= 2)
                pe.wait_ge(s.consts, consts_in)
                if heads == 1:
                    for h in range(2):
                        pe.wait_ge(s.kcopied, 2 * h + 2)
                        pe.matmul(k.aux[h][:, 0:2 * T], turn[:], k_raw[:, 2 * h:2 * h + 2], start=True, stop=True)\
                          .then_inc(s.kturned, 1)
                    pe.wait_ge(s.kcopied, 4)
                    for sl in range(4):
                        stream.multiply(pe, 1, sl, k.xn_hi, k.xn_lo, tokens_out=True)
                else:
                    pe.wait_ge(s.kcopied, 4)
                    pe.matmul(k.z[0][:, 0:2 * T], turn[:], k_raw[:], start=True, stop=True).then_inc(s.kturned, 1)
                    pe.matmul(k.z[1][:, 0:2 * T], k.blocks[:], q_sq[:], start=True, stop=True).then_inc(s.kturned, 1)

                def scores(i, p):
                    for h in range(2):
                        kv = kv_of(i, p, h)
                        for b in range(2):
                            out = k.aux[2 * p + h][:, b * T:b * T + T]
                            if heads == 1:
                                q, key = q_rot[:, h, P * b:P * b + P], keys[:, bass.ds(kv, 1)]
                            else:
                                lo = 64 * h
                                q, key = q_rot[lo:lo + 64, p, P * b:P * b + P], keys[lo:lo + 64, kv]
                            ins = pe.matmul(out, q, key, start=True, stop=True)
                    ins.then_inc(s.scores, 1)

                def flip(i, p):
                    u = pairs * i + p
                    pe.wait_ge(s.soft, M * u + 12)
                    for h in range(2):
                        for b in range(2):
                            for kb in range(2):
                                ins = pe.transpose(k.aux[2 * p + h][:, kb * T + b * P:kb * T + b * P + P],
                                                   S[p][:, h, b, kb * P:kb * P + P], k.ident[:])
                    ins.then_inc(s.flipped, 1)

                def mix(i, p):
                    u = pairs * i + p
                    pe.wait_ge(s.fcopied, 2 * u + 2)
                    if heads == 1:
                        pe.wait_ge(s.vcur, i + 1)
                    for h in range(2):
                        for kb in range(2):
                            if heads == 1:
                                out, v = k.aux[0][:, h * T:h * T + T], values_now[:, kb]
                            else:
                                at = 64 * kv_of(i, p, h)
                                out, v = k.aux[2 * p][64 * h:64 * h + 64, 0:T], values[:, kb, at:at + 64]
                            ins = pe.matmul(out, v, W[p][:, h, kb], start=kb == 0, stop=kb == 1)
                    ins.then_inc(s.mixed, 1)

                def body(i, prev, nxt):
                    g = i + G0
                    if prev:
                        pe.wait_ge(s.rope, R * i)
                    else:
                        pe.wait_ge(s.vcopied, 4 // heads)
                        pe.wait_ge(s.ksteps, K_STEPS)
                    stream.multiply(pe, g, 0, k.xn_hi, k.xn_lo)
                    if prev and pairs == 2:
                        if i >= 2:
                            pe.wait_ge(s.ysteps, 2 * pairs * (i - 1))
                        scores(i - 1, 1)
                    stream.multiply(pe, g, 1, k.xn_hi, k.xn_lo)
                    if prev:
                        flip(i - 1, 0)
                        pe.wait_ge(s.gmul, 2 * i)
                    stream.multiply(pe, g, 2, k.xn_hi, k.xn_lo)
                    if prev:
                        mix(i - 1, 0)
                        if pairs == 2:
                            flip(i - 1, 1)
                    pe.wait_ge(s.qcopied, C * i + C)
                    ins = pe.matmul(k.z[0][:, 0:2 * T], turn[:], q_raw[:], start=True, stop=True)
                    if heads == 2:
                        ins = pe.matmul(k.z[1][:, 0:2 * T], k.blocks[:], q_sq[:], start=True, stop=True)
                    ins.then_inc(s.turned, 1)
                    stream.multiply(pe, g, 3, k.xn_hi, k.xn_lo)
                    if prev and pairs == 2:
                        mix(i - 1, 1)
                    if prev:
                        pe.wait_ge(s.ysteps, 2 * pairs * (i - 1) + 1)
                    pe.wait_ge(s.rope, R * i + R)
                    scores(i, 0)

                def tail(i):
                    if pairs == 2:
                        pe.wait_ge(s.ysteps, 2 * pairs * i)
                        scores(i, 1)
                    for p in range(pairs):
                        flip(i, p)
                    for p in range(pairs):
                        mix(i, p)
                run_passes(pe, a.passes, body, tail)


def run_passes(engine, count, body, tail):
    body(0, False, True)
    if count > 4:
        with engine.Fori(1, count - 1) as i:
            body(i, True, True)
    else:
        for i in range(1, count - 1):
            body(i, True, True)
    body(count - 1, True, False)
    tail(count - 1)
def conv_phase(k, layer):
    nc = k.nc
    B = B_TILES
    name = "conv"
    with phase(nc, name, STREAM + "params pw cleared acopied gsig gated zsig zgated taps summed centred squared squares "
               "std ln lsig hid mixed ysteps yrounded") as s:
        stream = Stream(k, s, k.w2, layer * SLOTS_2 + SLOT_CONV_2)
        params = s.sbuf("params", [P, P2_COLS])
        pw = s.sbuf("pw", [P, B, B * P])
        padded = s.sbuf("padded", [P, B, TAPS_B - 1 + T])
        a_now, gsig = s.sbuf("a_now", [P, 2, T]), s.sbuf("gsig", [P, 2, T])
        zgate = s.sbuf("zgate", [P, B, T])
        acc, sq, sig = (s.sbuf(n, [P, B, T]) for n in ("acc", "sq", "sig"))
        std, rstd = s.sbuf("std", [P, T]), s.sbuf("rstd", [P, T])
        y = zgate

        def col(at):
            return params[:, at:at + 1]

        with nc.Block() as block:
            @block.sync
            def _(sp):
                sp.dma_start(params[:], k.p2[bass.ds(layer, 1)].rearrange("a p n -> p (a n)")).then_inc(s.params, 16)
                sp.dma_start(pw[:].rearrange("p a n -> p (a n)"), k.pw[bass.ds(layer, 1)].rearrange("a p n -> p (a n)"))\
                  .then_inc(s.pw, 16)
                for i in range(3):
                    stream_steps(sp, stream.load)(i)

            def halves(act, i):
                if i < 2:
                    act.wait_ge(s.used, stream.done(i, 1))
                    if i:
                        act.wait_ge(s.gated, 2 * i)
                    for b in range(2):
                        act.activation(a_now[:, b], k.z[b][:, 0:T], ACT.Copy).then_inc(s.acopied, 1)
                    act.wait_ge(s.used, stream.done(i, 3))
                    for b in range(2):
                        act.activation(gsig[:, b], k.z[2 + b][:, 0:T], ACT.Sigmoid).then_inc(s.gsig, 1)
                else:
                    act.wait_ge(s.used, stream.done(i, 3))
                    for b in range(4):
                        act.activation(zgate[:, b], k.z[b][:, 0:T], ACT.Sigmoid).then_inc(s.zsig, 1)

            @block.scalar
            def _(act):
                for i in range(3):
                    stream_steps(act, stream.round)(i)
                    if i >= 1:
                        halves(act, i - 1)
                halves(act, 2)
                for t in range(B):
                    act.wait_ge(s.centred, t + 1)
                    act.activation(sq[:, t], acc[:, t], ACT.Square).then_inc(s.squared, 1)
                act.wait_ge(s.squares, 1)
                act.activation(std[:], k.aux[1][:, 0:T], ACT.Sqrt, bias=k.eps[:], scale=1.0 / (B * P)).then_inc(s.std, 1)
                for t in range(B):
                    act.wait_ge(s.ln, t + 2)
                    act.activation(sig[:, t], acc[:, t], ACT.Sigmoid, bias=col(P2_LNB + t)).then_inc(s.lsig, 1)
                for t in range(B):
                    act.wait_ge(s.ysteps, t + 1)
                    act.activation(k.y_hi[:, 6 + t], y[:, t], ACT.Copy).then_inc(s.yrounded, 1)

            def gate(dve, i):
                dve.wait_ge(s.acopied, 2 * i + 2)
                dve.wait_ge(s.gsig, 2 * i + 2)
                for b in range(2):
                    dve.tensor_tensor(padded[:, 2 * i + b, TAPS_B - 1:TAPS_B - 1 + T], a_now[:, b], gsig[:, b], ALU.mult)\
                       .then_inc(s.gated, 1)

            @block.vector
            def _(dve):
                stream.open_dve(dve)
                dve.memset(padded[:], 0.0).then_inc(s.cleared, 1)
                dve.wait_ge(s.cleared, 1)
                for i in range(3):
                    stream_steps(dve, stream.residual)(i)
                    if i >= 1:
                        gate(dve, i - 1)
                dve.wait_ge(s.zsig, 4)
                for b in range(4):
                    dve.tensor_tensor(zgate[:, b], k.z[b][:, 0:T], zgate[:, b], ALU.mult).then_inc(s.zgated, 1)
                dve.wait_ge(s.params, 16)
                dve.wait_ge(s.gated, 4)
                for t in range(B):
                    dve.tensor_scalar(acc[:, t], padded[:, t, 0:T], col(P2_BCONV + t), col(P2_BCONVB + t), ALU.mult, ALU.add)\
                       .then_inc(s.taps, 1)
                with dve.Fori(1, TAPS_B) as tap:
                    for t in range(B):
                        dve.wait_ge(s.taps, B * tap + t - B + 1)
                        dve.scalar_tensor_tensor(out=acc[:, t:t + 1], in0=padded[:, t:t + 1, bass.ds(tap, T)],
                                                 scalar=params[:, bass.ds(B * tap + P2_BCONV + t, 1)],
                                                 in1=acc[:, t:t + 1], op0=ALU.mult, op1=ALU.add).then_inc(s.taps, 1)
                dve.wait_ge(s.summed, 1)
                for t in range(B):
                    dve.scalar_tensor_tensor(out=acc[:, t], in0=k.aux[0][:, 0:T], scalar=-1.0 / (B * P), in1=acc[:, t],
                                             op0=ALU.mult, op1=ALU.add).then_inc(s.centred, 1)
                dve.wait_ge(s.std, 1)
                dve.reciprocal(rstd[:], std[:]).then_inc(s.ln, 1)
                dve.wait_ge(s.ln, 1)
                for t in range(B):
                    dve.scalar_tensor_tensor(out=acc[:, t], in0=acc[:, t], scalar=col(P2_LNW + t), in1=rstd[:],
                                             op0=ALU.mult, op1=ALU.mult).then_inc(s.ln, 1)
                for t in range(B):
                    dve.wait_ge(s.lsig, t + 1)
                    dve.scalar_tensor_tensor(out=sig[:, t], in0=acc[:, t], scalar=col(P2_LNB + t), in1=sig[:, t],
                                             op0=ALU.add, op1=ALU.mult).then_inc(s.hid, 1)
                for t in range(B):
                    dve.wait_ge(s.mixed, t + 1)
                    dve.scalar_tensor_tensor(out=y[:, t], in0=k.z[t][:, 0:T], scalar=col(P2_PWB + t), in1=zgate[:, t],
                                             op0=ALU.add, op1=ALU.mult).then_inc(s.ysteps, 1)
                for t in range(B):
                    dve.wait_ge(s.yrounded, t + 1)
                    dve.tensor_tensor(k.y_lo[:, 6 + t], y[:, t], k.y_hi[:, 6 + t].bitcast(F32), ALU.subtract)\
                       .then_inc(s.hid, 1)

            @block.tensor
            def _(pe):
                stream.open_pe(pe)
                for i in range(3):
                    for sl in range(4):
                        if i and sl == 0:
                            pe.wait_ge(s.acopied, 2 * i)
                        if i and sl == 2:
                            pe.wait_ge(s.gsig, 2 * i)
                        stream.multiply(pe, i, sl, k.xn_hi, k.xn_lo)
                pe.wait_ge(s.taps, B * TAPS_B)
                for t in range(B):
                    ins = pe.matmul(k.aux[0][:, 0:T], k.ones[:], acc[:, t], start=t == 0, stop=t == B - 1)
                ins.then_inc(s.summed, 1)
                for t in range(B):
                    pe.wait_ge(s.squared, t + 1)
                    ins = pe.matmul(k.aux[1][:, 0:T], k.ones[:], sq[:, t], start=t == 0, stop=t == B - 1)
                ins.then_inc(s.squares, 1)
                pe.wait_ge(s.pw, 16)
                pe.wait_ge(s.zgated, 4)
                pe.wait_ge(s.hid, B)
                for m in range(B):
                    for t in range(B):
                        ins = pe.matmul(k.z[m][:, 0:T], pw[:, t, P * m:P * m + P], sig[:, t], start=t == 0, stop=t == B - 1)
                    ins.then_inc(s.mixed, 1)


def delta_inputs_phase(k, layer, keep):
    nc = k.nc
    H = C_HEADS
    PAD = TAPS_C - 1
    with phase(nc, "din", STREAM + "params w12 rows cleared copied conv sig qkv zg squared summed std norm split12 rounded12 "
               "bg chain exped negexp") as s:
        stream = Stream(k, s, k.w2, layer * SLOTS_2 + SLOT_DELTA_2)
        params = s.sbuf("params", [P, P2_COLS])
        w12, w12_lo = s.sbuf("w12", [P, KT, 2 * H]), s.sbuf("w12_lo", [P, KT, 2 * H], F32R)
        w12_hi = s.sbuf("w12_hi", [P, KT, 2 * H], F32R)
        rows = s.sbuf("rows", [P, 2, H])
        padded = s.sbuf("padded", [P, 3, PAD + T])
        conv, sig = s.sbuf("conv", [P, 3, T]), s.sbuf("sig", [P, 3, T])
        zsig = s.sbuf("zsig", [P, T])
        qk, sq = s.sbuf("qk", [P, 2, T]), s.sbuf("sq", [P, 2, T])
        std, rstd = s.sbuf("std", [P, 2, T]), s.sbuf("rstd", [P, 2, T])
        x, t0, t1, t2 = (s.sbuf(n, [P, 2, H]) for n in ("x", "t0", "t1", "t2"))

        with nc.Block() as block:
            @block.sync
            def _(sp):
                sp.dma_start(params[:], k.p2[bass.ds(layer, 1)].rearrange("a p n -> p (a n)")).then_inc(s.params, 16)
                sp.dma_start(w12[:].rearrange("p k n -> p (k n)"), k.w12[bass.ds(layer, 1)].rearrange("a p n -> p (a n)"))\
                  .then_inc(s.w12, 16)
                sp.dma_start(rows[:].rearrange("p a n -> p (a n)"), k.rows_c[bass.ds(layer, 1)].to_broadcast([P, 2 * H]))\
                  .then_inc(s.rows, 16)
                pipelined(sp, H, [(0, stream_steps(sp, stream.load))])

            @block.scalar
            def _(act):
                act.wait_ge(s.w12, 16)
                act.activation(w12_hi[:], w12[:], ACT.Copy).then_inc(s.rounded12, 1)
                act.wait_ge(s.rows, 16)
                act.activation(rows[:, 0], rows[:, 0], ACT.Exp).then_inc(s.negexp, 1)
                act.wait_ge(s.bg, 1)
                for b in range(2):
                    act.activation(keep.beta[:, b], k.aux[1][:, 16 * b:16 * b + H], ACT.Sigmoid).then_inc(s.exped, 1)
                act.wait_ge(s.chain, 4)
                act.activation(t1[:], t0[:], ACT.Exp).then_inc(s.exped, 1)
                act.wait_ge(s.cleared, 1)

                def inputs(i):
                    act.wait_ge(s.used, stream.done(i, 1))
                    act.wait_ge(s.conv, 12 * i + 1)
                    for t in range(2):
                        act.activation(padded[:, t, PAD:PAD + T], k.z[t][:, 0:T], ACT.Copy).then_inc(s.copied, 1)
                    act.wait_ge(s.used, stream.done(i, 3))
                    act.activation(padded[:, 2, PAD:PAD + T], k.z[2][:, 0:T], ACT.Copy).then_inc(s.copied, 1)
                    act.wait_ge(s.zg, i + 1)
                    act.activation(zsig[:], k.z[3][:, 0:T], ACT.Sigmoid).then_inc(s.copied, 1)

                def silu(i):
                    act.wait_ge(s.conv, 12 * i + 13)
                    act.activation(sig[:], conv[:], ACT.Sigmoid).then_inc(s.sig, 1)
                    act.wait_ge(s.qkv, 2 * i + 1)
                    act.activation(sq[:], qk[:], ACT.Square).then_inc(s.squared, 1)

                def root(i):
                    act.wait_ge(s.summed, i + 1)
                    act.activation(std[:], k.aux[0][:, 0:2 * T].rearrange("p (b t) -> p b t", b=2), ACT.Sqrt,
                                   bias=k.eps[:]).then_inc(s.std, 1)
                pipelined(act, H, [(0, stream_steps(act, stream.round)), (2, root), (1, inputs), (1, silu)])

            @block.vector
            def _(dve):
                stream.open_dve(dve)
                dve.sem_inc(s.conv, 1)
                dve.sem_inc(s.zg, 1)
                dve.memset(padded[:], 0.0).then_inc(s.cleared, 1)
                dve.wait_ge(s.rounded12, 1)
                dve.tensor_tensor(w12_lo[:], w12[:], w12_hi[:].bitcast(F32), ALU.subtract).then_inc(s.split12, 1)
                link = chain(dve, s.chain)
                dve.wait_ge(s.bg, 1)
                dve.wait_ge(s.negexp, 1)
                dve.wait_ge(s.exped, 2)
                for b in range(2):
                    link(lambda: dve.tensor_tensor(x[:, b], k.aux[1][:, 16 * b + H:16 * b + 2 * H], rows[:, 1], ALU.add))
                link(lambda: dve.tensor_scalar(t0[:], x[:], -1.0, None, ALU.mult))
                link(lambda: dve.tensor_tensor(t0[:], t0[:], x[:], ALU.min))
                dve.wait_ge(s.exped, 3)
                softplus_tail(link, dve, x[:], t1[:], t0[:], t2[:])
                for b in range(2):
                    link(lambda: dve.scalar_tensor_tensor(out=keep.g[:, b], in0=x[:, b], scalar=-1.0, in1=rows[:, 0],
                                                          op0=ALU.mult, op1=ALU.mult))
                dve.wait_ge(s.params, 16)

                def convolve(i):
                    dve.wait_ge(s.copied, 4 * i + 8)
                    dve.tensor_tensor(keep.z_all[:, bass.ds(i, 1)], k.z[3][:, None, 0:T], zsig[:, None], ALU.mult)\
                       .then_inc(s.zg, 1)
                    for tap in range(TAPS_C):
                        for t in range(3):
                            c, src = conv[:, t], padded[:, t, tap:tap + T]
                            w = params[:, bass.ds(P2_CCONV + 3 * C_HEADS * tap + t + 3 * i, 1)]
                            if tap:
                                dve.wait_ge(s.conv, 12 * i + 1 + 3 * (tap - 1) + t + 1)
                                ins = dve.scalar_tensor_tensor(out=c, in0=src, scalar=w, in1=c, op0=ALU.mult, op1=ALU.add)
                            else:
                                ins = dve.tensor_scalar(c, src, w, None, ALU.mult)
                            ins.then_inc(s.conv, 1)
                    dve.wait_ge(s.sig, i + 1)
                    dve.tensor_tensor(qk[:], conv[:, 0:2], sig[:, 0:2], ALU.mult).then_inc(s.qkv, 1)
                    dve.tensor_tensor(keep.v_all[:, bass.ds(i, 1)], conv[:, 2:3], sig[:, 2:3], ALU.mult).then_inc(s.qkv, 1)

                def norm(i):
                    dve.wait_ge(s.std, i + 1)
                    dve.reciprocal(rstd[:], std[:]).then_inc(s.norm, 1)
                    dve.wait_ge(s.norm, 3 * i + 1)
                    dve.scalar_tensor_tensor(out=k.feat[:, bass.ds(2 * i, 1)], in0=qk[:, 0:1], scalar=C_DIM ** -0.5,
                                             in1=rstd[:, 0:1], op0=ALU.mult, op1=ALU.mult).then_inc(s.norm, 1)
                    dve.tensor_tensor(k.feat[:, bass.ds(2 * i + 1, 1)], qk[:, 1:2], rstd[:, 1:2], ALU.mult).then_inc(s.norm, 1)

                pipelined(dve, H, [(0, stream_steps(dve, stream.residual)), (2, norm), (1, convolve)])

            @block.tensor
            def _(pe):
                stream.open_pe(pe)
                pe.wait_ge(s.split12, 1)
                for b in range(2):
                    n = 0
                    for kk in range(KT):
                        hi, lo = k.xn_hi[:, kk, P * b:P * b + P], k.xn_lo[:, kk, P * b:P * b + P]
                        for x_, w_ in ((hi, w12_hi[:, kk]), (hi, w12_lo[:, kk]), (lo, w12_hi[:, kk])):
                            ins = pe.matmul(k.aux[1][:, 16 * b:16 * b + 2 * H], x_, w_, start=n == 0, stop=n == 3 * KT - 1)
                            n += 1
                ins.then_inc(s.bg, 1)
                pe.sem_inc(s.copied, 4)

                def products(i):
                    pe.wait_ge(s.copied, 4 * i + 4)
                    pe.wait_ge(s.zg, i + 1)
                    for sl in range(SLOTS):
                        stream.multiply(pe, i, sl, k.xn_hi, k.xn_lo)

                def sums(i):
                    pe.wait_ge(s.squared, i + 1)
                    pe.matmul(k.aux[0][:, 0:2 * T], k.ones[:], sq[:], start=True, stop=True).then_inc(s.summed, 1)
                pipelined(pe, H, [(0, products), (1, sums)])
def delta_phase(k, layer, keep):
    nc = k.nc
    with phase(nc, "delta", "consts took chain kv_turned rows sums kk exps amat steps1 aturned acopied xstep bt ux ucopied xx "
               "tok uw vnew ws so sstate kvp sq osum std gout yrounded ylo cleared ez") as s:
        strict, not_after, not_before = (s.sbuf(n, [P, P]) for n in ("strict", "not_after", "not_before"))
        cumulate = s.sbuf("cumulate", [P, P])
        levels, levels_t = s.sbuf("levels", [P, 6, P]), s.sbuf("levels_t", [P, 6, P])
        onorm = s.sbuf("onorm", [P, 2])
        pool = k.w_raw[:].rearrange("p a k n -> p (a k n)")

        def unit4(n):
            return pool[:, 512 * n:512 * n + 512].rearrange("p (u t) -> p u t", u=4)
        q, kk_, v = (unit4(n).rearrange("p u t -> p (u t)").rearrange("p (h t) -> p h t", h=2) for n in range(3))
        A, AT, BT = unit4(3), unit4(4), unit4(5)
        X, XT = unit4(6), unit4(7)
        k_tok, v_beta, k_end, k_beta = (s.sbuf(n, [P, 4, P]) for n in ("k_tok", "v_beta", "k_end", "k_beta"))
        intra, grown, decay, decay_t = (s.sbuf(n, [P, 4, P]) for n in ("intra", "grown", "decay", "decay_t"))
        U, WT = decay, decay_t
        UX = s.sbuf("UX", [P, 4, P])
        q_grown = BT
        S, vn = s.sbuf("S", [P, 2, P]), s.sbuf("vn", [P, 2, P])
        bg = s.sbuf("bg", [P, 2, 4])
        sums = s.sbuf("sums", [P, 2, 4])
        sc = s.sbuf("sc", [P, 5, 4])
        std, rstd = AT, A

        def flat(x):
            return x.rearrange("p u t -> p (u t)")

        def masks(m):
            return m[:, None, :].to_broadcast([P, 4, P])

        with nc.Block() as block:
            @block.sync
            def _(sp):
                for t, name in ((strict, "strict"), (not_after, "not_after"), (not_before, "not_before"), (cumulate, "cumulate")):
                    sp.dma_start(t[:], constant(k, name)).then_inc(s.consts, 16)
                sp.dma_start(levels[:].rearrange("p l t -> p (l t)"), constant(k, "levels")).then_inc(s.consts, 16)
                sp.dma_start(levels_t[:].rearrange("p l t -> p (l t)"), constant(k, "levels_t")).then_inc(s.consts, 16)
                sp.dma_start(onorm[:], k.p2[bass.ds(layer, 1), :, P2_ONORM:P2_ONORM + 2].rearrange("a p n -> p (a n)"))\
                  .then_inc(s.consts, 16)
                sp.wait_ge(s.consts, 7 * 16)
        counted = [x for x in s.all if x is not s.consts]
        shared = record(flat=flat, masks=masks, A=A, AT=AT, BT=BT, X=X, XT=XT, UX=UX, bg=bg, q=q, kk_=kk_, v=v, sums=sums, sc=sc,
                        decay=decay, decay_t=decay_t, grown=grown, U=U, WT=WT, std=std, rstd=rstd, cumulate=cumulate,
                        v_beta=v_beta, k_beta=k_beta, S=S, vn=vn, q_grown=q_grown, intra=intra, k_end=k_end, k_tok=k_tok,
                        not_after=not_after, not_before=not_before, strict=strict, levels=levels, levels_t=levels_t,
                        onorm=onorm)
        with nc.Fori(0, C_HEADS // 2) as turn:
            delta_turn(k, s, shared, turn, keep)
            with nc.Block() as block:
                @block.sync
                def _(sp):
                    for sem in counted:
                        sp.sem_clear(sem)


def delta_turn(k, s, b, turn, keep):
    nc = k.nc
    flat, masks = b.flat, b.masks
    A, AT, BT, X, XT, UX = b.A, b.AT, b.BT, b.X, b.XT, b.UX

    def bank4(bank):
        return bank[:, 0:512].rearrange("p (u t) -> p u t", u=4)

    def by_unit(x):
        return x.rearrange("p h (r t) -> p r h t", r=2)

    with nc.Block() as block:
        @block.gpsimd
        def _(pool):
            pool.tensor_copy(b.bg[:, 0].rearrange("p (r h) -> p r h", r=2), keep.beta[:, :, bass.ds(2 * turn, 2)]).then_inc(s.took, 1)
            pool.tensor_copy(b.bg[:, 1].rearrange("p (r h) -> p r h", r=2), keep.g[:, :, bass.ds(2 * turn, 2)]).then_inc(s.took, 1)

        @block.scalar
        def _(act):
            act.activation(b.q, k.feat[:, bass.ds(4 * turn, 4)].rearrange("p (h c) t -> p h c t", c=2)[:, :, 0], ACT.Copy)\
               .then_inc(s.cleared, 1)
            act.wait_ge(s.chain, 2)
            act.activation(b.sc[:, 2], b.sums[:, 0], ACT.Exp).then_inc(s.exps, 1)
            act.activation(b.sc[:, 3], b.sc[:, 1], ACT.Exp).then_inc(s.exps, 1)
            act.wait_ge(s.steps1, 2)
            for u in range(4):
                act.activation(b.decay[:, u], b.decay[:, u], ACT.Exp, bias=b.sums[:, 0, u:u + 1]).then_inc(s.exps, 1)
            for u in range(4):
                act.activation(b.decay_t[:, u], b.decay_t[:, u], ACT.Exp, bias=b.sc[:, 0, u:u + 1]).then_inc(s.exps, 1)
            act.wait_ge(s.rows, 1)
            act.activation(b.grown[:], bank4(k.aux[2]), ACT.Exp).then_inc(s.exps, 1)
            act.wait_ge(s.aturned, 1)
            act.activation(AT, bank4(k.z[2]), ACT.Copy).then_inc(s.acopied, 1)
            for level in range(1, 6):
                act.wait_ge(s.ux, level)
                act.activation(UX[:], bank4(k.aux[3]), ACT.Copy).then_inc(s.ucopied, 1)
            act.wait_ge(s.uw, 1)
            act.activation(b.U[:], bank4(k.aux[0]), ACT.Copy).then_inc(s.acopied, 1)
            act.wait_ge(s.so, 8)
            act.activation(UX[:], bank4(k.z[2]), ACT.Square).then_inc(s.sq, 1)
            act.wait_ge(s.osum, 1)
            act.activation(b.std, bank4(k.z[3]), ACT.Sqrt, bias=k.eps[:], scale=1.0 / C_DIM).then_inc(s.std, 1)
            act.wait_ge(s.gout, 3)
            act.activation(k.y_hi[:, bass.ds(10 + 2 * turn, 2)], b.rstd.rearrange("p u t -> p (u t)").rearrange("p (h t) -> p h t", h=2),
                           ACT.Copy).then_inc(s.yrounded, 1)

        @block.tensor
        def _(pe):
            pe.wait_ge(s.cleared, 3)
            for bank, src in ((k.aux[0], b.kk_), (k.aux[1], b.v)):
                for u in range(4):
                    ins = pe.transpose(bank[:, P * u:P * u + P], src[:, u % 2, P * (u // 2):P * (u // 2) + P], k.ident[:])
                ins.then_inc(s.kv_turned, 1)
            pe.wait_ge(s.took, 2)
            pe.matmul(k.aux[3][:, 0:4], b.cumulate[:], b.bg[:, 1], start=True, stop=True).then_inc(s.sums, 1)
            pe.matmul(k.aux[3][:, 4:8], k.blocks[:], b.bg[:, 1], start=True, stop=True).then_inc(s.sums, 1)
            for u in range(4):
                ins = pe.matmul(k.aux[2][:, P * u:P * u + P], b.bg[:, 1, u:u + 1].to_broadcast([P, P]), b.cumulate[:],
                                start=True, stop=True)
            ins.then_inc(s.rows, 1)
            for bank, right in ((k.z[0], b.kk_), (k.z[1], b.q)):
                for u in range(4):
                    t = slice(P * (u // 2), P * (u // 2) + P)
                    ins = pe.matmul(bank[:, P * u:P * u + P], b.kk_[:, u % 2, t], right[:, u % 2, t], start=True, stop=True)
                ins.then_inc(s.kk, 1)
            pe.wait_ge(s.amat, 5)
            for u in range(4):
                ins = pe.transpose(k.z[2][:, P * u:P * u + P], A[:, u], k.ident[:])
            ins.then_inc(s.aturned, 1)
            for level in range(1, 6):
                pe.wait_ge(s.bt, level)
                pe.wait_ge(s.xstep, 2 * level)
                for u in range(4):
                    ins = pe.matmul(k.aux[3][:, P * u:P * u + P], BT[:, u], X[:, u], start=True, stop=True)
                ins.then_inc(s.ux, 1)
                pe.wait_ge(s.ucopied, level)
                for u in range(4):
                    ins = pe.matmul(k.z[2][:, P * u:P * u + P], XT[:, u], UX[:, u], start=True, stop=True)
                ins.then_inc(s.xx, 1)
                for u in range(4):
                    ins = pe.matmul(k.z[3][:, P * u:P * u + P], UX[:, u], XT[:, u], start=True, stop=True)
                ins.then_inc(s.xx, 1)
            pe.wait_ge(s.xstep, 12)
            pe.wait_ge(s.tok, 13)
            for u in range(4):
                ins = pe.matmul(k.aux[0][:, P * u:P * u + P], XT[:, u], b.v_beta[:, u], start=True, stop=True)
            ins.then_inc(s.uw, 1)
            for u in range(4):
                ins = pe.matmul(k.aux[1][:, P * u:P * u + P], b.k_beta[:, u], XT[:, u], start=True, stop=True)
            ins.then_inc(s.uw, 1)
            for c in range(4):
                r, off = c // 2, (c % 2) * CHUNK
                rows = slice(off, off + CHUNK)
                if c == 0:
                    pe.wait_ge(s.vnew, 3)
                    pe.wait_ge(s.gout, 1)
                else:
                    pe.wait_ge(s.sstate, 2 * c)
                for h in range(2):
                    ins = pe.matmul(k.aux[3][rows, P * h:P * h + P], b.WT[:, 2 * r + h, rows], b.S[:, h], start=True, stop=True)
                ins.then_inc(s.ws, 1)
                pe.wait_ge(s.vnew, 4 + c)
                for h in range(2):
                    u = 2 * r + h
                    out = k.z[2][:, T * h + CHUNK * c:T * h + CHUNK * c + CHUNK]
                    pe.matmul(out, b.S[:, h], b.q_grown[:, u, rows], start=True, stop=False)
                    pe.matmul(out, b.vn[:, h], b.intra[:, u, rows], start=False, stop=True).then_inc(s.so, 1)
                for h in range(2):
                    ins = pe.matmul(k.aux[2][:, P * h:P * h + P], b.k_end[rows, 2 * r + h], b.vn[rows, h], start=True, stop=True)
                ins.then_inc(s.kvp, 1)
            pe.wait_ge(s.sq, 1)
            pe.matmul(k.z[3][:, 0:2 * T], k.ones[:], flat(UX[:]), start=True, stop=True).then_inc(s.osum, 1)

        @block.vector
        def _(dve):
            heads = k.feat[:, bass.ds(4 * turn, 4)].rearrange("p (h c) t -> p h c t", c=2)
            dve.tensor_copy(b.kk_, heads[:, :, 1]).then_inc(s.cleared, 1)
            dve.tensor_copy(b.v, keep.v_all[:, bass.ds(2 * turn, 2)]).then_inc(s.cleared, 1)
            dve.wait_ge(s.took, 2)
            dve.wait_ge(s.sums, 2)
            link = chain(dve, s.chain)
            link(lambda: dve.tensor_copy(b.sums[:].rearrange("p a u -> p (a u)"), k.aux[3][:, 0:8]))
            dve.tensor_scalar(b.sc[:, 0], b.sums[:, 0], -1.0, None, ALU.mult).then_inc(s.ez, 1)
            link(lambda: dve.tensor_tensor(b.sc[:, 1], b.sums[:, 1], b.sums[:, 0], ALU.subtract))
            dve.wait_ge(s.ez, 1)
            dve.wait_ge(s.rows, 1)
            dve.scalar_tensor_tensor(out=b.decay[:], in0=bank4(k.aux[2]), scalar=-1.0, in1=masks(b.not_after),
                                     op0=ALU.mult, op1=ALU.add).then_inc(s.steps1, 1)
            dve.tensor_tensor(b.decay_t[:], bank4(k.aux[2]), masks(b.not_before), ALU.add).then_inc(s.steps1, 1)
            dve.wait_ge(s.kv_turned, 2)
            dve.tensor_copy(b.k_tok[:], bank4(k.aux[0])).then_inc(s.tok, 1)
            for u in range(4):
                dve.tensor_scalar(b.v_beta[:, u], k.aux[1][:, P * u:P * u + P], b.bg[:, 0, u:u + 1], None, ALU.mult)\
                   .then_inc(s.tok, 1)
            dve.wait_ge(s.exps, 2)
            link(lambda: dve.tensor_tensor(b.sc[:, 4], b.sc[:, 2], b.bg[:, 0], ALU.mult))
            dve.wait_ge(s.tok, 1)
            for u in range(4):
                dve.tensor_scalar(b.k_beta[:, u], b.k_tok[:, u], b.sc[:, 4, u:u + 1], None, ALU.mult).then_inc(s.tok, 1)
                dve.tensor_scalar(b.k_end[:, u], b.k_tok[:, u], b.sc[:, 3, u:u + 1], None, ALU.mult).then_inc(s.tok, 1)
            dve.wait_ge(s.kk, 2)
            dve.wait_ge(s.exps, 10)
            for u in range(4):
                dve.scalar_tensor_tensor(out=A[:, u], in0=k.z[0][:, P * u:P * u + P], scalar=b.bg[:, 0, u:u + 1],
                                         in1=b.decay[:, u], op0=ALU.mult, op1=ALU.mult).then_inc(s.amat, 1)
            dve.wait_ge(s.amat, 4)
            dve.tensor_tensor(A, A, masks(b.strict), ALU.mult).then_inc(s.amat, 1)
            dve.tensor_tensor(b.intra[:], bank4(k.z[1]), b.decay_t[:], ALU.mult).then_inc(s.steps1, 1)
            dve.wait_ge(s.amat, 5)
            dve.tensor_tensor(X, A, masks(b.levels[:, 0]), ALU.mult).then_inc(s.xstep, 1)
            dve.wait_ge(s.xstep, 1)
            dve.tensor_tensor(X, X, masks(k.ident), ALU.add).then_inc(s.xstep, 1)
            dve.wait_ge(s.acopied, 1)
            link(lambda: dve.tensor_tensor(XT, AT, masks(b.levels_t[:, 0]), ALU.mult))
            link(lambda: dve.tensor_tensor(XT, XT, masks(k.ident), ALU.add))
            for level in range(1, 6):
                if level > 1:
                    dve.wait_ge(s.ux, level - 1)
                dve.tensor_tensor(BT, AT, masks(b.levels_t[:, level]), ALU.mult).then_inc(s.bt, 1)
                dve.wait_ge(s.xx, 2 * level - 1 + 1)
                dve.tensor_tensor(X, bank4(k.z[2]), X, ALU.add).then_inc(s.xstep, 1)
                dve.tensor_tensor(XT, bank4(k.z[3]), XT, ALU.add).then_inc(s.xstep, 1)
            dve.memset(b.S[:], 0.0).then_inc(s.vnew, 1)
            dve.memset(b.vn[:], 0.0).then_inc(s.vnew, 1)
            dve.wait_ge(s.exps, 11)
            dve.wait_ge(s.ux, 5)
            dve.tensor_tensor(b.q_grown.rearrange("p (r h) t -> p r h t", r=2), by_unit(b.q),
                              b.grown[:].rearrange("p (r h) t -> p r h t", r=2), ALU.mult).then_inc(s.gout, 1)
            dve.wait_ge(s.uw, 2)
            dve.tensor_copy(b.WT[:], bank4(k.aux[1])).then_inc(s.vnew, 1)
            dve.wait_ge(s.acopied, 2)
            for c in range(4):
                r, off = c // 2, (c % 2) * CHUNK
                rows = slice(off, off + CHUNK)
                dve.wait_ge(s.ws, c + 1)
                if c:
                    dve.wait_ge(s.kvp, c)
                else:
                    dve.wait_ge(s.vnew, 3)
                dve.tensor_tensor(b.vn[rows], b.U[rows, 2 * r:2 * r + 2],
                                  k.aux[3][rows, 0:2 * P].rearrange("p (h t) -> p h t", h=2), ALU.subtract).then_inc(s.vnew, 1)
                dve.wait_ge(s.kvp, c + 1)
                for h in range(2):
                    dve.scalar_tensor_tensor(out=b.S[:, h], in0=b.S[:, h], scalar=b.grown[:, 2 * r + h, off + CHUNK - 1:off + CHUNK],
                                             in1=k.aux[2][:, P * h:P * h + P], op0=ALU.mult, op1=ALU.add).then_inc(s.sstate, 1)
            dve.wait_ge(s.std, 1)
            dve.reciprocal(b.rstd, b.std).then_inc(s.gout, 1)
            dve.wait_ge(s.gout, 2)
            dve.wait_ge(s.so, 8)
            dve.scalar_tensor_tensor(out=flat(UX[:]), in0=k.z[2][:, 0:512], scalar=b.onorm[:, 0:1], in1=flat(b.rstd), op0=ALU.mult,
                                     op1=ALU.mult).then_inc(s.ylo, 1)
            dve.wait_ge(s.ylo, 1)
            y2 = flat(b.rstd).rearrange("p (h t) -> p h t", h=2)
            dve.tensor_tensor(y2, flat(UX[:]).rearrange("p (h t) -> p h t", h=2), keep.z_all[:, bass.ds(2 * turn, 2)], ALU.mult)\
               .then_inc(s.gout, 1)
            dve.wait_ge(s.yrounded, 1)
            dve.tensor_tensor(k.y_lo[:, bass.ds(10 + 2 * turn, 2)], y2, k.y_hi[:, bass.ds(10 + 2 * turn, 2)].bitcast(F32),
                              ALU.subtract).then_inc(s.ylo, 1)


def out_phase_1(k, x_dram):
    nc = k.nc
    with phase(nc, "out1", STREAM + "params xin merged_hi merged_lo copied acc sq summed std norm step cleared") as s:
        stream = Stream(k, s, k.w1, SLOT_OUT_1)
        o = s.sbuf("o", [P, KT, T])
        acc, sq = s.sbuf("acc", [P, T]), s.sbuf("sq", [P, 4, T])
        std, rstd = s.sbuf("std", [P, T]), s.sbuf("rstd", [P, T])
        w = s.sbuf("w", [P, KT])
        passes = KT // 4
        with nc.Block() as block:
            @block.sync
            def _(sp):
                sp.dma_start(w[:], k.p1[:, P1_POST:P1_POST + KT]).then_inc(s.params, 16)
                for i in range(1):
                    stream.load(sp, 0, 0)
                    stream.load(sp, 0, 1)
                sp.wait_ge(s.merged_lo, 4)
                sp.dma_start(k.feat[:], x_dram).then_inc(s.xin, 16)
                stream.load(sp, 0, 2)
                stream.load(sp, 0, 3)
                with sp.Fori(1, passes) as i:
                    stream_steps(sp, stream.load)(i)

            @block.scalar
            def _(act):
                for q in range(4):
                    act.activation(k.xn_hi[:, 4 * q:4 * q + 4], k.feat[:, 4 * q:4 * q + 4], ACT.Copy).then_inc(s.merged_hi, 1)

                def copies(i):
                    act.wait_ge(s.acc, 4 * i + 4)
                    for half in range(2):
                        act.wait_ge(s.used, stream.done(i, 2 * half + 1))
                        for b in (2 * half, 2 * half + 1):
                            act.activation(sq[:, b], k.z[b][:, 0:T], ACT.Square).then_inc(s.sq, 1)
                        for b in (2 * half, 2 * half + 1):
                            act.activation(o[:, bass.ds(4 * i + b, 1)], k.z[b][:, None, 0:T], ACT.Copy).then_inc(s.copied, 1)
                pipelined(act, passes, [(0, stream_steps(act, stream.round)), (1, copies)])
                act.wait_ge(s.summed, 1)
                act.activation(std[:], k.aux[0][:, 0:T], ACT.Sqrt, bias=k.eps[:], scale=1.0 / D).then_inc(s.std, 1)

            @block.vector
            def _(dve):
                stream.open_dve(dve)
                dve.sem_inc(s.acc, 4)
                dve.memset(acc[:], 0.0).then_inc(s.cleared, 1)
                dve.wait_ge(s.cleared, 1)
                for q in range(4):
                    dve.wait_ge(s.merged_hi, q + 1)
                    dve.tensor_tensor(k.xn_lo[:, 4 * q:4 * q + 4], k.feat[:, 4 * q:4 * q + 4],
                                      k.xn_hi[:, 4 * q:4 * q + 4].bitcast(F32), ALU.subtract).then_inc(s.merged_lo, 1)

                def sums(i):
                    dve.wait_ge(s.sq, 4 * i + 4)
                    for b in range(4):
                        dve.tensor_tensor(acc[:], acc[:], sq[:, b], ALU.add).then_inc(s.acc, 1)
                        dve.wait_ge(s.acc, 4 * i + 5 + b)
                pipelined(dve, passes, [(0, stream_steps(dve, stream.residual)), (1, sums)])
                dve.wait_ge(s.std, 1)
                dve.reciprocal(rstd[:], std[:]).then_inc(s.norm, 1)
                dve.wait_ge(s.norm, 1)
                dve.wait_ge(s.params, 16)
                dve.wait_ge(s.xin, 16)
                for t in range(KT):
                    dve.scalar_tensor_tensor(out=o[:, t], in0=o[:, t], scalar=w[:, t:t + 1], in1=rstd[:], op0=ALU.mult,
                                             op1=ALU.mult).then_inc(s.norm, 1)
                for q in range(4):
                    dve.wait_ge(s.norm, 4 * q + 5)
                    f = k.feat[:, 4 * q:4 * q + 4]
                    dve.tensor_tensor(f, f, o[:, 4 * q:4 * q + 4], ALU.add).then_inc(s.step, 1)

            @block.tensor
            def _(pe):
                stream.open_pe(pe)
                pe.sem_inc(s.copied, 4)
                pe.wait_ge(s.merged_lo, 4)

                def products(i):
                    for sl in range(SLOTS):
                        if sl % 2 == 0:
                            pe.wait_ge(s.copied, 4 * i + 2 + sl)
                        stream.multiply(pe, i, sl, k.xn_hi, k.xn_lo)
                pipelined(pe, passes, [(0, products)])
                pe.wait_ge(s.acc, 4 * passes + 4)
                pe.matmul(k.aux[0][:, 0:T], k.ones[:], acc[:], start=True, stop=True).then_inc(s.summed, 1)


def out_phase_2(k, layer, state, out):
    nc = k.nc
    with phase(nc, "out2", STREAM + "xin added stored") as s:
        stream = Stream(k, s, k.w2, layer * SLOTS_2 + SLOT_OUT_2)
        passes = KT // 4
        with nc.Block() as block:
            @block.sync
            def _(sp):
                sp.dma_start(k.feat[:], state).then_inc(s.xin, 16)
                pipelined(sp, passes, [(0, stream_steps(sp, stream.load))])
                sp.wait_ge(s.added, 4 * passes + 4)
                sp.dma_start(out, k.feat[:]).then_inc(s.stored, 16)
                sp.wait_ge(s.stored, 16)

            @block.scalar
            def _(act):
                pipelined(act, passes, [(0, stream_steps(act, stream.round))])

            @block.vector
            def _(dve):
                stream.open_dve(dve)

                def add(i):
                    for b in range(4):
                        dve.wait_ge(s.used, stream.done(i, 1 if b < 2 else 3))
                        f = k.feat[:, bass.ds(4 * i + b, 1)]
                        dve.tensor_tensor(f, k.z[b][:, None, 0:T], f, ALU.add).then_inc(s.added, 1)

                def await_x(i):
                    dve.wait_ge(s.xin, 16)
                pipelined(dve, passes, [(0, stream_steps(dve, stream.residual)), (0, await_x), (1, add)])

            @block.tensor
            def _(pe):
                stream.open_pe(pe)
                pe.sem_inc(s.added, 4)

                def products(i):
                    for sl in range(SLOTS):
                        if sl % 2 == 0:
                            pe.wait_ge(s.added, 4 * i + 2 + sl)
                        stream.multiply(pe, i, sl, k.y_hi, k.y_lo)
                pipelined(pe, passes, [(0, products)])


class Kernel:
    pass


def build(nc, t, stop=None):
    with ExitStack() as stack:
        def sbuf(name, shape, dt=F32):
            return stack.enter_context(nc.sbuf_tensor(name, shape, dt))
        k = Kernel()
        k.nc = nc
        k.constants, k.w1, k.w2, k.p1, k.p2 = t["constants"], t["w1"], t["w2"], t["p1"], t["p2"]
        k.lru_w, k.pw, k.w12, k.rows_c = t["lru_w"], t["pw"], t["w12"], t["rows_c"]
        k.w_raw = sbuf("w_raw", [P, RAW, SLOT_K, CHUNK_COLS])
        k.w_hi = sbuf("w_hi", [P, SLOTS, SLOT_K, CHUNK_COLS], F32R)
        k.w_lo = sbuf("w_lo", [P, SLOTS, SLOT_K, CHUNK_COLS], F32R)
        k.xn_hi, k.xn_lo = sbuf("xn_hi", [P, KT, T], F32R), sbuf("xn_lo", [P, KT, T], F32R)
        k.y_hi, k.y_lo = sbuf("y_hi", [P, KT, T], F32R), sbuf("y_lo", [P, KT, T], F32R)
        k.feat = sbuf("feat", [P, KT, T])
        k.ident, k.ones, k.blocks = sbuf("ident", [P, P]), sbuf("ones", [P, P]), sbuf("blocks", [P, P])
        k.eps = sbuf("eps", [P, 1])
        k.cos_t, k.sin_t = sbuf("cos_t", [P, T]), sbuf("sin_t", [P, T])
        k.z = [stack.enter_context(nc.psum_tensor(f"z{n}", [P, 2 * T], F32)) for n in range(4)]
        k.aux = [stack.enter_context(nc.psum_tensor(f"aux{n}", [P, 2 * T], F32)) for n in range(4)]

        setup_phase(k)
        norm_phase(k, "norm1", t["p1"][:, P1_NORM:P1_NORM + KT], t["x"], None)
        lru_phase(k)
        if stop == "lru":
            return dump(k, t)
        merge_phase(k, "merge_a", SLOT_MERGE_A, True)
        rope_tables(k, "rope1", None, "freq_1")
        if stop == "rope":
            return dump(k, t)
        attention_phase(k, "att1", record(
            heads_per_tile=1, n_heads=16, passes=8, weights=k.w1, first_slot=SLOT_ATT_1, kv_width=512, turn="turn_1",
            mask="window_1", sinks=t["sinks_1"], norms=None, scale=HEAD_DIM_1 ** -0.5))
        if stop == "att1":
            return dump(k, t)
        merge_phase(k, "merge_b", SLOT_MERGE_B, False)
        out_phase_1(k, t["x"])
        if stop == "block1":
            return dump(k, t)
        rope_tables(k, "rope2", t["positions"], "freq_2")
        with nc.Fori(0, LAYERS) as layer:
            norm_phase(k, "norm2", t["p2"][bass.ds(layer, 1), :, P2_NORM:P2_NORM + KT].rearrange("a p n -> p (a n)"),
                       None, t["state"])
            attention_phase(k, "att2", record(
                heads_per_tile=2, n_heads=HEADS_2, passes=3, weights=k.w2, first_slot=layer * SLOTS_2 + SLOT_ATT_2,
                kv_width=256, turn="turn_2", mask="window_2", sinks=t["sinks_2"][bass.ds(layer, 1)],
                norms=t["p2"][bass.ds(layer, 1), :, P2_QN:P2_KN + 1].rearrange("a p n -> p (a n)"),
                scale=HEAD_DIM_2 ** -0.5))
            if stop == "att2":
                pass
            else:
                conv_phase(k, layer)
                with ExitStack() as kept:
                    keep = record(**{n: kept.enter_context(nc.sbuf_tensor(f"keep_{n}", shape, F32)) for n, shape in (
                        ("v_all", [P, C_HEADS, T]), ("z_all", [P, C_HEADS, T]), ("beta", [P, 2, C_HEADS]),
                        ("g", [P, 2, C_HEADS]))})
                    delta_inputs_phase(k, layer, keep)
                    delta_phase(k, layer, keep)
            out_phase_2(k, layer, t["state"], t["out"])
        if stop == "att2":
            dump(k, t)


def dump(k, t):
    nc = k.nc
    with nc.semaphore("dumped") as sem:
        with nc.Block() as block:
            @block.sync
            def _(sp):
                for name, src in (("feat", k.feat[:]), ("y_hi", k.y_hi[:].bitcast(F32)), ("y_lo", k.y_lo[:].bitcast(F32)),
                                  ("cos", k.cos_t[:]), ("sin", k.sin_t[:])):
                    if "dbg_" + name in t and not (name in ("cos", "sin") and "no_rope" in t):
                        sp.dma_start(t["dbg_" + name], src).then_inc(sem, 16)
                sp.wait_ge(sem, 80 if "dbg_cos" in t else 48)


def slots_of(matrix, column_tiles):
    out = []
    for a, b in zip(column_tiles[0::2], column_tiles[1::2]):
        chunk = np.concatenate([matrix[:, a:a + P], matrix[:, b:b + P]], 1)
        halves = chunk.reshape(2, SLOT_K, P, CHUNK_COLS).transpose(0, 2, 1, 3)
        out.append(halves.reshape(2, P, SLOT_K * CHUNK_COLS))
    return np.concatenate(out, 0)


def tiles(start, n):
    return [start + P * j for j in range(n)]


def by_partition(v):
    v = np.asarray(v)
    return v.reshape(-1, P).T


def lay_out(x, norm_pre_w, w_in, conv_w, conv_b, lru_w_r, lru_b_r, lru_w_i, lru_b_i, lru_lambda, attn_sink, w_proj_a,
            w_proj_b, w_out, norm_post_w, positions_2, norm_w_2, w_in_2, q_norm_w_2, k_norm_w_2, sinks_2, b_conv_w_2,
            b_conv_b_2, b_ln_w_2, b_ln_b_2, b_pw_w_2, b_pw_b_2, c_conv_w_2, c_a_log_2, c_dt_bias_2, c_onorm_w_2, w_out_2):
    a = {"x": x[0].T.reshape(KT, P, T).transpose(1, 0, 2)}
    u0, g0, q0 = 0, D, 2 * D
    k0, v0 = 3 * D, 3 * D + 512
    ga0, ml0, ma0 = 3 * D + 1024, 4 * D + 1024, 5 * D + 1024
    w = w_in[0]
    lru = [c for i in range(8) for s in (u0, g0) for c in tiles(s + 256 * i, 2)]
    att = tiles(k0, 4) + tiles(v0, 4) + [c for i in range(8) for s in (q0, ga0) for c in tiles(s + 256 * i, 2)]

    def merged(m0, proj):
        m, p_ = slots_of(w, tiles(m0, KT)), slots_of(proj, tiles(0, KT))
        return np.stack([m.reshape(8, 2, P, -1), p_.reshape(8, 2, P, -1)], 1).reshape(32, P, -1)
    a["w1"] = np.concatenate([slots_of(w, lru), merged(ml0, w_proj_a[0]), slots_of(w, att), merged(ma0, w_proj_b[0]),
                              slots_of(w_out[0], tiles(0, KT))], 0)
    a["p1"] = np.concatenate([by_partition(v) for v in (norm_pre_w, conv_w, conv_b, lru_b_r, lru_b_i, lru_lambda, norm_post_w)], 1)
    lw = np.stack([lru_w_r[0], lru_w_i[0]], 0)
    a["lru_w"] = lw.transpose(2, 3, 1, 0, 4).reshape(8, 2, P, 4, P).transpose(0, 2, 1, 3, 4).reshape(8, P, 8 * P)
    a["sinks_1"] = attn_sink
    a["sinks_2"] = sinks_2
    a["positions"] = positions_2
    widths = (768, 256, 256, 768, 512, 512, 512, 768, 768, 768, 6, 6, 768)
    q_, k_, v_, za, ba, bg, zb, cq, ck, cv, b_, a_, zc = np.cumsum((0,) + widths[:-1]).tolist()
    order = tiles(k_, 2) + tiles(v_, 2) + [c for i in range(3) for s in (q_, za) for c in tiles(s + 256 * i, 2)]
    order += tiles(ba, 2) + tiles(bg, 2) + tiles(ba + 256, 2) + tiles(bg + 256, 2) + tiles(zb, 4)
    order += [s + P * h for h in range(C_HEADS) for s in (cq, ck, cv, zc)]
    a["w2"] = np.concatenate([np.concatenate([slots_of(w_in_2[l], order), slots_of(w_out_2[l], tiles(0, KT))], 0)
                              for l in range(LAYERS)], 0)
    a["w12"] = w_in_2[:, :, b_:b_ + 12].reshape(LAYERS, KT, P, 12).transpose(0, 2, 1, 3).reshape(LAYERS, P, KT * 12)
    rows = []
    for l in range(LAYERS):
        qn, kn = (np.concatenate([v[l], v[l]])[:, None] for v in (q_norm_w_2, k_norm_w_2))
        cc = c_conv_w_2[l].reshape(TAPS_C, 3, C_HEADS, P).transpose(3, 0, 2, 1).reshape(P, -1)
        rows.append(np.concatenate([by_partition(norm_w_2[l]), qn, kn, c_onorm_w_2[l][:, None], by_partition(b_conv_w_2[l]),
                                    by_partition(b_conv_b_2[l]), by_partition(b_ln_w_2[l]), by_partition(b_ln_b_2[l]),
                                    by_partition(b_pw_b_2[l]), cc], 1))
    a["p2"] = np.stack(rows, 0)
    a["pw"] = b_pw_w_2.reshape(LAYERS, B_TILES, P, B_TILES * P).transpose(0, 2, 1, 3).reshape(LAYERS, P, -1)
    a["rows_c"] = np.concatenate([c_a_log_2, c_dt_bias_2], 1)
    a["constants"] = CONSTANTS
    return {n: np.ascontiguousarray(v) for n, v in a.items()}


def kernel(**inputs):
    import concourse.bacc as bacc
    from concourse.bass_utils import run_bass_kernel_spmd

    arrays = lay_out(**{n: np.asarray(v) for n, v in inputs.items()})
    nc = bacc.Bacc("TRN2", target_bir_lowering=False, num_devices=1)
    t = {n: nc.dram_tensor(f"in_{n}_dram", v.shape, mybir.dt.from_np(v.dtype), kind="ExternalInput").ap()
         for n, v in arrays.items()}
    t["out"] = nc.dram_tensor("out_0_dram", (P, KT, T), F32, kind="ExternalOutput").ap()
    t["state"] = nc.dram_tensor("state_dram", (P, KT, T), F32, kind="Internal").ap()
    build(nc, t)
    r = run_bass_kernel_spmd(nc, [{f"in_{n}_dram": v for n, v in arrays.items()}], core_ids=[0])
    y = r.results[0]["out_0_dram"]
    return np.ascontiguousarray(y.transpose(2, 1, 0).reshape(1, T, D))
```

```python
import math
from collections import namedtuple
from contextlib import ExitStack, contextmanager

import numpy as np

import concourse.bass as bass
from concourse import mybir

F32 = mybir.dt.float32
F32R = mybir.dt.float32r
I32 = mybir.dt.int32
ACT = mybir.ActivationFunctionType
ALU = mybir.AluOpType
AX_X = mybir.AxisListType.X

P = 128
D = 2048
T = 256
KT = D // P
CHUNK_COLS = 256
SLOT_K = KT // 2
SLOTS = 4
RAW = 2
NORM_EPS = 1e-6
NEG = -1e30
ROPE_THETA = 500000.0

LRU_PASSES = KT // 2
KV_HEADS_1, HEAD_DIM_1, ROT_1 = 4, 128, 32
LAYERS = 2
HEAD_DIM_2, HEADS_2, ROT_2 = 64, 12, 16
B_TILES = 4
TAPS_B = 31
C_HEADS, C_DIM, CHUNK = 6, 128, 64
TAPS_C = 4

SLOT_LRU = 0
SLOT_MERGE_A = SLOT_LRU + 4 * LRU_PASSES
SLOT_ATT_1 = SLOT_MERGE_A + 4 * (KT // 2)
SLOT_MERGE_B = SLOT_ATT_1 + 4 * 2 + 4 * (KT // 2)
SLOT_OUT_1 = SLOT_MERGE_B + 4 * (KT // 2)
SLOTS_1 = SLOT_OUT_1 + 2 * (KT // 2)
SLOT_ATT_2 = 0
SLOT_CONV_2 = SLOT_ATT_2 + 4 + 4 * 3
SLOT_DELTA_2 = SLOT_CONV_2 + 4 * 3
SLOT_OUT_2 = SLOT_DELTA_2 + 4 * C_HEADS
SLOTS_2 = SLOT_OUT_2 + 2 * (KT // 2)

P1_NORM, P1_CONV, P1_CONVB = 0, 16, 80
P1_BR, P1_BI, P1_LAM, P1_POST = 96, 128, 160, 192
P1_COLS = 208
P2_NORM, P2_QN, P2_KN, P2_ONORM = 0, 16, 17, 18
P2_BCONV, P2_BCONVB, P2_LNW, P2_LNB, P2_PWB = 19, 19 + 124, 147, 151, 155
P2_CCONV = 159
P2_COLS = P2_CCONV + TAPS_C * 3 * C_HEADS


def constant_columns():
    cols, parts, at = {}, [], 0

    def put(name, a):
        nonlocal at
        a = np.asarray(a, np.float32).reshape(P, -1)
        cols[name] = (at, a.shape[1])
        parts.append(a)
        at += a.shape[1]

    i, j = np.arange(P)[:, None], np.arange(P)[None, :]
    same = i // CHUNK == j // CHUNK
    put("ident", i == j)
    put("ones", np.ones((P, P)))
    put("blocks", same)
    put("cumulate", same & (i <= j))
    put("not_after", np.where(same & (j <= i), 0.0, NEG))
    put("not_before", np.where(same & (j >= i), 0.0, NEG))
    put("strict", same & (j < i))
    for name, flip in (("levels", False), ("levels_t", True)):
        masks = []
        for level in range(6):
            b = 1 << level
            m = -1.0 * ((i // (2 * b) == j // (2 * b)) & (i // b % 2 == 1) & (j // b % 2 == 0))
            masks.append(m.T if flip else m)
        put(name, np.stack(masks, 1))
    q = np.arange(P)[:, None, None] + P * np.arange(2)[None, :, None]
    s = np.arange(T)[None, None, :]
    put("window_1", np.where(np.abs(q - s) <= 128, 0.0, NEG))
    put("window_2", np.where((q - s >= 0) & (q - s < 128), 0.0, NEG))
    for name, rot, head in (("1", ROT_1, HEAD_DIM_1), ("2", ROT_2, HEAD_DIM_2)):
        half = rot // 2
        freq = ROPE_THETA ** (-np.arange(0, rot, 2, dtype=np.float64) / rot)
        column, turn = np.zeros(P), np.zeros((P, P))
        for base in range(0, P, head):
            for d in range(rot):
                column[base + d] = freq[d % half]
            for d in range(half):
                turn[base + d + half, base + d] = -1.0
                turn[base + d, base + d + half] = 1.0
        put("freq_" + name, np.stack([column, column], 1))
        put("turn_" + name, turn)
    return cols, np.concatenate(parts, 1)


CONST_COLS, CONSTANTS = constant_columns()


def record(**fields):
    return namedtuple("Record", fields.keys())(*fields.values())


@contextmanager
def phase(nc, name, sems):
    with ExitStack() as stack:
        def sbuf(n, shape, dt=F32):
            return stack.enter_context(nc.sbuf_tensor(f"{name}_{n}", shape, dt))
        named = {n: stack.enter_context(nc.semaphore(f"{name}_{n}")) for n in sems.split()}
        s = record(**named, sbuf=sbuf, all=list(named.values()))
        yield s
        with nc.Block() as block:
            @block.sync
            def _(sp):
                for sem in s.all:
                    sp.sem_clear(sem)


STREAM = "loaded0 loaded1 rounded split used "


class Stream:

    def __init__(self, k, s, first):
        self.k, self.s, self.first = k, s, first
        self.loaded = (s.loaded0, s.loaded1)

    def open_act(self, act):
        act.sem_inc(self.s.rounded, SLOTS)

    def open_dve(self, dve):
        dve.sem_inc(self.s.split, RAW + SLOTS)

    def open_pe(self, pe, free=SLOTS):
        pe.sem_inc(self.s.used, free)

    def load(self, sp, i, s):
        sp.wait_ge(self.s.split, 4 * i + s + 1)
        src = self.k.w[bass.ds(self.first + 4 * i + s, 1)].rearrange("a p n -> p (a n)")
        dst = self.k.w_raw[:, s % RAW].rearrange("p k n -> p (k n)")
        sp.dma_start(dst, src).then_inc(self.loaded[s % RAW], 16)

    def round(self, act, i, s):
        act.wait_ge(self.loaded[s % RAW], 16 * (2 * (i - 1) + s // RAW + 1))
        act.wait_ge(self.s.used, 4 * i + s + 1)
        act.activation(self.k.w_hi[:, s], self.k.w_raw[:, s % RAW], ACT.Copy).then_inc(self.s.rounded, 1)

    def residual(self, dve, i, s):
        dve.wait_ge(self.s.rounded, 4 * i + s + 1)
        dve.tensor_tensor(self.k.w_lo[:, s], self.k.w_raw[:, s % RAW], self.k.w_hi[:, s].bitcast(F32),
                          ALU.subtract).then_inc(self.s.split, 1)

    def loads(self, sp, passes):
        with sp.Fori(1, passes + 1) as i:
            for s in range(SLOTS):
                self.load(sp, i, s)

    def multiply(self, pe, i, s, hi, lo, tokens_out=False):
        k = self.k
        pe.wait_ge(self.s.split, 4 * i + s + 1 + RAW)
        for m in range(2):
            out = k.z[2 * (s // 2) + m][:, 0:T]
            for kk in range(SLOT_K):
                row = SLOT_K * (s % 2) + kk
                first, last = row == 0, row == KT - 1
                if tokens_out:
                    w_hi, w_lo = k.w_hi[:, s, kk], k.w_lo[:, s, kk]
                    x_hi, x_lo = hi[:, row, P * m:P * m + P], lo[:, row, P * m:P * m + P]
                    pairs = ((x_hi, w_hi), (x_hi, w_lo), (x_lo, w_hi))
                else:
                    w_hi, w_lo = k.w_hi[:, s, kk, P * m:P * m + P], k.w_lo[:, s, kk, P * m:P * m + P]
                    pairs = ((w_hi, hi[:, row]), (w_hi, lo[:, row]), (w_lo, hi[:, row]))
                for n, (a, b) in enumerate(pairs):
                    ins = pe.matmul(out, a, b, start=first and n == 0, stop=last and n == 2)
        ins.then_inc(self.s.used, 1)

    def done(self, i, s):
        return SLOTS + 4 * i + s + 1


def run_passes(engine, count, body, tail=None):
    body(0, False)
    if count > 4:
        with engine.Fori(1, count) as i:
            body(i, True)
    else:
        for i in range(1, count):
            body(i, True)
    if tail is not None:
        tail(count - 1)


def stream_steps(engine, act):
    def step(i):
        for s in range(SLOTS):
            act(engine, i, s)
    return step


def constant(k, name, p=P):
    at, n = CONST_COLS[name]
    return k.constants[0:p, at:at + n]


def setup_phase(k):
    nc = k.nc
    with phase(nc, "setup", "loaded") as s:
        with nc.Block() as block:
            @block.sync
            def _(sp):
                sp.dma_start(k.ident[:], constant(k, "ident")).then_inc(s.loaded, 16)
                sp.dma_start(k.ones[:], constant(k, "ones")).then_inc(s.loaded, 16)
                sp.dma_start(k.blocks[:], constant(k, "blocks")).then_inc(s.loaded, 16)
                sp.wait_ge(s.loaded, 48)

            @block.gpsimd
            def _(pool):
                pool.memset(k.eps[:], NORM_EPS)


def norm_phase(k, name, weight, source, keep, fill=False):
    nc = k.nc
    with phase(nc, name, STREAM + "x0 x1 x2 x3 weight squared summed std rstd scaled xrounded xsplit kept") as s:
        squares = s.sbuf("squares", [P, KT, T])
        std, rstd = s.sbuf("std", [P, T]), s.sbuf("rstd", [P, T])
        w = s.sbuf("w", [P, KT])
        x_loaded = (s.x0, s.x1, s.x2, s.x3)
        stream = Stream(k, s, -SLOTS)
        q4 = [slice(4 * q, 4 * q + 4) for q in range(4)]
        with nc.Block() as block:
            @block.sync
            def _(sp):
                if source is not None:
                    for q in range(4):
                        sp.dma_start(k.feat[:, q4[q]], source[:, q4[q]]).then_inc(x_loaded[q], 16)
                sp.dma_start(w[:], weight).then_inc(s.weight, 16)
                if fill:
                    for n in range(SLOTS):
                        stream.load(sp, 1, n)
                if keep is not None:
                    sp.dma_start(keep, k.feat[:]).then_inc(s.kept, 16)
                    sp.wait_ge(s.kept, 16)

            @block.scalar
            def _(act):
                for q in range(4):
                    if source is not None:
                        act.wait_ge(x_loaded[q], 16)
                    act.activation(squares[:, q4[q]], k.feat[:, q4[q]], ACT.Square).then_inc(s.squared, 1)
                if fill:
                    stream.open_act(act)
                    stream.round(act, 1, 0)
                    stream.round(act, 1, 1)
                act.wait_ge(s.summed, 1)
                act.activation(std[:], k.aux[0][:, 0:T], ACT.Sqrt, bias=k.eps[:], scale=1.0 / D).then_inc(s.std, 1)
                for q in range(4):
                    act.wait_ge(s.scaled, 4 * q + 4)
                    act.activation(k.xn_hi[:, q4[q]], squares[:, q4[q]], ACT.Copy).then_inc(s.xrounded, 1)
                if fill:
                    stream.round(act, 1, 2)
                    stream.round(act, 1, 3)

            @block.tensor
            def _(pe):
                if fill:
                    stream.open_pe(pe, 2 * SLOTS)
                for t in range(KT):
                    if t % 4 == 0:
                        pe.wait_ge(s.squared, t // 4 + 1)
                    ins = pe.matmul(k.aux[0][:, 0:T], k.ones[:], squares[:, t], start=t == 0, stop=t == KT - 1)
                ins.then_inc(s.summed, 1)

            @block.vector
            def _(dve):
                if fill:
                    stream.open_dve(dve)
                    stream.residual(dve, 1, 0)
                    stream.residual(dve, 1, 1)
                dve.wait_ge(s.weight, 16)
                dve.wait_ge(s.std, 1)
                dve.reciprocal(rstd[:], std[:]).then_inc(s.rstd, 1)
                dve.wait_ge(s.rstd, 1)
                for t in range(KT):
                    dve.scalar_tensor_tensor(out=squares[:, t], in0=k.feat[:, t], scalar=w[:, t:t + 1], in1=rstd[:],
                                             op0=ALU.mult, op1=ALU.mult).then_inc(s.scaled, 1)
                for q in range(4):
                    dve.wait_ge(s.xrounded, q + 1)
                    dve.tensor_tensor(k.xn_lo[:, q4[q]], squares[:, q4[q]], k.xn_hi[:, q4[q]].bitcast(F32),
                                      ALU.subtract).then_inc(s.xsplit, 1)
                if fill:
                    stream.residual(dve, 1, 2)
                    stream.residual(dve, 1, 3)


def softplus_tail(link, dve, x, w, z, acc):
    link(lambda: dve.tensor_scalar(z, w, 2.0, None, ALU.add))
    link(lambda: dve.reciprocal(acc, z))
    link(lambda: dve.tensor_tensor(w, w, acc, ALU.mult))
    link(lambda: dve.tensor_tensor(z, w, w, ALU.mult))
    link(lambda: dve.tensor_scalar(acc, z, 1.0 / 17, 1.0 / 15, ALU.mult, ALU.add))
    for n in range(13, 0, -2):
        link(lambda: dve.tensor_tensor(acc, acc, z, ALU.mult))
        link(lambda: dve.tensor_scalar(acc, acc, 1.0 / n, None, ALU.add))
    link(lambda: dve.tensor_tensor(acc, acc, w, ALU.mult))
    link(lambda: dve.tensor_scalar(x, x, 0.0, None, ALU.max))
    link(lambda: dve.scalar_tensor_tensor(out=x, in0=acc, scalar=2.0, in1=x, op0=ALU.mult, op1=ALU.add))


def after(engine, sem, value):
    if not (isinstance(value, int) and value == 0):
        engine.wait_ge(sem, value)


def chain(engine, sem):
    count = [0]

    def link(make):
        count[0] += 1
        make().then_inc(sem, 1)
        engine.wait_ge(sem, count[0])
    return link


def lru_phase(k):
    nc = k.nc
    CONV = 8
    DSTEPS = 8
    with phase(nc, "lru", STREAM + "gated weights params exped chain cleared ucopied conv gsig zcopied gates0 gates taken "
               "decay dsteps rounded_y ydone") as s:
        stream = Stream(k, s, SLOT_LRU)
        params = s.sbuf("params", [P, P1_COLS])
        gate_w = s.sbuf("gate_w", [P, 2, 4, P])
        padded = s.sbuf("padded", [P, 2, T + 4])
        g_all = s.sbuf("g_all", [P, KT, T])
        gsig = s.sbuf("gsig", [P, 2, T])
        gate_r, gate_i, decay, tau = (s.sbuf(n, [P, 2, 2, T]) for n in ("gate_r", "gate_i", "decay", "tau"))
        y = s.sbuf("y", [P, 2, T])
        scale_a, scale_t = s.sbuf("scale_a", [P, 32]), s.sbuf("scale_t", [P, 32])
        tmp = [s.sbuf(f"tmp{n}", [P, 32]) for n in range(3)]
        rate = s.sbuf("rate", [P, 32])

        def col(at, i=0):
            return params[:, bass.ds(at + i, 1)]

        with nc.Block() as block:
            @block.sync
            def _(sp):
                sp.dma_start(params[:], k.p1).then_inc(s.params, 16)

                def body(i, prev):
                    sp.wait_ge(s.gates, i + 1)
                    sp.dma_start(gate_w[:].rearrange("p b g n -> p (b g n)"),
                                 k.lru_w[bass.ds(i, 1)].rearrange("a p n -> p (a n)")).then_inc(s.weights, 16)
                    for n in range(SLOTS):
                        stream.load(sp, i + 1, n)
                run_passes(sp, LRU_PASSES, body)

            @block.scalar
            def _(act):
                stream.open_act(act)
                act.wait_ge(s.chain, 2)
                act.activation(tmp[1][:], tmp[0][:], ACT.Exp).then_inc(s.exped, 1)
                act.wait_ge(s.cleared, 1)

                def gate_inputs(i):
                    act.wait_ge(s.used, stream.done(i, 3))
                    for b in range(2):
                        act.activation(gsig[:, b], k.z[2 + b][:, 0:T], ACT.Sigmoid).then_inc(s.gsig, 1)

                def inputs(i):
                    act.wait_ge(s.used, stream.done(i, 1))
                    act.wait_ge(s.conv, CONV * i + 1)
                    for b in range(2):
                        act.activation(padded[:, b, 2:2 + T], k.z[b][:, 0:T], ACT.Copy).then_inc(s.ucopied, 1)

                def gates(i):
                    act.wait_ge(s.dsteps, DSTEPS * i + 1)
                    act.wait_ge(s.gates, i + 2)
                    for b in range(2):
                        for d in range(2):
                            act.activation(gate_r[:, b, d], k.aux[2 * b + d][:, 0:T], ACT.Sigmoid,
                                           bias=col(P1_BR + 16 * d + b, 2 * i)).then_inc(s.taken, 1)
                            act.activation(gate_i[:, b, d], k.aux[2 * b + d][:, T:2 * T], ACT.Sigmoid,
                                           bias=col(P1_BI + 16 * d + b, 2 * i)).then_inc(s.taken, 1)

                def tanhs(i):
                    act.wait_ge(s.taken, 8 * i + 9)
                    for b in range(2):
                        for d in range(2):
                            act.activation(tau[:, b, d], gate_r[:, b, d], ACT.Tanh,
                                           scale=scale_t[:, bass.ds(16 * d + b + 2 * i, 1)]).then_inc(s.decay, 1)

                def exps(i):
                    for b in range(2):
                        for d in range(2):
                            act.activation(decay[:, b, d], gate_r[:, b, d], ACT.Exp,
                                           scale=scale_a[:, bass.ds(16 * d + b + 2 * i, 1)]).then_inc(s.decay, 1)
                    act.wait_ge(s.decay, 9 * i + 8)
                    act.activation(tau[:], tau[:], ACT.Sqrt).then_inc(s.decay, 1)

                def round_y(i):
                    act.wait_ge(s.dsteps, DSTEPS * i + DSTEPS + 1)
                    act.activation(k.y_hi[:, bass.ds(2 * i, 2)], y[:], ACT.Copy).then_inc(s.rounded_y, 1)

                def body(i, prev):
                    if prev:
                        gate_inputs(i - 1)
                        gates(i - 1)
                    stream.round(act, i + 1, 0)
                    if prev:
                        tanhs(i - 1)
                    stream.round(act, i + 1, 1)
                    inputs(i)
                    if prev:
                        exps(i - 1)
                    stream.round(act, i + 1, 2)
                    stream.round(act, i + 1, 3)
                    if prev:
                        round_y(i - 1)

                def tail(i):
                    gate_inputs(i)
                    gates(i)
                    tanhs(i)
                    exps(i)
                    round_y(i)
                run_passes(act, LRU_PASSES, body, tail)

            @block.gpsimd
            def _(pool):
                def gated(i, prev=True):
                    for b in range(2):
                        pool.wait_ge(s.taken, 8 * i + 9)
                        u = k.feat[:, bass.ds(2 * i + b, 1)].to_broadcast([P, 2, T])
                        pool.tensor_tensor(gate_i[:, b], gate_i[:, b], u, ALU.mult).then_inc(s.gated, 1)
                run_passes(pool, LRU_PASSES, gated)

            @block.vector
            def _(dve):
                stream.open_dve(dve)
                dve.sem_inc(s.conv, 1)
                dve.sem_inc(s.dsteps, 1)
                dve.memset(padded[:], 0.0).then_inc(s.cleared, 1)
                link = chain(dve, s.chain)
                dve.wait_ge(s.params, 16)
                link(lambda: dve.tensor_scalar(rate[:], params[:, P1_LAM:P1_LAM + 32], -1.0, None, ALU.mult))

                link(lambda: dve.tensor_tensor(tmp[0][:], rate[:], params[:, P1_LAM:P1_LAM + 32], ALU.min))
                dve.wait_ge(s.exped, 1)
                softplus_tail(link, dve, rate[:], tmp[1][:], tmp[0][:], tmp[2][:])
                link(lambda: dve.tensor_scalar(scale_a[:], rate[:], -8.0, None, ALU.mult))
                link(lambda: dve.tensor_scalar(scale_t[:], rate[:], 4.0, None, ALU.mult))

                def convolve(i):
                    dve.wait_ge(s.ucopied, 2 * i + 4)
                    for tap in range(4):
                        for b in range(2):
                            if tap:
                                dve.wait_ge(s.conv, CONV * i + 1 + 2 * (tap - 1) + b + 1)
                            u, x = k.feat[:, bass.ds(2 * i + b, 1)], padded[:, b, tap:tap + T]
                            if tap == 0:
                                ins = dve.tensor_scalar(u, x[:, None], col(P1_CONV + b, 2 * i), col(P1_CONVB + b, 2 * i),
                                                        ALU.mult, ALU.add)
                            else:
                                ins = dve.scalar_tensor_tensor(out=u, in0=x[:, None], scalar=col(P1_CONV + 16 * tap + b, 2 * i),
                                                               in1=u, op0=ALU.mult, op1=ALU.add)
                            ins.then_inc(s.conv, 1)

                def open_gates(i):
                    dve.wait_ge(s.gsig, 2 * i + 2)
                    for b in range(2):
                        dve.tensor_tensor(g_all[:, bass.ds(2 * i + b, 1)], k.z[2 + b][:, None, 0:T], gsig[:, b:b + 1],
                                          ALU.mult).then_inc(s.zcopied, 1)

                def scan(i):
                    def step(n):
                        dve.wait_ge(s.dsteps, DSTEPS * i + n + 1)
                    dve.wait_ge(s.decay, 9 * i + 9)
                    dve.scalar_tensor_tensor(out=tau[:], in0=decay[:], scalar=1.0, in1=tau[:], op0=ALU.add,
                                             op1=ALU.mult).then_inc(s.dsteps, 1)
                    step(1)
                    dve.wait_ge(s.gated, 2 * i + 2)
                    dve.tensor_tensor(tau[:], tau[:], gate_i[:], ALU.mult).then_inc(s.dsteps, 1)
                    step(2)
                    for b in range(2):
                        dve.tensor_tensor_scan(gate_r[:, b, 0], decay[:, b, 0], tau[:, b, 0], 0.0, ALU.mult,
                                               ALU.add).then_inc(s.dsteps, 1)
                        dve.tensor_tensor_scan(gate_r[:, b, 1, ::-1], decay[:, b, 1, ::-1], tau[:, b, 1, ::-1], 0.0,
                                               ALU.mult, ALU.add).then_inc(s.dsteps, 1)

                def outputs(i):
                    dve.wait_ge(s.dsteps, DSTEPS * i + 7)
                    dve.tensor_tensor(gate_r[:, :, 0], gate_r[:, :, 0], gate_r[:, :, 1], ALU.add).then_inc(s.dsteps, 1)
                    dve.wait_ge(s.dsteps, DSTEPS * i + 8)
                    dve.tensor_tensor(y[:], gate_r[:, :, 0], g_all[:, bass.ds(2 * i, 2)], ALU.mult).then_inc(s.dsteps, 1)

                def split_y(i):
                    dve.wait_ge(s.rounded_y, i + 1)
                    dve.tensor_tensor(k.y_lo[:, bass.ds(2 * i, 2)], y[:], k.y_hi[:, bass.ds(2 * i, 2)].bitcast(F32),
                                      ALU.subtract).then_inc(s.ydone, 1)
                    dve.wait_ge(s.ydone, i + 1)

                def body(i, prev):
                    if prev:
                        open_gates(i - 1)
                    stream.residual(dve, i + 1, 0)
                    stream.residual(dve, i + 1, 1)
                    convolve(i)
                    if prev:
                        scan(i - 1)
                    stream.residual(dve, i + 1, 2)
                    if prev:
                        outputs(i - 1)
                    stream.residual(dve, i + 1, 3)
                    if prev:
                        split_y(i - 1)

                def tail(i):
                    open_gates(i)
                    scan(i)
                    outputs(i)
                    split_y(i)
                run_passes(dve, LRU_PASSES, body, tail)

            @block.tensor
            def _(pe):
                stream.open_pe(pe)
                pe.sem_inc(s.gates, 1)
                pe.sem_inc(s.ucopied, 2)
                pe.sem_inc(s.zcopied, 2)
                pe.sem_inc(s.taken, 1)

                def products(i):
                    pe.wait_ge(s.ucopied, 2 * i + 2)
                    for sl in (0, 1):
                        stream.multiply(pe, i, sl, k.xn_hi, k.xn_lo)
                    pe.wait_ge(s.zcopied, 2 * i + 2)
                    for sl in (2, 3):
                        stream.multiply(pe, i, sl, k.xn_hi, k.xn_lo)

                def gates(i):
                    pe.wait_ge(s.conv, CONV * i + 1 + CONV)
                    pe.wait_ge(s.weights, 16 * i + 16)
                    pe.wait_ge(s.taken, 8 * i + 1)
                    for b in range(2):
                        for d in range(2):
                            for g in range(2):
                                ins = pe.matmul(k.aux[2 * b + d][:, g * T:g * T + T], gate_w[:, b, 2 * d + g],
                                                k.feat[:, bass.ds(2 * i + b, 1)], start=True, stop=True)
                    ins.then_inc(s.gates, 1)

                def body(i, prev):
                    products(i)
                    gates(i)
                run_passes(pe, LRU_PASSES, body)


def merge_phase(k, name, first_slot, y_first):
    nc = k.nc
    with phase(nc, name, STREAM + "gsig taken steps") as s:
        stream = Stream(k, s, first_slot)
        gate, part = s.sbuf("gate", [P, 2, T]), s.sbuf("part", [P, 2, T])
        with nc.Block() as block:
            @block.sync
            def _(sp):
                stream.loads(sp, KT // 2)

            @block.scalar
            def _(act):
                stream.open_act(act)

                def body(i, prev):
                    stream.round(act, i + 1, 0)
                    stream.round(act, i + 1, 1)
                    act.wait_ge(s.used, stream.done(i, 1))
                    act.wait_ge(s.taken, 2 * i + 2)
                    for b in range(2):
                        act.activation(gate[:, b], k.z[b][:, 0:T], ACT.Sigmoid).then_inc(s.gsig, 1)
                    stream.round(act, i + 1, 2)
                    stream.round(act, i + 1, 3)
                run_passes(act, KT // 2, body)

            @block.vector
            def _(dve):
                stream.open_dve(dve)
                dve.sem_inc(s.taken, 2)

                def merge(i):
                    dve.wait_ge(s.gsig, 2 * i + 4)
                    dve.wait_ge(s.used, stream.done(i, 3))
                    out = k.feat[:, bass.ds(2 * i, 2)] if y_first else part[:]
                    for b in range(2):
                        o = k.feat[:, bass.ds(2 * i + b, 1)] if y_first else part[:, b:b + 1]
                        dve.tensor_tensor(o, k.z[2 + b][:, None, 0:T], gate[:, b:b + 1], ALU.mult).then_inc(s.taken, 1)
                    if not y_first:
                        dve.wait_ge(s.taken, 2 * i + 4)
                        f = k.feat[:, bass.ds(2 * i, 2)]
                        dve.tensor_tensor(f, f, part[:], ALU.add).then_inc(s.steps, 1)
                        dve.wait_ge(s.steps, i + 1)

                def body(i, prev):
                    if prev:
                        merge(i - 1)
                    for n in range(SLOTS):
                        stream.residual(dve, i + 1, n)
                run_passes(dve, KT // 2, body, merge)

            @block.tensor
            def _(pe):
                stream.open_pe(pe)
                pe.sem_inc(s.gsig, 2)

                def products(i):
                    pe.wait_ge(s.gsig, 2 * i + 2)
                    for sl in (0, 1):
                        stream.multiply(pe, i, sl, k.xn_hi, k.xn_lo)
                    pe.wait_ge(s.taken, 2 * i + 2)
                    for sl in (2, 3):
                        stream.multiply(pe, i, sl, k.y_hi, k.y_lo)
                run_passes(pe, KT // 2, lambda i, prev: products(i))


def rope_tables(k, name, positions, freq):
    nc = k.nc
    turn_parts = (6.28125, 0.0019350051879882812, 3.019916e-07)
    turn_parts = turn_parts[:2] + (2 * math.pi - sum(turn_parts[:2]),)
    magic = 1.5 * 2.0 ** 23
    with phase(nc, name, "loaded counted chain looked") as s:
        pos_i = s.sbuf("pos_i", [P, T], I32)
        angle, turns, rest = (s.sbuf(n, [P, T]) for n in ("angle", "turns", "rest"))
        f = s.sbuf("f", [P, 2])
        with nc.Block() as block:
            @block.sync
            def _(sp):
                sp.dma_start(f[:], constant(k, freq)).then_inc(s.loaded, 16)
                if positions is not None:
                    sp.dma_start(pos_i[:], positions.to_broadcast([P, T])).then_inc(s.loaded, 16)

            @block.gpsimd
            def _(pool):
                if positions is None:
                    pool.iota(pos_i[:], [[1, T]], base=0, channel_multiplier=0).then_inc(s.counted, 1)

            @block.vector
            def _(dve):
                link = chain(dve, s.chain)
                if positions is None:
                    dve.wait_ge(s.counted, 1)
                    dve.wait_ge(s.loaded, 16)
                else:
                    dve.wait_ge(s.loaded, 32)
                link(lambda: dve.tensor_copy(angle[:], pos_i[:]))
                link(lambda: dve.tensor_scalar(angle[:], angle[:], f[:, 0:1], None, ALU.mult))
                for n, (table, quarter) in enumerate(((k.sin_t, 0.0), (k.cos_t, 0.25))):
                    if n:
                        dve.wait_ge(s.looked, 1)
                    link(lambda: dve.tensor_scalar(turns[:], angle[:], 0.5 / math.pi, quarter, ALU.mult, ALU.add))
                    link(lambda: dve.tensor_scalar(turns[:], turns[:], magic, None, ALU.add))
                    link(lambda: dve.tensor_scalar(turns[:], turns[:], -magic, None, ALU.add))
                    for m, part in enumerate(turn_parts):
                        link(lambda: dve.scalar_tensor_tensor(out=rest[:], in0=turns[:], scalar=-part,
                                                              in1=rest[:] if m else angle[:], op0=ALU.mult, op1=ALU.add))
                    link(lambda: dve.tensor_scalar(rest[:], rest[:], quarter * 2 * math.pi, 3.1415925, ALU.add, ALU.min))
                    link(lambda: dve.tensor_scalar(rest[:], rest[:], -3.1415925, None, ALU.max))

            @block.scalar
            def _(act):
                for n, table in enumerate((k.sin_t, k.cos_t)):
                    act.wait_ge(s.chain, 2 + 8 * (n + 1))
                    act.activation(table[:], rest[:], ACT.Sin).then_inc(s.looked, 1)


def attention_phase(k, name, a):
    nc = k.nc
    heads = a.heads_per_tile
    pairs = heads
    M = 12
    R = 5 if heads == 2 else 3
    C = 4 if heads == 2 else 2
    KV_PASSES = 2 // heads
    G0 = 2 if heads == 1 else 1
    K_STEPS = 6 if heads == 1 else R + 8
    MIXED = 1 if heads == 1 else 0
    with phase(nc, name, STREAM + "consts ready kcopied kturned ksteps kdone kdup vcopied vcur qcopied turned rope "
               "qstd gsig gmul scores soft exped flipped fcopied mixed ysteps yrounded") as s:
        stream = Stream(k, s, a.first_slot)
        turn = s.sbuf("turn", [P, P])
        mask = s.sbuf("mask", [P, 2, T])
        sinks, sink_row = s.sbuf("sinks", [P, a.n_heads, 2]), s.sbuf("sink_row", [P, a.n_heads])
        norms = s.sbuf("norms", [P, 2])
        kt_n = 4 // heads
        keys = s.sbuf("keys", [P, 4, T])
        values = s.sbuf("values", [P, 2, a.kv_width])
        values_now = s.sbuf("values_now", [P, 2, P]) if heads == 1 else None
        q_raw, q_sq, q_rot, part = (s.sbuf(n, [P, 2, T]) for n in ("q_raw", "q_sq", "q_rot", "part"))
        k_raw = s.sbuf("k_raw", [P, 4, T]) if heads == 1 else q_raw
        std, rstd = (s.sbuf(n, [P, 2, T]) for n in ("std", "rstd")) if heads == 2 else (None, None)
        gsig, gate = s.sbuf("gsig", [P, 2, T]), s.sbuf("gate", [P, 2, T])
        S = [s.sbuf(f"S{p}", [P, 2, 2, T]) for p in range(pairs)]
        W = [s.sbuf(f"W{p}", [P, 2, 2, T]) for p in range(pairs)]
        small = [s.sbuf(f"small{p}", [P, 6, 4]) for p in range(pairs)]
        y = s.sbuf("y", [P, 2, T])
        cos_b = k.cos_t[:, None, :].to_broadcast([P, 2, T])
        sin_b = k.sin_t[:, None, :].to_broadcast([P, 2, T])

        def both(bank):
            return bank[:, 0:2 * T].rearrange("p (b t) -> p b t", b=2)

        def kv_of(i, p, h):
            return i // 2 if heads == 1 else (4 * i + 2 * p + h) // 3

        with nc.Block() as block:
            @block.sync
            def _(sp):
                sp.dma_start(turn[:], constant(k, a.turn)).then_inc(s.consts, 16)
                sp.dma_start(mask[:].rearrange("p b t -> p (b t)"), constant(k, a.mask)).then_inc(s.consts, 16)
                sp.dma_start(sink_row[:], a.sinks.to_broadcast([P, a.n_heads])).then_inc(s.consts, 16)
                if a.norms is not None:
                    sp.dma_start(norms[:], a.norms).then_inc(s.consts, 16)
                stream.loads(sp, G0 + a.passes)

            consts_in = 48 if a.norms is None else 64

            @block.gpsimd
            def _(pool):
                if heads == 1:
                    pool.wait_ge(s.vcopied, 4)

                    def values_here(i, prev):
                        pool.wait_ge(s.mixed, i + 1)
                        pool.tensor_copy(values_now[:], values[:, :, bass.ds((i // 2) * P, P)]).then_inc(s.vcur, 1)
                    run_passes(pool, a.passes, values_here)

            @block.scalar
            def _(act):
                stream.open_act(act)
                stream.round(act, 1, 0)
                stream.round(act, 1, 1)
                if heads == 1:
                    for t in range(4):
                        if t == 2:
                            stream.round(act, 1, 2)
                            stream.round(act, 1, 3)
                        act.wait_ge(s.used, stream.done(0, 2 * (t // 2) + 1))
                        act.activation(k_raw[:, t], k.z[t][:, 0:T], ACT.Copy).then_inc(s.kcopied, 1)
                    for n in range(4):
                        if n % 2 == 0:
                            stream.round(act, 2, n)
                            stream.round(act, 2, n + 1)
                        act.wait_ge(s.used, stream.done(1, 2 * (n // 2) + 1))
                        act.activation(values[:, n % 2, T * (n // 2):T * (n // 2) + T], k.z[n][:, 0:T], ACT.Copy)\
                           .then_inc(s.vcopied, 1)
                else:
                    act.wait_ge(s.consts, consts_in)
                    act.wait_ge(s.used, stream.done(0, 1))
                    for t in range(2):
                        act.activation(k_raw[:, t], k.z[t][:, 0:T], ACT.Copy, scale=norms[:, 1:2]).then_inc(s.kcopied, 1)
                        act.activation(q_sq[:, t], k.z[t][:, 0:T], ACT.Square).then_inc(s.kcopied, 1)
                    stream.round(act, 1, 2)
                    stream.round(act, 1, 3)
                    act.wait_ge(s.used, stream.done(0, 3))
                    for n in range(2):
                        act.activation(values[:, n, 0:T], k.z[2 + n][:, 0:T], ACT.Copy).then_inc(s.vcopied, 1)
                    act.wait_ge(s.kturned, 2)
                    act.activation(std[:], both(k.aux[1]), ACT.Sqrt, bias=k.eps[:], scale=1.0 / HEAD_DIM_2).then_inc(s.qstd, 1)

                def exps(i, p):
                    u = pairs * i + p
                    act.wait_ge(s.soft, M * u + 5)
                    for h in range(2):
                        for b in range(2):
                            c = 2 * h + b
                            act.activation(S[p][:, h, b], S[p][:, h, b], ACT.Exp, bias=small[p][:, 1, c:c + 1],
                                           accum_out=small[p][:, 3, c:c + 1]).then_inc(s.exped, 1)
                    act.wait_ge(s.soft, M * u + 6)
                    act.activation(small[p][:, 4], small[p][:, 2], ACT.Exp).then_inc(s.exped, 1)

                def copy_weights(i, p):
                    u = pairs * i + p
                    act.wait_ge(s.flipped, u + 1)
                    for h in range(2):
                        act.activation(W[p][:, h], both(k.aux[2 * p + h]), ACT.Copy).then_inc(s.fcopied, 1)

                def round_y(i, p):
                    u = pairs * i + p
                    act.wait_ge(s.ysteps, 2 * u + 1)
                    if heads == 1:
                        act.activation(k.y_hi[:, bass.ds(2 * i, 2)], y[:], ACT.Copy).then_inc(s.yrounded, 1)
                    else:
                        act.activation(k.y_hi[:, 2 * i + p], y[:, 0], ACT.Copy).then_inc(s.yrounded, 1)

                def body(i, prev):
                    g = i + G0
                    if prev:
                        act.wait_ge(s.used, stream.done(g - 1, 3))
                        for b in range(2):
                            act.activation(gsig[:, b], k.z[2 + b][:, 0:T], ACT.Sigmoid).then_inc(s.gsig, 1)
                        exps(i - 1, 0)
                    stream.round(act, g + 1, 0)
                    if prev and pairs == 2:
                        exps(i - 1, 1)
                    stream.round(act, g + 1, 1)
                    act.wait_ge(s.used, stream.done(g, 1))
                    if prev:
                        act.wait_ge(s.rope, R * i)
                    elif heads == 2:
                        act.wait_ge(s.ksteps, K_STEPS)
                    for t in range(2):
                        if heads == 2:
                            act.activation(q_raw[:, t], k.z[t][:, 0:T], ACT.Copy, scale=norms[:, 0:1]).then_inc(s.qcopied, 1)
                            act.activation(q_sq[:, t], k.z[t][:, 0:T], ACT.Square).then_inc(s.qcopied, 1)
                        else:
                            act.activation(q_raw[:, t], k.z[t][:, 0:T], ACT.Copy).then_inc(s.qcopied, 1)
                    if prev:
                        copy_weights(i - 1, 0)
                    stream.round(act, g + 1, 2)
                    if heads == 2:
                        act.wait_ge(s.turned, i + 1)
                        act.activation(std[:], both(k.z[1]), ACT.Sqrt, bias=k.eps[:], scale=1.0 / HEAD_DIM_2).then_inc(s.qstd, 1)
                    if prev:
                        round_y(i - 1, 0)
                    if prev and pairs == 2:
                        copy_weights(i - 1, 1)
                    stream.round(act, g + 1, 3)
                    if prev and pairs == 2:
                        round_y(i - 1, 1)

                def tail(i):
                    act.wait_ge(s.used, stream.done(i + G0, 3))
                    for b in range(2):
                        act.activation(gsig[:, b], k.z[2 + b][:, 0:T], ACT.Sigmoid).then_inc(s.gsig, 1)
                    for p in range(pairs):
                        exps(i, p)
                    for p in range(pairs):
                        copy_weights(i, p)
                        round_y(i, p)
                run_passes(act, a.passes, body, tail)

            @block.vector
            def _(dve):
                stream.open_dve(dve)
                for n in range(SLOTS):
                    stream.residual(dve, 1, n)
                dve.wait_ge(s.consts, consts_in)
                for b in range(2):
                    dve.tensor_copy(sinks[:, :, b], sink_row[:]).then_inc(s.ready, 1)

                def rotate(i, p, wait, sem, base, raw, out):
                    wait(0)
                    after(dve, sem, base)
                    dve.tensor_tensor(part[:], raw, cos_b, ALU.mult).then_inc(sem, 1)
                    dve.tensor_tensor(out, both(p), sin_b, ALU.mult).then_inc(sem, 1)
                    dve.wait_ge(sem, base + 2)
                    dve.tensor_tensor(out, out, part[:], ALU.add).then_inc(sem, 1)
                    if heads == 2:
                        wait(1)
                        dve.reciprocal(rstd[:], std[:]).then_inc(sem, 1)
                        dve.wait_ge(sem, base + 4)
                        dve.tensor_tensor(out, out, rstd[:], ALU.mult).then_inc(sem, 1)

                if heads == 1:
                    for h in range(2):
                        rotate(0, k.aux[h], lambda n: dve.wait_ge(s.kturned, h + 1), s.ksteps, R * h,
                               k_raw[:, 2 * h:2 * h + 2], keys[:, 2 * h:2 * h + 2])
                else:
                    rotate(0, k.aux[0], lambda n: dve.wait_ge(s.qstd if n else s.kturned, 1), s.ksteps, 0, k_raw[:], q_rot[:])
                    dve.wait_ge(s.ksteps, R)
                    for kv in range(4):
                        half = (kv % 2) * 64
                        for to in (0, 64):
                            dve.tensor_copy(keys[to:to + 64, kv], q_rot[half:half + 64, kv // 2]).then_inc(s.ksteps, 1)
                if heads == 1:
                    for n in range(SLOTS):
                        stream.residual(dve, 2, n)

                def soften(i, p):
                    u = pairs * i + p
                    dve.wait_ge(s.scores, u + 1)
                    for h in range(2):
                        dve.scalar_tensor_tensor(out=S[p][:, h], in0=both(k.aux[2 * p + h]), scalar=a.scale, in1=mask[:],
                                                 op0=ALU.mult, op1=ALU.add).then_inc(s.soft, 1)
                    dve.wait_ge(s.soft, M * u + 2)
                    m = small[p]
                    dve.tensor_reduce(m[:, 0], S[p][:].rearrange("p h b t -> p (h b) t"), AX_X, ALU.max).then_inc(s.soft, 1)
                    dve.wait_ge(s.soft, M * u + 3)
                    sink = sinks[:, bass.ds(2 * u, 2)].rearrange("p h b -> p (h b)")
                    dve.tensor_tensor(m[:, 0], m[:, 0], sink, ALU.max).then_inc(s.soft, 1)
                    dve.wait_ge(s.soft, M * u + 4)
                    dve.tensor_scalar(m[:, 1], m[:, 0], -1.0, None, ALU.mult).then_inc(s.soft, 1)
                    dve.wait_ge(s.soft, M * u + 5)
                    dve.tensor_tensor(m[:, 2], m[:, 1], sink, ALU.add).then_inc(s.soft, 1)

                def normalise(i, p):
                    u = pairs * i + p
                    m = small[p]
                    dve.wait_ge(s.exped, 5 * u + 5)
                    dve.tensor_tensor(m[:, 5], m[:, 3], m[:, 4], ALU.add).then_inc(s.soft, 1)
                    dve.wait_ge(s.soft, M * u + 7)
                    dve.reciprocal(m[:, 0], m[:, 5]).then_inc(s.soft, 1)
                    dve.wait_ge(s.soft, M * u + 8)
                    for h in range(2):
                        for b in range(2):
                            c = 2 * h + b
                            dve.tensor_scalar(S[p][:, h, b], S[p][:, h, b], m[:, 0, c:c + 1], None, ALU.mult)\
                               .then_inc(s.soft, 1)

                def open_gates(i):
                    dve.wait_ge(s.gsig, 2 * i + 2)
                    for b in range(2):
                        dve.tensor_tensor(gate[:, b], k.z[2 + b][:, 0:T], gsig[:, b], ALU.mult).then_inc(s.gmul, 1)

                def finish(i, p):
                    u = pairs * i + p
                    dve.wait_ge(s.mixed, u + 1 + MIXED)
                    dve.wait_ge(s.gmul, 2 * i + 2)
                    if heads == 1:
                        dve.tensor_tensor(y[:], both(k.aux[0]), gate[:], ALU.mult).then_inc(s.ysteps, 1)
                        hi, lo, v = k.y_hi[:, bass.ds(2 * i, 2)], k.y_lo[:, bass.ds(2 * i, 2)], y[:]
                    else:
                        dve.tensor_tensor(y[:, 0], k.aux[2 * p][:, 0:T], gate[:, p], ALU.mult).then_inc(s.ysteps, 1)
                        hi, lo, v = k.y_hi[:, 2 * i + p], k.y_lo[:, 2 * i + p], y[:, 0]
                    dve.wait_ge(s.yrounded, u + 1)
                    dve.tensor_tensor(lo, v, hi.bitcast(F32), ALU.subtract).then_inc(s.ysteps, 1)
                    dve.wait_ge(s.ysteps, 2 * u + 2)

                def body(i, prev):
                    g = i + G0
                    if prev:
                        open_gates(i - 1)
                        soften(i - 1, 0)
                    stream.residual(dve, g + 1, 0)
                    if prev:
                        normalise(i - 1, 0)
                        if pairs == 2:
                            soften(i - 1, 1)
                    stream.residual(dve, g + 1, 1)
                    if prev and pairs == 2:
                        normalise(i - 1, 1)
                    stream.residual(dve, g + 1, 2)
                    if not prev:
                        dve.wait_ge(s.ksteps, K_STEPS)
                    rotate(i, k.z[0], lambda n: dve.wait_ge(s.qstd, i + 2) if n else dve.wait_ge(s.turned, i + 1), s.rope, R * i,
                           q_raw[:], q_rot[:])
                    if prev:
                        finish(i - 1, 0)
                    stream.residual(dve, g + 1, 3)
                    if prev and pairs == 2:
                        finish(i - 1, 1)

                def tail(i):
                    open_gates(i)
                    for p in range(pairs):
                        soften(i, p)
                        normalise(i, p)
                    for p in range(pairs):
                        finish(i, p)
                run_passes(dve, a.passes, body, tail)

            @block.tensor
            def _(pe):
                stream.open_pe(pe)
                if heads == 1:
                    pe.sem_inc(s.mixed, 1)
                for sl in range(4):
                    stream.multiply(pe, 0, sl, k.xn_hi, k.xn_lo, tokens_out=heads == 2 and sl >= 2)
                pe.wait_ge(s.consts, consts_in)
                if heads == 1:
                    for h in range(2):
                        pe.wait_ge(s.kcopied, 2 * h + 2)
                        pe.matmul(k.aux[h][:, 0:2 * T], turn[:], k_raw[:, 2 * h:2 * h + 2], start=True, stop=True)\
                          .then_inc(s.kturned, 1)
                    pe.wait_ge(s.kcopied, 4)
                    for sl in range(4):
                        stream.multiply(pe, 1, sl, k.xn_hi, k.xn_lo, tokens_out=True)
                else:
                    pe.wait_ge(s.kcopied, 4)
                    pe.matmul(k.aux[0][:, 0:2 * T], turn[:], k_raw[:], start=True, stop=True).then_inc(s.kturned, 1)
                    pe.matmul(k.aux[1][:, 0:2 * T], k.blocks[:], q_sq[:], start=True, stop=True).then_inc(s.kturned, 1)

                def scores(i, p):
                    for h in range(2):
                        kv = kv_of(i, p, h)
                        for b in range(2):
                            out = k.aux[2 * p + h][:, b * T:b * T + T]
                            if heads == 1:
                                q, key = q_rot[:, h, P * b:P * b + P], keys[:, bass.ds(kv, 1)]
                            else:
                                lo = 64 * h
                                q, key = q_rot[lo:lo + 64, p, P * b:P * b + P], keys[lo:lo + 64, kv]
                            ins = pe.matmul(out, q, key, start=True, stop=True)
                    ins.then_inc(s.scores, 1)

                def flip(i, p):
                    u = pairs * i + p
                    pe.wait_ge(s.soft, M * u + 12)
                    for h in range(2):
                        for b in range(2):
                            for kb in range(2):
                                ins = pe.transpose(k.aux[2 * p + h][:, kb * T + b * P:kb * T + b * P + P],
                                                   S[p][:, h, b, kb * P:kb * P + P], k.ident[:])
                    ins.then_inc(s.flipped, 1)

                def mix(i, p):
                    u = pairs * i + p
                    pe.wait_ge(s.fcopied, 2 * u + 2)
                    if heads == 1:
                        pe.wait_ge(s.vcur, i + 1)
                    for h in range(2):
                        for kb in range(2):
                            if heads == 1:
                                out, v = k.aux[0][:, h * T:h * T + T], values_now[:, kb]
                            else:
                                at = 64 * kv_of(i, p, h)
                                out, v = k.aux[2 * p][64 * h:64 * h + 64, 0:T], values[:, kb, at:at + 64]
                            ins = pe.matmul(out, v, W[p][:, h, kb], start=kb == 0, stop=kb == 1)
                    ins.then_inc(s.mixed, 1)

                def body(i, prev):
                    g = i + G0
                    if prev:
                        pe.wait_ge(s.rope, R * i)
                    elif heads == 1:
                        pe.wait_ge(s.vcopied, 2)
                    stream.multiply(pe, g, 0, k.xn_hi, k.xn_lo)
                    if prev and pairs == 2:
                        if i >= 2:
                            pe.wait_ge(s.ysteps, 2 * pairs * (i - 1))
                        scores(i - 1, 1)
                    stream.multiply(pe, g, 1, k.xn_hi, k.xn_lo)
                    if prev:
                        flip(i - 1, 0)
                        pe.wait_ge(s.gmul, 2 * i)
                    else:
                        pe.wait_ge(s.vcopied, 4 // heads)
                    stream.multiply(pe, g, 2, k.xn_hi, k.xn_lo)
                    if prev:
                        mix(i - 1, 0)
                        if pairs == 2:
                            flip(i - 1, 1)
                    pe.wait_ge(s.qcopied, C * i + C)
                    ins = pe.matmul(k.z[0][:, 0:2 * T], turn[:], q_raw[:], start=True, stop=True)
                    if heads == 2:
                        ins = pe.matmul(k.z[1][:, 0:2 * T], k.blocks[:], q_sq[:], start=True, stop=True)
                    ins.then_inc(s.turned, 1)
                    stream.multiply(pe, g, 3, k.xn_hi, k.xn_lo)
                    if prev and pairs == 2:
                        mix(i - 1, 1)
                    if prev:
                        pe.wait_ge(s.ysteps, 2 * pairs * (i - 1) + 1)
                    else:
                        pe.wait_ge(s.ksteps, K_STEPS)
                    pe.wait_ge(s.rope, R * i + R)
                    scores(i, 0)

                def tail(i):
                    if pairs == 2:
                        pe.wait_ge(s.ysteps, 2 * pairs * i)
                        scores(i, 1)
                    for p in range(pairs):
                        flip(i, p)
                    for p in range(pairs):
                        mix(i, p)
                run_passes(pe, a.passes, body, tail)


def conv_phase(k, layer):
    nc = k.nc
    B = B_TILES
    name = "conv"
    with phase(nc, name, STREAM + "params pw cleared acopied gsig gated zsig zgated taps summed centred squared squares "
               "std ln lsig hid mixed ysteps yrounded") as s:
        stream = Stream(k, s, layer * SLOTS_2 + SLOTS_1 + SLOT_CONV_2)
        params = s.sbuf("params", [P, P2_COLS])
        pw = s.sbuf("pw", [P, B, B * P])
        padded = s.sbuf("padded", [P, B, TAPS_B - 1 + T])
        a_now, gsig = s.sbuf("a_now", [P, 2, T]), s.sbuf("gsig", [P, 2, T])
        zgate = s.sbuf("zgate", [P, B, T])
        acc, sq, sig = (s.sbuf(n, [P, B, T]) for n in ("acc", "sq", "sig"))
        std, rstd = s.sbuf("std", [P, T]), s.sbuf("rstd", [P, T])
        y = zgate

        def col(at):
            return params[:, at:at + 1]

        with nc.Block() as block:
            @block.sync
            def _(sp):
                sp.dma_start(params[:], k.p2[bass.ds(layer, 1)].rearrange("a p n -> p (a n)")).then_inc(s.params, 16)
                sp.dma_start(pw[:].rearrange("p a n -> p (a n)"), k.pw[bass.ds(layer, 1)].rearrange("a p n -> p (a n)"))\
                  .then_inc(s.pw, 16)
                stream.loads(sp, 3)

            @block.scalar
            def _(act):
                stream.open_act(act)
                for i in range(3):
                    stream.round(act, i + 1, 0)
                    stream.round(act, i + 1, 1)
                    act.wait_ge(s.used, stream.done(i, 1))
                    for b in range(2):
                        if i < 2:
                            if i:
                                act.wait_ge(s.gated, 2)
                            act.activation(a_now[:, b], k.z[b][:, 0:T], ACT.Copy).then_inc(s.acopied, 1)
                        else:
                            act.activation(zgate[:, b], k.z[b][:, 0:T], ACT.Sigmoid).then_inc(s.zsig, 1)
                    stream.round(act, i + 1, 2)
                    stream.round(act, i + 1, 3)
                    act.wait_ge(s.used, stream.done(i, 3))
                    for b in range(2):
                        if i < 2:
                            act.activation(gsig[:, b], k.z[2 + b][:, 0:T], ACT.Sigmoid).then_inc(s.gsig, 1)
                        else:
                            act.activation(zgate[:, 2 + b], k.z[2 + b][:, 0:T], ACT.Sigmoid).then_inc(s.zsig, 1)
                for t in range(B):
                    act.wait_ge(s.centred, t + 1)
                    act.activation(sq[:, t], acc[:, t], ACT.Square).then_inc(s.squared, 1)
                act.wait_ge(s.squares, 1)
                act.activation(std[:], k.aux[1][:, 0:T], ACT.Sqrt, bias=k.eps[:], scale=1.0 / (B * P)).then_inc(s.std, 1)
                for t in range(B):
                    act.wait_ge(s.ln, t + 2)
                    act.activation(sig[:, t], acc[:, t], ACT.Sigmoid, bias=col(P2_LNB + t)).then_inc(s.lsig, 1)
                for t in range(B):
                    act.wait_ge(s.ysteps, t + 1)
                    act.activation(k.y_hi[:, 6 + t], y[:, t], ACT.Copy).then_inc(s.yrounded, 1)

            def gate(dve, i):
                dve.wait_ge(s.acopied, 2 * i + 2)
                dve.wait_ge(s.gsig, 2 * i + 2)
                for b in range(2):
                    dve.tensor_tensor(padded[:, 2 * i + b, TAPS_B - 1:TAPS_B - 1 + T], a_now[:, b], gsig[:, b], ALU.mult)\
                       .then_inc(s.gated, 1)

            @block.vector
            def _(dve):
                stream.open_dve(dve)
                dve.memset(padded[:], 0.0).then_inc(s.cleared, 1)
                dve.wait_ge(s.cleared, 1)
                for i in range(3):
                    if i >= 1:
                        gate(dve, i - 1)
                    for n in range(SLOTS):
                        stream.residual(dve, i + 1, n)
                dve.wait_ge(s.zsig, 4)
                for b in range(4):
                    dve.tensor_tensor(zgate[:, b], k.z[b][:, 0:T], zgate[:, b], ALU.mult).then_inc(s.zgated, 1)
                dve.wait_ge(s.params, 16)
                dve.wait_ge(s.gated, 4)
                for t in range(B):
                    dve.tensor_scalar(acc[:, t], padded[:, t, 0:T], col(P2_BCONV + t), col(P2_BCONVB + t), ALU.mult, ALU.add)\
                       .then_inc(s.taps, 1)
                with dve.Fori(1, TAPS_B) as tap:
                    for t in range(B):
                        dve.wait_ge(s.taps, B * tap + t - B + 1)
                        dve.scalar_tensor_tensor(out=acc[:, t:t + 1], in0=padded[:, t:t + 1, bass.ds(tap, T)],
                                                 scalar=params[:, bass.ds(B * tap + P2_BCONV + t, 1)],
                                                 in1=acc[:, t:t + 1], op0=ALU.mult, op1=ALU.add).then_inc(s.taps, 1)
                dve.wait_ge(s.summed, 1)
                for t in range(B):
                    dve.scalar_tensor_tensor(out=acc[:, t], in0=k.aux[0][:, 0:T], scalar=-1.0 / (B * P), in1=acc[:, t],
                                             op0=ALU.mult, op1=ALU.add).then_inc(s.centred, 1)
                dve.wait_ge(s.std, 1)
                dve.reciprocal(rstd[:], std[:]).then_inc(s.ln, 1)
                dve.wait_ge(s.ln, 1)
                for t in range(B):
                    dve.scalar_tensor_tensor(out=acc[:, t], in0=acc[:, t], scalar=col(P2_LNW + t), in1=rstd[:],
                                             op0=ALU.mult, op1=ALU.mult).then_inc(s.ln, 1)
                for t in range(B):
                    dve.wait_ge(s.lsig, t + 1)
                    dve.scalar_tensor_tensor(out=sig[:, t], in0=acc[:, t], scalar=col(P2_LNB + t), in1=sig[:, t],
                                             op0=ALU.add, op1=ALU.mult).then_inc(s.hid, 1)
                for t in range(B):
                    dve.wait_ge(s.mixed, t + 1)
                    dve.scalar_tensor_tensor(out=y[:, t], in0=k.z[t][:, 0:T], scalar=col(P2_PWB + t), in1=zgate[:, t],
                                             op0=ALU.add, op1=ALU.mult).then_inc(s.ysteps, 1)
                for t in range(B):
                    dve.wait_ge(s.yrounded, t + 1)
                    dve.tensor_tensor(k.y_lo[:, 6 + t], y[:, t], k.y_hi[:, 6 + t].bitcast(F32), ALU.subtract)\
                       .then_inc(s.hid, 1)

            @block.tensor
            def _(pe):
                stream.open_pe(pe)
                for i in range(3):
                    for sl in range(4):
                        if i and sl == 0:
                            pe.wait_ge(s.acopied, 2 * i)
                        if i and sl == 2:
                            pe.wait_ge(s.gsig, 2 * i)
                        stream.multiply(pe, i, sl, k.xn_hi, k.xn_lo)
                pe.wait_ge(s.taps, B * TAPS_B)
                for t in range(B):
                    ins = pe.matmul(k.aux[0][:, 0:T], k.ones[:], acc[:, t], start=t == 0, stop=t == B - 1)
                ins.then_inc(s.summed, 1)
                for t in range(B):
                    pe.wait_ge(s.squared, t + 1)
                    ins = pe.matmul(k.aux[1][:, 0:T], k.ones[:], sq[:, t], start=t == 0, stop=t == B - 1)
                ins.then_inc(s.squares, 1)
                pe.wait_ge(s.pw, 16)
                pe.wait_ge(s.zgated, 4)
                pe.wait_ge(s.hid, B)
                for m in range(B):
                    for t in range(B):
                        ins = pe.matmul(k.z[m][:, 0:T], pw[:, t, P * m:P * m + P], sig[:, t], start=t == 0, stop=t == B - 1)
                    ins.then_inc(s.mixed, 1)


def delta_inputs_phase(k, layer, keep):
    nc = k.nc
    H = C_HEADS
    PAD = TAPS_C - 1
    with phase(nc, "din", STREAM + "params w12 rows cleared copied conv sig qkv zg squared summed std norm split12 rounded12 "
               "bg chain exped negexp") as s:
        stream = Stream(k, s, layer * SLOTS_2 + SLOTS_1 + SLOT_DELTA_2)
        params = s.sbuf("params", [P, P2_COLS])
        w12, w12_lo = s.sbuf("w12", [P, KT, 2 * H]), s.sbuf("w12_lo", [P, KT, 2 * H], F32R)
        w12_hi = s.sbuf("w12_hi", [P, KT, 2 * H], F32R)
        rows = s.sbuf("rows", [P, 2, H])
        padded = s.sbuf("padded", [P, 3, PAD + T])
        conv, sig = s.sbuf("conv", [P, 3, T]), s.sbuf("sig", [P, 3, T])
        zsig = s.sbuf("zsig", [P, T])
        qk, sq = s.sbuf("qk", [P, 2, T]), s.sbuf("sq", [P, 2, T])
        std, rstd = s.sbuf("std", [P, 2, T]), s.sbuf("rstd", [P, 2, T])
        x, t0, t1, t2 = (s.sbuf(n, [P, 2, H]) for n in ("x", "t0", "t1", "t2"))

        with nc.Block() as block:
            @block.sync
            def _(sp):
                sp.dma_start(params[:], k.p2[bass.ds(layer, 1)].rearrange("a p n -> p (a n)")).then_inc(s.params, 16)
                sp.dma_start(w12[:].rearrange("p k n -> p (k n)"), k.w12[bass.ds(layer, 1)].rearrange("a p n -> p (a n)"))\
                  .then_inc(s.w12, 16)
                sp.dma_start(rows[:].rearrange("p a n -> p (a n)"), k.rows_c[bass.ds(layer, 1)].to_broadcast([P, 2 * H]))\
                  .then_inc(s.rows, 16)
                stream.loads(sp, H)

            @block.scalar
            def _(act):
                stream.open_act(act)
                act.wait_ge(s.w12, 16)
                act.activation(w12_hi[:], w12[:], ACT.Copy).then_inc(s.rounded12, 1)
                act.wait_ge(s.rows, 16)
                act.activation(rows[:, 0], rows[:, 0], ACT.Exp).then_inc(s.negexp, 1)
                act.wait_ge(s.bg, 1)
                for b in range(2):
                    act.activation(keep.beta[:, b], k.aux[1][:, 16 * b:16 * b + H], ACT.Sigmoid).then_inc(s.exped, 1)
                act.wait_ge(s.chain, 4)
                act.activation(t1[:], t0[:], ACT.Exp).then_inc(s.exped, 1)
                act.wait_ge(s.cleared, 1)

                def inputs(i):
                    act.wait_ge(s.used, stream.done(i, 1))
                    act.wait_ge(s.conv, 12 * i + 1)
                    for t in range(2):
                        act.activation(padded[:, t, PAD:PAD + T], k.z[t][:, 0:T], ACT.Copy).then_inc(s.copied, 1)

                def inputs_2(i):
                    act.wait_ge(s.used, stream.done(i, 3))
                    act.activation(padded[:, 2, PAD:PAD + T], k.z[2][:, 0:T], ACT.Copy).then_inc(s.copied, 1)
                    act.wait_ge(s.zg, i + 1)
                    act.activation(zsig[:], k.z[3][:, 0:T], ACT.Sigmoid).then_inc(s.copied, 1)

                def silu(i):
                    act.wait_ge(s.conv, 12 * i + 13)
                    act.activation(sig[:], conv[:], ACT.Sigmoid).then_inc(s.sig, 1)

                def square(i):
                    act.wait_ge(s.qkv, 2 * i + 1)
                    act.activation(sq[:], qk[:], ACT.Square).then_inc(s.squared, 1)

                def root(i):
                    act.wait_ge(s.summed, i + 1)
                    act.activation(std[:], k.aux[0][:, 0:2 * T].rearrange("p (b t) -> p b t", b=2), ACT.Sqrt,
                                   bias=k.eps[:]).then_inc(s.std, 1)

                def body(i, prev):
                    if prev:
                        inputs_2(i - 1)
                    stream.round(act, i + 1, 0)
                    if prev:
                        silu(i - 1)
                    stream.round(act, i + 1, 1)
                    inputs(i)
                    if prev:
                        square(i - 1)
                    stream.round(act, i + 1, 2)
                    stream.round(act, i + 1, 3)
                    if prev:
                        root(i - 1)

                def tail(i):
                    inputs_2(i)
                    silu(i)
                    square(i)
                    root(i)
                run_passes(act, H, body, tail)

            @block.vector
            def _(dve):
                stream.open_dve(dve)
                dve.sem_inc(s.conv, 1)
                dve.sem_inc(s.zg, 1)
                dve.memset(padded[:], 0.0).then_inc(s.cleared, 1)
                dve.wait_ge(s.rounded12, 1)
                dve.tensor_tensor(w12_lo[:], w12[:], w12_hi[:].bitcast(F32), ALU.subtract).then_inc(s.split12, 1)
                link = chain(dve, s.chain)
                dve.wait_ge(s.bg, 1)
                dve.wait_ge(s.negexp, 1)
                dve.wait_ge(s.exped, 2)
                for b in range(2):
                    link(lambda: dve.tensor_tensor(x[:, b], k.aux[1][:, 16 * b + H:16 * b + 2 * H], rows[:, 1], ALU.add))
                link(lambda: dve.tensor_scalar(t0[:], x[:], -1.0, None, ALU.mult))
                link(lambda: dve.tensor_tensor(t0[:], t0[:], x[:], ALU.min))
                dve.wait_ge(s.exped, 3)
                softplus_tail(link, dve, x[:], t1[:], t0[:], t2[:])
                for b in range(2):
                    link(lambda: dve.scalar_tensor_tensor(out=keep.g[:, b], in0=x[:, b], scalar=-1.0, in1=rows[:, 0],
                                                          op0=ALU.mult, op1=ALU.mult))
                dve.wait_ge(s.params, 16)

                def convolve(i):
                    dve.wait_ge(s.copied, 4 * i + 8)
                    dve.tensor_tensor(keep.z_all[:, bass.ds(i, 1)], k.z[3][:, None, 0:T], zsig[:, None], ALU.mult)\
                       .then_inc(s.zg, 1)
                    for tap in range(TAPS_C):
                        for t in range(3):
                            c, src = conv[:, t], padded[:, t, tap:tap + T]
                            w = params[:, bass.ds(P2_CCONV + 3 * C_HEADS * tap + t + 3 * i, 1)]
                            if tap:
                                dve.wait_ge(s.conv, 12 * i + 1 + 3 * (tap - 1) + t + 1)
                                ins = dve.scalar_tensor_tensor(out=c, in0=src, scalar=w, in1=c, op0=ALU.mult, op1=ALU.add)
                            else:
                                ins = dve.tensor_scalar(c, src, w, None, ALU.mult)
                            ins.then_inc(s.conv, 1)

                def activate(i):
                    dve.wait_ge(s.sig, i + 1)
                    dve.tensor_tensor(qk[:], conv[:, 0:2], sig[:, 0:2], ALU.mult).then_inc(s.qkv, 1)
                    dve.tensor_tensor(keep.v_all[:, bass.ds(i, 1)], conv[:, 2:3], sig[:, 2:3], ALU.mult).then_inc(s.qkv, 1)

                def norm(i):
                    dve.wait_ge(s.std, i + 1)
                    dve.reciprocal(rstd[:], std[:]).then_inc(s.norm, 1)
                    dve.wait_ge(s.norm, 3 * i + 1)
                    dve.scalar_tensor_tensor(out=k.feat[:, bass.ds(2 * i, 1)], in0=qk[:, 0:1], scalar=C_DIM ** -0.5,
                                             in1=rstd[:, 0:1], op0=ALU.mult, op1=ALU.mult).then_inc(s.norm, 1)
                    dve.tensor_tensor(k.feat[:, bass.ds(2 * i + 1, 1)], qk[:, 1:2], rstd[:, 1:2], ALU.mult).then_inc(s.norm, 1)

                def body(i, prev):
                    if prev:
                        convolve(i - 1)
                    stream.residual(dve, i + 1, 0)
                    if prev:
                        activate(i - 1)
                    for n in (1, 2, 3):
                        stream.residual(dve, i + 1, n)
                    if prev:
                        norm(i - 1)

                def tail(i):
                    convolve(i)
                    activate(i)
                    norm(i)
                run_passes(dve, H, body, tail)

            @block.tensor
            def _(pe):
                stream.open_pe(pe)
                pe.wait_ge(s.split12, 1)
                for b in range(2):
                    n = 0
                    for kk in range(KT):
                        hi, lo = k.xn_hi[:, kk, P * b:P * b + P], k.xn_lo[:, kk, P * b:P * b + P]
                        for x_, w_ in ((hi, w12_hi[:, kk]), (hi, w12_lo[:, kk]), (lo, w12_hi[:, kk])):
                            ins = pe.matmul(k.aux[1][:, 16 * b:16 * b + 2 * H], x_, w_, start=n == 0, stop=n == 3 * KT - 1)
                            n += 1
                ins.then_inc(s.bg, 1)
                pe.sem_inc(s.copied, 4)

                def sums(i):
                    pe.wait_ge(s.squared, i + 1)
                    pe.matmul(k.aux[0][:, 0:2 * T], k.ones[:], sq[:], start=True, stop=True).then_inc(s.summed, 1)

                def body(i, prev):
                    pe.wait_ge(s.copied, 4 * i + 2)
                    stream.multiply(pe, i, 0, k.xn_hi, k.xn_lo)
                    stream.multiply(pe, i, 1, k.xn_hi, k.xn_lo)
                    pe.wait_ge(s.copied, 4 * i + 4)
                    pe.wait_ge(s.zg, i + 1)
                    stream.multiply(pe, i, 2, k.xn_hi, k.xn_lo)
                    stream.multiply(pe, i, 3, k.xn_hi, k.xn_lo)
                    if prev:
                        sums(i - 1)
                run_passes(pe, H, body, sums)


def delta_phase(k, layer, keep):
    nc = k.nc
    with phase(nc, "delta", "consts took chain kv_turned rows sums kk exps amat steps1 aturned acopied xstep bt ux ucopied xx "
               "tok uw vnew ws so sstate kvp sq osum std gout yrounded ylo cleared ez") as s:
        strict, not_after, not_before = (s.sbuf(n, [P, P]) for n in ("strict", "not_after", "not_before"))
        cumulate = s.sbuf("cumulate", [P, P])
        levels, levels_t = s.sbuf("levels", [P, 6, P]), s.sbuf("levels_t", [P, 6, P])
        onorm = s.sbuf("onorm", [P, 2])
        pool = k.w_raw[:].rearrange("p a k n -> p (a k n)")

        def unit4(n):
            return pool[:, 512 * n:512 * n + 512].rearrange("p (u t) -> p u t", u=4)
        q, kk_, v = (unit4(n).rearrange("p u t -> p (u t)").rearrange("p (h t) -> p h t", h=2) for n in range(3))
        A, AT, BT = unit4(3), unit4(4), unit4(5)
        X, XT = unit4(6), unit4(7)
        k_tok, v_beta, k_end, k_beta = (s.sbuf(n, [P, 4, P]) for n in ("k_tok", "v_beta", "k_end", "k_beta"))
        intra, grown, decay, decay_t = (s.sbuf(n, [P, 4, P]) for n in ("intra", "grown", "decay", "decay_t"))
        U, WT = decay, decay_t
        UX = s.sbuf("UX", [P, 4, P])
        q_grown = BT
        S, vn = s.sbuf("S", [P, 2, P]), s.sbuf("vn", [P, 2, P])
        bg = s.sbuf("bg", [P, 2, 4])
        sums = s.sbuf("sums", [P, 2, 4])
        sc = s.sbuf("sc", [P, 5, 4])
        std, rstd = AT, A

        def flat(x):
            return x.rearrange("p u t -> p (u t)")

        def masks(m):
            return m[:, None, :].to_broadcast([P, 4, P])

        with nc.Block() as block:
            @block.sync
            def _(sp):
                for t, name in ((strict, "strict"), (not_after, "not_after"), (not_before, "not_before"), (cumulate, "cumulate")):
                    sp.dma_start(t[:], constant(k, name)).then_inc(s.consts, 16)
                sp.dma_start(levels[:].rearrange("p l t -> p (l t)"), constant(k, "levels")).then_inc(s.consts, 16)
                sp.dma_start(levels_t[:].rearrange("p l t -> p (l t)"), constant(k, "levels_t")).then_inc(s.consts, 16)
                sp.dma_start(onorm[:], k.p2[bass.ds(layer, 1), :, P2_ONORM:P2_ONORM + 2].rearrange("a p n -> p (a n)"))\
                  .then_inc(s.consts, 16)
                sp.wait_ge(s.consts, 7 * 16)
        counted = [x for x in s.all if x is not s.consts]
        shared = record(flat=flat, masks=masks, A=A, AT=AT, BT=BT, X=X, XT=XT, UX=UX, bg=bg, q=q, kk_=kk_, v=v, sums=sums, sc=sc,
                        decay=decay, decay_t=decay_t, grown=grown, U=U, WT=WT, std=std, rstd=rstd, cumulate=cumulate,
                        v_beta=v_beta, k_beta=k_beta, S=S, vn=vn, q_grown=q_grown, intra=intra, k_end=k_end, k_tok=k_tok,
                        not_after=not_after, not_before=not_before, strict=strict, levels=levels, levels_t=levels_t,
                        onorm=onorm)
        with nc.Fori(0, C_HEADS // 2) as turn:
            delta_turn(k, s, shared, turn, keep)
            with nc.Block() as block:
                @block.sync
                def _(sp):
                    for sem in counted:
                        sp.sem_clear(sem)


def delta_turn(k, s, b, turn, keep):
    nc = k.nc
    flat, masks = b.flat, b.masks
    A, AT, BT, X, XT, UX = b.A, b.AT, b.BT, b.X, b.XT, b.UX

    def bank4(bank):
        return bank[:, 0:512].rearrange("p (u t) -> p u t", u=4)

    def by_unit(x):
        return x.rearrange("p h (r t) -> p r h t", r=2)

    with nc.Block() as block:
        @block.gpsimd
        def _(pool):
            pool.tensor_copy(b.bg[:, 0].rearrange("p (r h) -> p r h", r=2), keep.beta[:, :, bass.ds(2 * turn, 2)]).then_inc(s.took, 1)
            pool.tensor_copy(b.bg[:, 1].rearrange("p (r h) -> p r h", r=2), keep.g[:, :, bass.ds(2 * turn, 2)]).then_inc(s.took, 1)

        @block.scalar
        def _(act):
            act.activation(b.q, k.feat[:, bass.ds(4 * turn, 4)].rearrange("p (h c) t -> p h c t", c=2)[:, :, 0], ACT.Copy)\
               .then_inc(s.cleared, 1)
            act.wait_ge(s.chain, 2)
            act.activation(b.sc[:, 2], b.sums[:, 0], ACT.Exp).then_inc(s.exps, 1)
            act.activation(b.sc[:, 3], b.sc[:, 1], ACT.Exp).then_inc(s.exps, 1)
            act.wait_ge(s.steps1, 2)
            for u in range(4):
                act.activation(b.decay[:, u], b.decay[:, u], ACT.Exp, bias=b.sums[:, 0, u:u + 1]).then_inc(s.exps, 1)
            for u in range(4):
                act.activation(b.decay_t[:, u], b.decay_t[:, u], ACT.Exp, bias=b.sc[:, 0, u:u + 1]).then_inc(s.exps, 1)
            act.wait_ge(s.rows, 1)
            act.activation(b.grown[:], bank4(k.aux[2]), ACT.Exp).then_inc(s.exps, 1)
            act.wait_ge(s.aturned, 1)
            act.activation(AT, bank4(k.z[2]), ACT.Copy).then_inc(s.acopied, 1)
            for level in range(1, 6):
                act.wait_ge(s.ux, level)
                act.activation(UX[:], bank4(k.aux[3]), ACT.Copy).then_inc(s.ucopied, 1)
            act.wait_ge(s.uw, 1)
            act.activation(b.U[:], bank4(k.aux[0]), ACT.Copy).then_inc(s.acopied, 1)
            act.wait_ge(s.so, 8)
            act.activation(UX[:], bank4(k.z[2]), ACT.Square).then_inc(s.sq, 1)
            act.wait_ge(s.osum, 1)
            act.activation(b.std, bank4(k.z[3]), ACT.Sqrt, bias=k.eps[:], scale=1.0 / C_DIM).then_inc(s.std, 1)
            act.wait_ge(s.gout, 3)
            act.activation(k.y_hi[:, bass.ds(10 + 2 * turn, 2)], b.rstd.rearrange("p u t -> p (u t)").rearrange("p (h t) -> p h t", h=2),
                           ACT.Copy).then_inc(s.yrounded, 1)

        @block.tensor
        def _(pe):
            pe.wait_ge(s.cleared, 3)
            for bank, src in ((k.aux[0], b.kk_), (k.aux[1], b.v)):
                for u in range(4):
                    ins = pe.transpose(bank[:, P * u:P * u + P], src[:, u % 2, P * (u // 2):P * (u // 2) + P], k.ident[:])
                ins.then_inc(s.kv_turned, 1)
            pe.wait_ge(s.took, 2)
            pe.matmul(k.aux[3][:, 0:4], b.cumulate[:], b.bg[:, 1], start=True, stop=True).then_inc(s.sums, 1)
            pe.matmul(k.aux[3][:, 4:8], k.blocks[:], b.bg[:, 1], start=True, stop=True).then_inc(s.sums, 1)
            for u in range(4):
                ins = pe.matmul(k.aux[2][:, P * u:P * u + P], b.bg[:, 1, u:u + 1].to_broadcast([P, P]), b.cumulate[:],
                                start=True, stop=True)
            ins.then_inc(s.rows, 1)
            for bank, right in ((k.z[0], b.kk_), (k.z[1], b.q)):
                for u in range(4):
                    t = slice(P * (u // 2), P * (u // 2) + P)
                    ins = pe.matmul(bank[:, P * u:P * u + P], b.kk_[:, u % 2, t], right[:, u % 2, t], start=True, stop=True)
                ins.then_inc(s.kk, 1)
            pe.wait_ge(s.amat, 5)
            for u in range(4):
                ins = pe.transpose(k.z[2][:, P * u:P * u + P], A[:, u], k.ident[:])
            ins.then_inc(s.aturned, 1)
            for level in range(1, 6):
                pe.wait_ge(s.bt, level)
                pe.wait_ge(s.xstep, 2 * level)
                for u in range(4):
                    ins = pe.matmul(k.aux[3][:, P * u:P * u + P], BT[:, u], X[:, u], start=True, stop=True)
                ins.then_inc(s.ux, 1)
                pe.wait_ge(s.ucopied, level)
                for u in range(4):
                    ins = pe.matmul(k.z[2][:, P * u:P * u + P], XT[:, u], UX[:, u], start=True, stop=True)
                ins.then_inc(s.xx, 1)
                for u in range(4):
                    ins = pe.matmul(k.z[3][:, P * u:P * u + P], UX[:, u], XT[:, u], start=True, stop=True)
                ins.then_inc(s.xx, 1)
            pe.wait_ge(s.xstep, 12)
            pe.wait_ge(s.tok, 13)
            for u in range(4):
                ins = pe.matmul(k.aux[0][:, P * u:P * u + P], XT[:, u], b.v_beta[:, u], start=True, stop=True)
            ins.then_inc(s.uw, 1)
            for u in range(4):
                ins = pe.matmul(k.aux[1][:, P * u:P * u + P], b.k_beta[:, u], XT[:, u], start=True, stop=True)
            ins.then_inc(s.uw, 1)
            for c in range(4):
                r, off = c // 2, (c % 2) * CHUNK
                rows = slice(off, off + CHUNK)
                if c == 0:
                    pe.wait_ge(s.vnew, 3)
                    pe.wait_ge(s.gout, 1)
                else:
                    pe.wait_ge(s.sstate, 2 * c)
                for h in range(2):
                    ins = pe.matmul(k.aux[3][rows, P * h:P * h + P], b.WT[:, 2 * r + h, rows], b.S[:, h], start=True, stop=True)
                ins.then_inc(s.ws, 1)
                pe.wait_ge(s.vnew, 4 + c)
                for h in range(2):
                    u = 2 * r + h
                    out = k.z[2][:, T * h + CHUNK * c:T * h + CHUNK * c + CHUNK]
                    pe.matmul(out, b.S[:, h], b.q_grown[:, u, rows], start=True, stop=False)
                    pe.matmul(out, b.vn[:, h], b.intra[:, u, rows], start=False, stop=True).then_inc(s.so, 1)
                for h in range(2):
                    ins = pe.matmul(k.aux[2][:, P * h:P * h + P], b.k_end[rows, 2 * r + h], b.vn[rows, h], start=True, stop=True)
                ins.then_inc(s.kvp, 1)
            pe.wait_ge(s.sq, 1)
            pe.matmul(k.z[3][:, 0:2 * T], k.ones[:], flat(UX[:]), start=True, stop=True).then_inc(s.osum, 1)

        @block.vector
        def _(dve):
            heads = k.feat[:, bass.ds(4 * turn, 4)].rearrange("p (h c) t -> p h c t", c=2)
            dve.tensor_copy(b.kk_, heads[:, :, 1]).then_inc(s.cleared, 1)
            dve.tensor_copy(b.v, keep.v_all[:, bass.ds(2 * turn, 2)]).then_inc(s.cleared, 1)
            dve.wait_ge(s.took, 2)
            dve.wait_ge(s.sums, 2)
            link = chain(dve, s.chain)
            link(lambda: dve.tensor_copy(b.sums[:].rearrange("p a u -> p (a u)"), k.aux[3][:, 0:8]))
            dve.tensor_scalar(b.sc[:, 0], b.sums[:, 0], -1.0, None, ALU.mult).then_inc(s.ez, 1)
            link(lambda: dve.tensor_tensor(b.sc[:, 1], b.sums[:, 1], b.sums[:, 0], ALU.subtract))
            dve.wait_ge(s.ez, 1)
            dve.wait_ge(s.rows, 1)
            dve.scalar_tensor_tensor(out=b.decay[:], in0=bank4(k.aux[2]), scalar=-1.0, in1=masks(b.not_after),
                                     op0=ALU.mult, op1=ALU.add).then_inc(s.steps1, 1)
            dve.tensor_tensor(b.decay_t[:], bank4(k.aux[2]), masks(b.not_before), ALU.add).then_inc(s.steps1, 1)
            dve.wait_ge(s.kv_turned, 2)
            dve.tensor_copy(b.k_tok[:], bank4(k.aux[0])).then_inc(s.tok, 1)
            for u in range(4):
                dve.tensor_scalar(b.v_beta[:, u], k.aux[1][:, P * u:P * u + P], b.bg[:, 0, u:u + 1], None, ALU.mult)\
                   .then_inc(s.tok, 1)
            dve.wait_ge(s.exps, 2)
            link(lambda: dve.tensor_tensor(b.sc[:, 4], b.sc[:, 2], b.bg[:, 0], ALU.mult))
            dve.wait_ge(s.tok, 1)
            for u in range(4):
                dve.tensor_scalar(b.k_beta[:, u], b.k_tok[:, u], b.sc[:, 4, u:u + 1], None, ALU.mult).then_inc(s.tok, 1)
                dve.tensor_scalar(b.k_end[:, u], b.k_tok[:, u], b.sc[:, 3, u:u + 1], None, ALU.mult).then_inc(s.tok, 1)
            dve.wait_ge(s.kk, 2)
            dve.wait_ge(s.exps, 10)
            for u in range(4):
                dve.scalar_tensor_tensor(out=A[:, u], in0=k.z[0][:, P * u:P * u + P], scalar=b.bg[:, 0, u:u + 1],
                                         in1=b.decay[:, u], op0=ALU.mult, op1=ALU.mult).then_inc(s.amat, 1)
            dve.wait_ge(s.amat, 4)
            dve.tensor_tensor(A, A, masks(b.strict), ALU.mult).then_inc(s.amat, 1)
            dve.tensor_tensor(b.intra[:], bank4(k.z[1]), b.decay_t[:], ALU.mult).then_inc(s.steps1, 1)
            dve.wait_ge(s.amat, 5)
            dve.tensor_tensor(X, A, masks(b.levels[:, 0]), ALU.mult).then_inc(s.xstep, 1)
            dve.wait_ge(s.xstep, 1)
            dve.tensor_tensor(X, X, masks(k.ident), ALU.add).then_inc(s.xstep, 1)
            dve.wait_ge(s.acopied, 1)
            link(lambda: dve.tensor_tensor(XT, AT, masks(b.levels_t[:, 0]), ALU.mult))
            link(lambda: dve.tensor_tensor(XT, XT, masks(k.ident), ALU.add))
            for level in range(1, 6):
                if level > 1:
                    dve.wait_ge(s.ux, level - 1)
                dve.tensor_tensor(BT, AT, masks(b.levels_t[:, level]), ALU.mult).then_inc(s.bt, 1)
                dve.wait_ge(s.xx, 2 * level - 1 + 1)
                dve.tensor_tensor(X, bank4(k.z[2]), X, ALU.add).then_inc(s.xstep, 1)
                dve.tensor_tensor(XT, bank4(k.z[3]), XT, ALU.add).then_inc(s.xstep, 1)
            dve.memset(b.S[:], 0.0).then_inc(s.vnew, 1)
            dve.memset(b.vn[:], 0.0).then_inc(s.vnew, 1)
            dve.wait_ge(s.exps, 11)
            dve.wait_ge(s.ux, 5)
            dve.tensor_tensor(b.q_grown.rearrange("p (r h) t -> p r h t", r=2), by_unit(b.q),
                              b.grown[:].rearrange("p (r h) t -> p r h t", r=2), ALU.mult).then_inc(s.gout, 1)
            dve.wait_ge(s.uw, 2)
            dve.tensor_copy(b.WT[:], bank4(k.aux[1])).then_inc(s.vnew, 1)
            dve.wait_ge(s.acopied, 2)
            for c in range(4):
                r, off = c // 2, (c % 2) * CHUNK
                rows = slice(off, off + CHUNK)
                dve.wait_ge(s.ws, c + 1)
                if c:
                    dve.wait_ge(s.kvp, c)
                else:
                    dve.wait_ge(s.vnew, 3)
                dve.tensor_tensor(b.vn[rows], b.U[rows, 2 * r:2 * r + 2],
                                  k.aux[3][rows, 0:2 * P].rearrange("p (h t) -> p h t", h=2), ALU.subtract).then_inc(s.vnew, 1)
                dve.wait_ge(s.kvp, c + 1)
                for h in range(2):
                    dve.scalar_tensor_tensor(out=b.S[:, h], in0=b.S[:, h], scalar=b.grown[:, 2 * r + h, off + CHUNK - 1:off + CHUNK],
                                             in1=k.aux[2][:, P * h:P * h + P], op0=ALU.mult, op1=ALU.add).then_inc(s.sstate, 1)
            dve.wait_ge(s.std, 1)
            dve.reciprocal(b.rstd, b.std).then_inc(s.gout, 1)
            dve.wait_ge(s.gout, 2)
            dve.wait_ge(s.so, 8)
            dve.scalar_tensor_tensor(out=flat(UX[:]), in0=k.z[2][:, 0:512], scalar=b.onorm[:, 0:1], in1=flat(b.rstd), op0=ALU.mult,
                                     op1=ALU.mult).then_inc(s.ylo, 1)
            dve.wait_ge(s.ylo, 1)
            y2 = flat(b.rstd).rearrange("p (h t) -> p h t", h=2)
            dve.tensor_tensor(y2, flat(UX[:]).rearrange("p (h t) -> p h t", h=2), keep.z_all[:, bass.ds(2 * turn, 2)], ALU.mult)\
               .then_inc(s.gout, 1)
            dve.wait_ge(s.yrounded, 1)
            dve.tensor_tensor(k.y_lo[:, bass.ds(10 + 2 * turn, 2)], y2, k.y_hi[:, bass.ds(10 + 2 * turn, 2)].bitcast(F32),
                              ALU.subtract).then_inc(s.ylo, 1)


def out_phase_1(k, x_dram):
    nc = k.nc
    with phase(nc, "out1", STREAM + "params xin merged_hi merged_lo copied acc sq summed std norm step cleared") as s:
        stream = Stream(k, s, SLOT_OUT_1)
        o = s.sbuf("o", [P, KT, T])
        acc, sq = s.sbuf("acc", [P, T]), s.sbuf("sq", [P, 4, T])
        std, rstd = s.sbuf("std", [P, T]), s.sbuf("rstd", [P, T])
        w = s.sbuf("w", [P, KT])
        passes = KT // 4
        with nc.Block() as block:
            @block.sync
            def _(sp):
                sp.dma_start(w[:], k.p1[:, P1_POST:P1_POST + KT]).then_inc(s.params, 16)
                sp.wait_ge(s.merged_lo, 4)
                sp.dma_start(k.feat[:], x_dram).then_inc(s.xin, 16)
                stream.loads(sp, passes)

            @block.scalar
            def _(act):
                stream.open_act(act)
                for q in range(4):
                    act.activation(k.xn_hi[:, 4 * q:4 * q + 4], k.feat[:, 4 * q:4 * q + 4], ACT.Copy).then_inc(s.merged_hi, 1)

                def copies(i, half):
                    act.wait_ge(s.used, stream.done(i, 2 * half + 1))
                    act.wait_ge(s.acc, 4 * i + 2 * half + 2)
                    for b in (2 * half, 2 * half + 1):
                        act.activation(sq[:, b], k.z[b][:, 0:T], ACT.Square).then_inc(s.sq, 1)
                    for b in (2 * half, 2 * half + 1):
                        act.activation(o[:, bass.ds(4 * i + b, 1)], k.z[b][:, None, 0:T], ACT.Copy).then_inc(s.copied, 1)

                def body(i, prev):
                    if prev:
                        copies(i - 1, 1)
                    stream.round(act, i + 1, 0)
                    stream.round(act, i + 1, 1)
                    copies(i, 0)
                    stream.round(act, i + 1, 2)
                    stream.round(act, i + 1, 3)
                run_passes(act, passes, body, lambda i: copies(i, 1))
                act.wait_ge(s.summed, 1)
                act.activation(std[:], k.aux[0][:, 0:T], ACT.Sqrt, bias=k.eps[:], scale=1.0 / D).then_inc(s.std, 1)

            @block.vector
            def _(dve):
                stream.open_dve(dve)
                dve.sem_inc(s.acc, 4)
                dve.memset(acc[:], 0.0).then_inc(s.cleared, 1)
                dve.wait_ge(s.cleared, 1)
                for q in range(4):
                    dve.wait_ge(s.merged_hi, q + 1)
                    dve.tensor_tensor(k.xn_lo[:, 4 * q:4 * q + 4], k.feat[:, 4 * q:4 * q + 4],
                                      k.xn_hi[:, 4 * q:4 * q + 4].bitcast(F32), ALU.subtract).then_inc(s.merged_lo, 1)

                def sums(i, half):
                    dve.wait_ge(s.sq, 4 * i + 2 * half + 2)
                    for b in (2 * half, 2 * half + 1):
                        dve.tensor_tensor(acc[:], acc[:], sq[:, b], ALU.add).then_inc(s.acc, 1)
                        dve.wait_ge(s.acc, 4 * i + 5 + b)

                def body(i, prev):
                    if prev:
                        sums(i - 1, 1)
                    stream.residual(dve, i + 1, 0)
                    stream.residual(dve, i + 1, 1)
                    sums(i, 0)
                    stream.residual(dve, i + 1, 2)
                    stream.residual(dve, i + 1, 3)
                run_passes(dve, passes, body, lambda i: sums(i, 1))
                dve.wait_ge(s.std, 1)
                dve.reciprocal(rstd[:], std[:]).then_inc(s.norm, 1)
                dve.wait_ge(s.norm, 1)
                dve.wait_ge(s.params, 16)
                dve.wait_ge(s.xin, 16)
                for t in range(KT):
                    dve.scalar_tensor_tensor(out=o[:, t], in0=o[:, t], scalar=w[:, t:t + 1], in1=rstd[:], op0=ALU.mult,
                                             op1=ALU.mult).then_inc(s.norm, 1)
                for q in range(4):
                    dve.wait_ge(s.norm, 4 * q + 5)
                    f = k.feat[:, 4 * q:4 * q + 4]
                    dve.tensor_tensor(f, f, o[:, 4 * q:4 * q + 4], ALU.add).then_inc(s.step, 1)

            @block.tensor
            def _(pe):
                stream.open_pe(pe)
                pe.sem_inc(s.copied, 4)

                def products(i, prev):
                    for sl in range(SLOTS):
                        if not prev and sl < 2:
                            pe.wait_ge(s.merged_lo, 2 * sl + 2)
                        if sl % 2 == 0:
                            pe.wait_ge(s.copied, 4 * i + 2 + sl)
                        stream.multiply(pe, i, sl, k.xn_hi, k.xn_lo)
                run_passes(pe, passes, products)
                pe.wait_ge(s.acc, 4 * passes + 4)
                pe.matmul(k.aux[0][:, 0:T], k.ones[:], acc[:], start=True, stop=True).then_inc(s.summed, 1)


def out_phase_2(k, layer, state, out):
    nc = k.nc
    with phase(nc, "out2", STREAM + "xin added stored") as s:
        stream = Stream(k, s, layer * SLOTS_2 + SLOTS_1 + SLOT_OUT_2)
        passes = KT // 4
        with nc.Block() as block:
            @block.sync
            def _(sp):
                sp.dma_start(k.feat[:], state).then_inc(s.xin, 16)
                stream.loads(sp, passes)
                sp.wait_ge(s.added, 4 * passes + 4)
                sp.dma_start(out, k.feat[:]).then_inc(s.stored, 16)
                sp.wait_ge(s.stored, 16)

            @block.scalar
            def _(act):
                stream.open_act(act)
                with act.Fori(1, passes + 1) as i:
                    for n in range(SLOTS):
                        stream.round(act, i, n)

            @block.vector
            def _(dve):
                stream.open_dve(dve)

                def add(i, half):
                    for b in (2 * half, 2 * half + 1):
                        dve.wait_ge(s.used, stream.done(i, 2 * half + 1))
                        f = k.feat[:, bass.ds(4 * i + b, 1)]
                        dve.tensor_tensor(f, k.z[b][:, None, 0:T], f, ALU.add).then_inc(s.added, 1)

                def body(i, prev):
                    if prev:
                        add(i - 1, 1)
                    stream.residual(dve, i + 1, 0)
                    stream.residual(dve, i + 1, 1)
                    if not prev:
                        dve.wait_ge(s.xin, 16)
                    add(i, 0)
                    stream.residual(dve, i + 1, 2)
                    stream.residual(dve, i + 1, 3)
                run_passes(dve, passes, body, lambda i: add(i, 1))

            @block.tensor
            def _(pe):
                stream.open_pe(pe)
                pe.sem_inc(s.added, 4)

                def products(i, prev):
                    for sl in range(SLOTS):
                        if sl % 2 == 0:
                            pe.wait_ge(s.added, 4 * i + 2 + sl)
                        stream.multiply(pe, i, sl, k.y_hi, k.y_lo)
                run_passes(pe, passes, products)


class Kernel:
    pass


def build(nc, t, stop=None):
    with ExitStack() as stack:
        def sbuf(name, shape, dt=F32):
            return stack.enter_context(nc.sbuf_tensor(name, shape, dt))
        k = Kernel()
        k.nc = nc
        k.constants, k.w, k.p1, k.p2 = t["constants"], t["w"], t["p1"], t["p2"]
        k.lru_w, k.pw, k.w12, k.rows_c = t["lru_w"], t["pw"], t["w12"], t["rows_c"]
        k.w_raw = sbuf("w_raw", [P, RAW, SLOT_K, CHUNK_COLS])
        k.w_hi = sbuf("w_hi", [P, SLOTS, SLOT_K, CHUNK_COLS], F32R)
        k.w_lo = sbuf("w_lo", [P, SLOTS, SLOT_K, CHUNK_COLS], F32R)
        k.xn_hi, k.xn_lo = sbuf("xn_hi", [P, KT, T], F32R), sbuf("xn_lo", [P, KT, T], F32R)
        k.y_hi, k.y_lo = sbuf("y_hi", [P, KT, T], F32R), sbuf("y_lo", [P, KT, T], F32R)
        k.feat = sbuf("feat", [P, KT, T])
        k.ident, k.ones, k.blocks = sbuf("ident", [P, P]), sbuf("ones", [P, P]), sbuf("blocks", [P, P])
        k.eps = sbuf("eps", [P, 1])
        k.cos_t, k.sin_t = sbuf("cos_t", [P, T]), sbuf("sin_t", [P, T])
        k.z = [stack.enter_context(nc.psum_tensor(f"z{n}", [P, 2 * T], F32)) for n in range(4)]
        k.aux = [stack.enter_context(nc.psum_tensor(f"aux{n}", [P, 2 * T], F32)) for n in range(4)]

        setup_phase(k)
        norm_phase(k, "norm1", t["p1"][:, P1_NORM:P1_NORM + KT], t["x"], None, True)
        lru_phase(k)
        if stop == "lru":
            return dump(k, t)
        merge_phase(k, "merge_a", SLOT_MERGE_A, True)
        rope_tables(k, "rope1", None, "freq_1")
        if stop == "rope":
            return dump(k, t)
        attention_phase(k, "att1", record(
            heads_per_tile=1, n_heads=16, passes=8, first_slot=SLOT_ATT_1, kv_width=512, turn="turn_1",
            mask="window_1", sinks=t["sinks_1"], norms=None, scale=HEAD_DIM_1 ** -0.5))
        if stop == "att1":
            return dump(k, t)
        merge_phase(k, "merge_b", SLOT_MERGE_B, False)
        out_phase_1(k, t["x"])
        if stop == "block1":
            return dump(k, t)
        rope_tables(k, "rope2", t["positions"], "freq_2")
        with nc.Fori(0, LAYERS) as layer:
            norm_phase(k, "norm2", t["p2"][bass.ds(layer, 1), :, P2_NORM:P2_NORM + KT].rearrange("a p n -> p (a n)"),
                       None, t["state"])
            attention_phase(k, "att2", record(
                heads_per_tile=2, n_heads=HEADS_2, passes=3, first_slot=layer * SLOTS_2 + SLOTS_1 + SLOT_ATT_2,
                kv_width=256, turn="turn_2", mask="window_2", sinks=t["sinks_2"][bass.ds(layer, 1)],
                norms=t["p2"][bass.ds(layer, 1), :, P2_QN:P2_KN + 1].rearrange("a p n -> p (a n)"),
                scale=HEAD_DIM_2 ** -0.5))
            if stop == "att2":
                pass
            else:
                conv_phase(k, layer)
                with ExitStack() as kept:
                    keep = record(**{n: kept.enter_context(nc.sbuf_tensor(f"keep_{n}", shape, F32)) for n, shape in (
                        ("v_all", [P, C_HEADS, T]), ("z_all", [P, C_HEADS, T]), ("beta", [P, 2, C_HEADS]),
                        ("g", [P, 2, C_HEADS]))})
                    delta_inputs_phase(k, layer, keep)
                    delta_phase(k, layer, keep)
            out_phase_2(k, layer, t["state"], t["out"])
        if stop == "att2":
            dump(k, t)


def dump(k, t):
    nc = k.nc
    with nc.semaphore("dumped") as sem:
        with nc.Block() as block:
            @block.sync
            def _(sp):
                for name, src in (("feat", k.feat[:]), ("y_hi", k.y_hi[:].bitcast(F32)), ("y_lo", k.y_lo[:].bitcast(F32)),
                                  ("cos", k.cos_t[:]), ("sin", k.sin_t[:])):
                    if "dbg_" + name in t and not (name in ("cos", "sin") and "no_rope" in t):
                        sp.dma_start(t["dbg_" + name], src).then_inc(sem, 16)
                sp.wait_ge(sem, 80 if "dbg_cos" in t else 48)


def slots_of(matrix, column_tiles):
    out = []
    for a, b in zip(column_tiles[0::2], column_tiles[1::2]):
        chunk = np.concatenate([matrix[:, a:a + P], matrix[:, b:b + P]], 1)
        halves = chunk.reshape(2, SLOT_K, P, CHUNK_COLS).transpose(0, 2, 1, 3)
        out.append(halves.reshape(2, P, SLOT_K * CHUNK_COLS))
    return np.concatenate(out, 0)


def tiles(start, n):
    return [start + P * j for j in range(n)]


def by_partition(v):
    v = np.asarray(v)
    return v.reshape(-1, P).T


def lay_out(x, norm_pre_w, w_in, conv_w, conv_b, lru_w_r, lru_b_r, lru_w_i, lru_b_i, lru_lambda, attn_sink, w_proj_a,
            w_proj_b, w_out, norm_post_w, positions_2, norm_w_2, w_in_2, q_norm_w_2, k_norm_w_2, sinks_2, b_conv_w_2,
            b_conv_b_2, b_ln_w_2, b_ln_b_2, b_pw_w_2, b_pw_b_2, c_conv_w_2, c_a_log_2, c_dt_bias_2, c_onorm_w_2, w_out_2):
    a = {"x": x[0].T.reshape(KT, P, T).transpose(1, 0, 2)}
    u0, g0, q0 = 0, D, 2 * D
    k0, v0 = 3 * D, 3 * D + 512
    ga0, ml0, ma0 = 3 * D + 1024, 4 * D + 1024, 5 * D + 1024
    w = w_in[0]
    lru = [c for i in range(8) for s in (u0, g0) for c in tiles(s + 256 * i, 2)]
    att = tiles(k0, 4) + tiles(v0, 4) + [c for i in range(8) for s in (q0, ga0) for c in tiles(s + 256 * i, 2)]

    def merged(m0, proj):
        m, p_ = slots_of(w, tiles(m0, KT)), slots_of(proj, tiles(0, KT))
        return np.stack([m.reshape(8, 2, P, -1), p_.reshape(8, 2, P, -1)], 1).reshape(32, P, -1)
    w_1 = np.concatenate([slots_of(w, lru), merged(ml0, w_proj_a[0]), slots_of(w, att), merged(ma0, w_proj_b[0]),
                              slots_of(w_out[0], tiles(0, KT))], 0)
    a["p1"] = np.concatenate([by_partition(v) for v in (norm_pre_w, conv_w, conv_b, lru_b_r, lru_b_i, lru_lambda, norm_post_w)], 1)
    lw = np.stack([lru_w_r[0], lru_w_i[0]], 0)
    a["lru_w"] = lw.transpose(2, 3, 1, 0, 4).reshape(8, 2, P, 4, P).transpose(0, 2, 1, 3, 4).reshape(8, P, 8 * P)
    a["sinks_1"] = attn_sink
    a["sinks_2"] = sinks_2
    a["positions"] = positions_2
    widths = (768, 256, 256, 768, 512, 512, 512, 768, 768, 768, 6, 6, 768)
    q_, k_, v_, za, ba, bg, zb, cq, ck, cv, b_, a_, zc = np.cumsum((0,) + widths[:-1]).tolist()
    order = tiles(k_, 2) + tiles(v_, 2) + [c for i in range(3) for s in (q_, za) for c in tiles(s + 256 * i, 2)]
    order += tiles(ba, 2) + tiles(bg, 2) + tiles(ba + 256, 2) + tiles(bg + 256, 2) + tiles(zb, 4)
    order += [s + P * h for h in range(C_HEADS) for s in (cq, ck, cv, zc)]
    w_2 = [np.concatenate([slots_of(w_in_2[l], order), slots_of(w_out_2[l], tiles(0, KT))], 0) for l in range(LAYERS)]
    a["w"] = np.concatenate([w_1] + w_2 + [w_1[:SLOTS]], 0)
    a["w12"] = w_in_2[:, :, b_:b_ + 12].reshape(LAYERS, KT, P, 12).transpose(0, 2, 1, 3).reshape(LAYERS, P, KT * 12)
    rows = []
    for l in range(LAYERS):
        qn, kn = (np.concatenate([v[l], v[l]])[:, None] for v in (q_norm_w_2, k_norm_w_2))
        cc = c_conv_w_2[l].reshape(TAPS_C, 3, C_HEADS, P).transpose(3, 0, 2, 1).reshape(P, -1)
        rows.append(np.concatenate([by_partition(norm_w_2[l]), qn, kn, c_onorm_w_2[l][:, None], by_partition(b_conv_w_2[l]),
                                    by_partition(b_conv_b_2[l]), by_partition(b_ln_w_2[l]), by_partition(b_ln_b_2[l]),
                                    by_partition(b_pw_b_2[l]), cc], 1))
    a["p2"] = np.stack(rows, 0)
    a["pw"] = b_pw_w_2.reshape(LAYERS, B_TILES, P, B_TILES * P).transpose(0, 2, 1, 3).reshape(LAYERS, P, -1)
    a["rows_c"] = np.concatenate([c_a_log_2, c_dt_bias_2], 1)
    a["constants"] = CONSTANTS
    return {n: np.ascontiguousarray(v) for n, v in a.items()}


def kernel(**inputs):
    import concourse.bacc as bacc
    from concourse.bass_utils import run_bass_kernel_spmd

    arrays = lay_out(**{n: np.asarray(v) for n, v in inputs.items()})
    nc = bacc.Bacc("TRN2", target_bir_lowering=False, num_devices=1)
    t = {n: nc.dram_tensor(f"in_{n}_dram", v.shape, mybir.dt.from_np(v.dtype), kind="ExternalInput").ap()
         for n, v in arrays.items()}
    t["out"] = nc.dram_tensor("out_0_dram", (P, KT, T), F32, kind="ExternalOutput").ap()
    t["state"] = nc.dram_tensor("state_dram", (P, KT, T), F32, kind="Internal").ap()
    build(nc, t)
    r = run_bass_kernel_spmd(nc, [{f"in_{n}_dram": v for n, v in arrays.items()}], core_ids=[0])
    y = r.results[0]["out_0_dram"]
    return np.ascontiguousarray(y.transpose(2, 1, 0).reshape(1, T, D))
```

```python
import math
from collections import namedtuple
from contextlib import ExitStack, contextmanager

import numpy as np

import concourse.bass as bass
from concourse import mybir

F32 = mybir.dt.float32
F32R = mybir.dt.float32r
I32 = mybir.dt.int32
ACT = mybir.ActivationFunctionType
ALU = mybir.AluOpType
AX_X = mybir.AxisListType.X

P = 128
D = 2048
T = 256
KT = D // P
CHUNK_COLS = 256
SLOT_K = KT // 2
SLOTS = 4
RAW = 2
NORM_EPS = 1e-6
NEG = -1e30
ROPE_THETA = 500000.0

LRU_PASSES = KT // 2
KV_HEADS_1, HEAD_DIM_1, ROT_1 = 4, 128, 32
LAYERS = 2
HEAD_DIM_2, HEADS_2, ROT_2 = 64, 12, 16
B_TILES = 4
TAPS_B = 31
C_HEADS, C_DIM, CHUNK = 6, 128, 64
TAPS_C = 4

SLOT_LRU = 0
SLOT_MERGE_A = SLOT_LRU + 4 * LRU_PASSES
SLOT_ATT_1 = SLOT_MERGE_A + 4 * (KT // 2)
SLOT_MERGE_B = SLOT_ATT_1 + 4 * 2 + 4 * (KT // 2)
SLOT_OUT_1 = SLOT_MERGE_B + 4 * (KT // 2)
SLOTS_1 = SLOT_OUT_1 + 2 * (KT // 2)
SLOT_ATT_2 = 0
SLOT_CONV_2 = SLOT_ATT_2 + 4 + 4 * 3
SLOT_DELTA_2 = SLOT_CONV_2 + 4 * 3
SLOT_OUT_2 = SLOT_DELTA_2 + 4 * C_HEADS
SLOTS_2 = SLOT_OUT_2 + 2 * (KT // 2)

P1_NORM, P1_CONV, P1_CONVB = 0, 16, 80
P1_BR, P1_BI, P1_LAM, P1_POST = 96, 128, 160, 192
P1_COLS = 208
P2_NORM, P2_QN, P2_KN, P2_ONORM = 0, 16, 17, 18
P2_BCONV, P2_BCONVB, P2_LNW, P2_LNB, P2_PWB = 19, 19 + 124, 147, 151, 155
P2_CCONV = 159
P2_COLS = P2_CCONV + TAPS_C * 3 * C_HEADS


def constant_columns():
    cols, parts, at = {}, [], 0

    def put(name, a):
        nonlocal at
        a = np.asarray(a, np.float32).reshape(P, -1)
        cols[name] = (at, a.shape[1])
        parts.append(a)
        at += a.shape[1]

    i, j = np.arange(P)[:, None], np.arange(P)[None, :]
    same = i // CHUNK == j // CHUNK
    put("ident", i == j)
    put("ones", np.ones((P, P)))
    put("blocks", same)
    put("cumulate", same & (i <= j))
    put("before", np.where(same & (j < i), 0.0, NEG))
    put("not_before", np.where(same & (j >= i), 0.0, NEG))
    put("strict", same & (j < i))
    for name, flip in (("levels", False), ("levels_t", True)):
        masks = []
        for level in range(6):
            b = 1 << level
            m = -1.0 * ((i // (2 * b) == j // (2 * b)) & (i // b % 2 == 1) & (j // b % 2 == 0))
            masks.append(m.T if flip else m)
        put(name, np.stack(masks, 1))
    q = np.arange(P)[:, None, None] + P * np.arange(2)[None, :, None]
    s = np.arange(T)[None, None, :]
    put("window_1", np.where(np.abs(q - s) <= 128, 0.0, NEG))
    put("window_2", np.where((q - s >= 0) & (q - s < 128), 0.0, NEG))
    for name, rot, head in (("1", ROT_1, HEAD_DIM_1), ("2", ROT_2, HEAD_DIM_2)):
        half = rot // 2
        freq = ROPE_THETA ** (-np.arange(0, rot, 2, dtype=np.float64) / rot)
        column, turn = np.zeros(P), np.zeros((P, P))
        for base in range(0, P, head):
            for d in range(rot):
                column[base + d] = freq[d % half]
            for d in range(half):
                turn[base + d + half, base + d] = -1.0
                turn[base + d, base + d + half] = 1.0
        put("freq_" + name, np.stack([column, column], 1))
        put("turn_" + name, turn)
    return cols, np.concatenate(parts, 1)


CONST_COLS, CONSTANTS = constant_columns()


def record(**fields):
    return namedtuple("Record", fields.keys())(*fields.values())


@contextmanager
def phase(nc, name, sems):
    with ExitStack() as stack:
        def sbuf(n, shape, dt=F32):
            return stack.enter_context(nc.sbuf_tensor(f"{name}_{n}", shape, dt))
        named = {n: stack.enter_context(nc.semaphore(f"{name}_{n}")) for n in sems.split()}
        s = record(**named, sbuf=sbuf, all=list(named.values()))
        yield s
        with nc.Block() as block:
            @block.sync
            def _(sp):
                for sem in s.all[0::5]:
                    sp.sem_clear(sem)

            @block.gpsimd
            def _(pool):
                for sem in s.all[1::5]:
                    pool.sem_clear(sem)

            @block.scalar
            def _(act):
                for sem in s.all[2::5]:
                    act.sem_clear(sem)

            @block.vector
            def _(dve):
                for sem in s.all[3::5]:
                    dve.sem_clear(sem)

            @block.tensor
            def _(pe):
                for sem in s.all[4::5]:
                    pe.sem_clear(sem)


STREAM = "loaded0 loaded1 rounded split used "


class Stream:

    def __init__(self, k, s, first):
        self.k, self.s, self.first = k, s, first
        self.loaded = (s.loaded0, s.loaded1)

    def open_act(self, act):
        act.sem_inc(self.s.rounded, SLOTS)

    def open_dve(self, dve):
        dve.sem_inc(self.s.split, RAW + SLOTS)

    def open_pe(self, pe, free=SLOTS):
        pe.sem_inc(self.s.used, free)

    def load(self, sp, i, s):
        sp.wait_ge(self.s.split, 4 * i + s + 1)
        src = self.k.w[bass.ds(self.first + 4 * i + s, 1)].rearrange("a p n -> p (a n)")
        dst = self.k.w_raw[:, s % RAW].rearrange("p k n -> p (k n)")
        sp.dma_start(dst, src).then_inc(self.loaded[s % RAW], 16)

    def round(self, act, i, s):
        act.wait_ge(self.loaded[s % RAW], 16 * (2 * (i - 1) + s // RAW + 1))
        act.wait_ge(self.s.used, 4 * i + s + 1)
        act.activation(self.k.w_hi[:, s], self.k.w_raw[:, s % RAW], ACT.Copy).then_inc(self.s.rounded, 1)

    def residual(self, dve, i, s):
        dve.wait_ge(self.s.rounded, 4 * i + s + 1)
        dve.tensor_tensor(self.k.w_lo[:, s], self.k.w_raw[:, s % RAW], self.k.w_hi[:, s].bitcast(F32),
                          ALU.subtract).then_inc(self.s.split, 1)

    def loads(self, sp, passes):
        with sp.Fori(1, passes + 1) as i:
            for s in range(SLOTS):
                self.load(sp, i, s)

    def multiply(self, pe, i, s, hi, lo, tokens_out=False):
        k = self.k
        pe.wait_ge(self.s.split, 4 * i + s + 1 + RAW)
        for m in range(2):
            out = k.z[2 * (s // 2) + m][:, 0:T]
            for kk in range(SLOT_K):
                row = SLOT_K * (s % 2) + kk
                first, last = row == 0, row == KT - 1
                if tokens_out:
                    w_hi, w_lo = k.w_hi[:, s, kk], k.w_lo[:, s, kk]
                    x_hi, x_lo = hi[:, row, P * m:P * m + P], lo[:, row, P * m:P * m + P]
                    pairs = ((x_hi, w_hi), (x_hi, w_lo), (x_lo, w_hi))
                else:
                    w_hi, w_lo = k.w_hi[:, s, kk, P * m:P * m + P], k.w_lo[:, s, kk, P * m:P * m + P]
                    pairs = ((w_hi, hi[:, row]), (w_hi, lo[:, row]), (w_lo, hi[:, row]))
                for n, (a, b) in enumerate(pairs):
                    ins = pe.matmul(out, a, b, start=first and n == 0, stop=last and n == 2)
        ins.then_inc(self.s.used, 1)

    def done(self, i, s):
        return SLOTS + 4 * i + s + 1


def run_passes(engine, count, body, tail=None):
    body(0, False)
    if count > 4:
        with engine.Fori(1, count) as i:
            body(i, True)
    else:
        for i in range(1, count):
            body(i, True)
    if tail is not None:
        tail(count - 1)


def last_apart(engine, count, body, tail, then=None):
    body(0, False)
    if then is not None:
        then()
    with engine.Fori(1, count - 1) as i:
        body(i, True)
    body(count - 1, True, True)
    tail(count - 1)


def constant(k, name, p=P):
    at, n = CONST_COLS[name]
    return k.constants[0:p, at:at + n]


def norm_phase(k, name, weight, source, keep, first=False):
    nc = k.nc
    with phase(nc, name, STREAM + "consts eps x0 x1 x2 x3 weight squared summed rstd scaled xrounded xsplit kept") as s:
        squares = s.sbuf("squares", [P, KT, T])
        rstd = s.sbuf("rstd", [P, T])
        w = s.sbuf("w", [P, KT])
        x_loaded = (s.x0, s.x1, s.x2, s.x3)
        stream = Stream(k, s, -SLOTS)
        q4 = [slice(4 * q, 4 * q + 4) for q in range(4)]
        with nc.Block() as block:
            @block.sync
            def _(sp):
                if source is not None:
                    for q in range(4):
                        sp.dma_start(k.feat[:, q4[q]], source[:, q4[q]]).then_inc(x_loaded[q], 16)
                if first:
                    for there, name in ((k.ones, "ones"), (k.ident, "ident"), (k.blocks, "blocks")):
                        sp.dma_start(there[:], constant(k, name)).then_inc(s.consts, 16)
                sp.dma_start(w[:], weight).then_inc(s.weight, 16)
                if first:
                    for n in range(SLOTS):
                        stream.load(sp, 1, n)
                    sp.wait_ge(s.consts, 48)
                if keep is not None:
                    sp.dma_start(keep, k.feat[:]).then_inc(s.kept, 16)
                    sp.wait_ge(s.kept, 16)

            @block.gpsimd
            def _(pool):
                if first:
                    pool.memset(k.eps[:], NORM_EPS).then_inc(s.eps, 1)

            @block.scalar
            def _(act):
                for q in range(4):
                    if source is not None:
                        act.wait_ge(x_loaded[q], 16)
                    act.activation(squares[:, q4[q]], k.feat[:, q4[q]], ACT.Square).then_inc(s.squared, 1)
                if first:
                    stream.open_act(act)
                    stream.round(act, 1, 0)
                    stream.round(act, 1, 1)
                if first:
                    act.wait_ge(s.eps, 1)
                act.wait_ge(s.summed, 1)
                inverse_root(act, k, rstd[:], k.aux[0][:, 0:T], 1.0 / D, s.rstd, 0)
                for q in range(4):
                    act.wait_ge(s.scaled, 4 * q + 4)
                    act.activation(k.xn_hi[:, q4[q]], squares[:, q4[q]], ACT.Copy).then_inc(s.xrounded, 1)
                if first:
                    stream.round(act, 1, 2)
                    stream.round(act, 1, 3)

            @block.tensor
            def _(pe):
                if first:
                    stream.open_pe(pe, 2 * SLOTS)
                    pe.wait_ge(s.consts, 48)
                for t in range(KT):
                    if t % 4 == 0:
                        pe.wait_ge(s.squared, t // 4 + 1)
                    ins = pe.matmul(k.aux[0][:, 0:T], k.ones[:], squares[:, t], start=t == 0, stop=t == KT - 1)
                ins.then_inc(s.summed, 1)

            @block.vector
            def _(dve):
                if first:
                    stream.open_dve(dve)
                    stream.residual(dve, 1, 0)
                    stream.residual(dve, 1, 1)
                dve.wait_ge(s.weight, 16)
                dve.wait_ge(s.rstd, 2)
                for t in range(KT):
                    dve.scalar_tensor_tensor(out=squares[:, t], in0=k.feat[:, t], scalar=w[:, t:t + 1], in1=rstd[:],
                                             op0=ALU.mult, op1=ALU.mult).then_inc(s.scaled, 1)
                for q in range(4):
                    dve.wait_ge(s.xrounded, q + 1)
                    dve.tensor_tensor(k.xn_lo[:, q4[q]], squares[:, q4[q]], k.xn_hi[:, q4[q]].bitcast(F32),
                                      ALU.subtract).then_inc(s.xsplit, 1)
                if first:
                    stream.residual(dve, 1, 2)
                    stream.residual(dve, 1, 3)


def inverse_root(act, k, out, mean_of, scale, sem, before):
    act.activation(out, mean_of, ACT.Ln, bias=k.eps[:], scale=scale).then_inc(sem, 1)
    act.wait_ge(sem, before + 1)
    act.activation(out, out, ACT.Exp, scale=-0.5).then_inc(sem, 1)


def softplus_tail(link, dve, x, w, z, acc):
    link(lambda: dve.tensor_scalar(z, w, 2.0, None, ALU.add))
    link(lambda: dve.reciprocal(acc, z))
    link(lambda: dve.tensor_tensor(w, w, acc, ALU.mult))
    link(lambda: dve.tensor_tensor(z, w, w, ALU.mult))
    link(lambda: dve.tensor_scalar(acc, z, 1.0 / 17, 1.0 / 15, ALU.mult, ALU.add))
    for n in range(13, 0, -2):
        link(lambda: dve.tensor_tensor(acc, acc, z, ALU.mult))
        link(lambda: dve.tensor_scalar(acc, acc, 1.0 / n, None, ALU.add))
    link(lambda: dve.tensor_tensor(acc, acc, w, ALU.mult))
    link(lambda: dve.tensor_scalar(x, x, 0.0, None, ALU.max))
    link(lambda: dve.scalar_tensor_tensor(out=x, in0=acc, scalar=2.0, in1=x, op0=ALU.mult, op1=ALU.add))


def after(engine, sem, value):
    if not (isinstance(value, int) and value == 0):
        engine.wait_ge(sem, value)


def chain(engine, sem):
    count = [0]

    def link(make):
        count[0] += 1
        make().then_inc(sem, 1)
        engine.wait_ge(sem, count[0])
    return link


def lru_phase(k):
    nc = k.nc
    CONV = 8
    DSTEPS = 8
    with phase(nc, "lru", STREAM + "gated weights params exped chain cleared ucopied conv gsig zcopied gates taken "
               "decay dsteps rounded_y ydone") as s:
        stream = Stream(k, s, SLOT_LRU)
        params = s.sbuf("params", [P, P1_COLS])
        gate_w = s.sbuf("gate_w", [P, 2, 4, P])
        padded = s.sbuf("padded", [P, 2, T + 4])
        g_all = s.sbuf("g_all", [P, KT, T])
        gsig = s.sbuf("gsig", [P, 2, T])
        gate_r, gate_i, decay, tau = (s.sbuf(n, [P, 2, 2, T]) for n in ("gate_r", "gate_i", "decay", "tau"))
        y = s.sbuf("y", [P, 2, T])
        scale_a, scale_t = s.sbuf("scale_a", [P, 32]), s.sbuf("scale_t", [P, 32])
        tmp = [s.sbuf(f"tmp{n}", [P, 32]) for n in range(3)]
        rate = s.sbuf("rate", [P, 32])

        def col(at, i=0):
            return params[:, bass.ds(at + i, 1)]

        with nc.Block() as block:
            @block.sync
            def _(sp):
                sp.dma_start(params[:], k.p1).then_inc(s.params, 16)

                def body(i, prev):
                    sp.wait_ge(s.gates, i + 1)
                    sp.dma_start(gate_w[:].rearrange("p b g n -> p (b g n)"),
                                 k.lru_w[bass.ds(i, 1)].rearrange("a p n -> p (a n)")).then_inc(s.weights, 16)
                    for n in range(SLOTS):
                        stream.load(sp, i + 1, n)
                run_passes(sp, LRU_PASSES, body)

            @block.scalar
            def _(act):
                stream.open_act(act)
                act.wait_ge(s.chain, 2)
                act.activation(tmp[1][:], tmp[0][:], ACT.Exp).then_inc(s.exped, 1)
                act.wait_ge(s.cleared, 1)

                def gate_inputs(i):
                    act.wait_ge(s.used, stream.done(i, 3))
                    for b in range(2):
                        act.activation(gsig[:, b], k.z[2 + b][:, 0:T], ACT.Sigmoid).then_inc(s.gsig, 1)

                def inputs(i):
                    act.wait_ge(s.used, stream.done(i, 1))
                    act.wait_ge(s.conv, CONV * i + 1)
                    for b in range(2):
                        act.activation(padded[:, b, 2:2 + T], k.z[b][:, 0:T], ACT.Copy).then_inc(s.ucopied, 1)

                def gates(i):
                    act.wait_ge(s.dsteps, DSTEPS * i + 1)
                    act.wait_ge(s.gates, i + 2)
                    for b in range(2):
                        for d in range(2):
                            act.activation(gate_r[:, b, d], k.aux[2 * b + d][:, 0:T], ACT.Sigmoid,
                                           bias=col(P1_BR + 16 * d + b, 2 * i)).then_inc(s.taken, 1)
                            act.activation(gate_i[:, b, d], k.aux[2 * b + d][:, T:2 * T], ACT.Sigmoid,
                                           bias=col(P1_BI + 16 * d + b, 2 * i)).then_inc(s.taken, 1)

                def tanhs(i):
                    act.wait_ge(s.taken, 8 * i + 9)
                    for b in range(2):
                        for d in range(2):
                            act.activation(tau[:, b, d], gate_r[:, b, d], ACT.Tanh,
                                           scale=scale_t[:, bass.ds(16 * d + b + 2 * i, 1)]).then_inc(s.decay, 1)

                def exps(i):
                    for b in range(2):
                        for d in range(2):
                            act.activation(decay[:, b, d], gate_r[:, b, d], ACT.Exp,
                                           scale=scale_a[:, bass.ds(16 * d + b + 2 * i, 1)]).then_inc(s.decay, 1)
                    act.wait_ge(s.decay, 9 * i + 8)
                    act.activation(tau[:], tau[:], ACT.Sqrt).then_inc(s.decay, 1)

                def round_y(i):
                    act.wait_ge(s.dsteps, DSTEPS * i + DSTEPS + 1)
                    act.activation(k.y_hi[:, bass.ds(2 * i, 2)], y[:], ACT.Copy).then_inc(s.rounded_y, 1)

                def body(i, prev):
                    if prev:
                        gate_inputs(i - 1)
                        gates(i - 1)
                    stream.round(act, i + 1, 0)
                    if prev:
                        tanhs(i - 1)
                    stream.round(act, i + 1, 1)
                    inputs(i)
                    if prev:
                        exps(i - 1)
                    stream.round(act, i + 1, 2)
                    stream.round(act, i + 1, 3)
                    if prev:
                        round_y(i - 1)

                def tail(i):
                    gate_inputs(i)
                    gates(i)
                    tanhs(i)
                    exps(i)
                    round_y(i)
                run_passes(act, LRU_PASSES, body, tail)

            @block.gpsimd
            def _(pool):
                def gated(i, prev=True):
                    for b in range(2):
                        pool.wait_ge(s.taken, 8 * i + 9)
                        u = k.feat[:, bass.ds(2 * i + b, 1)].to_broadcast([P, 2, T])
                        pool.tensor_tensor(gate_i[:, b], gate_i[:, b], u, ALU.mult).then_inc(s.gated, 1)
                run_passes(pool, LRU_PASSES, gated)

            @block.vector
            def _(dve):
                stream.open_dve(dve)
                dve.sem_inc(s.conv, 1)
                dve.sem_inc(s.dsteps, 1)
                dve.memset(padded[:], 0.0).then_inc(s.cleared, 1)
                link = chain(dve, s.chain)
                dve.wait_ge(s.params, 16)
                link(lambda: dve.tensor_scalar(rate[:], params[:, P1_LAM:P1_LAM + 32], -1.0, None, ALU.mult))

                link(lambda: dve.tensor_tensor(tmp[0][:], rate[:], params[:, P1_LAM:P1_LAM + 32], ALU.min))
                dve.wait_ge(s.exped, 1)
                softplus_tail(link, dve, rate[:], tmp[1][:], tmp[0][:], tmp[2][:])
                link(lambda: dve.tensor_scalar(scale_a[:], rate[:], -8.0, None, ALU.mult))
                link(lambda: dve.tensor_scalar(scale_t[:], rate[:], 4.0, None, ALU.mult))

                def convolve(i):
                    dve.wait_ge(s.ucopied, 2 * i + 4)
                    for tap in range(4):
                        for b in range(2):
                            if tap:
                                dve.wait_ge(s.conv, CONV * i + 1 + 2 * (tap - 1) + b + 1)
                            u, x = k.feat[:, bass.ds(2 * i + b, 1)], padded[:, b, tap:tap + T]
                            if tap == 0:
                                ins = dve.tensor_scalar(u, x[:, None], col(P1_CONV + b, 2 * i), col(P1_CONVB + b, 2 * i),
                                                        ALU.mult, ALU.add)
                            else:
                                ins = dve.scalar_tensor_tensor(out=u, in0=x[:, None], scalar=col(P1_CONV + 16 * tap + b, 2 * i),
                                                               in1=u, op0=ALU.mult, op1=ALU.add)
                            ins.then_inc(s.conv, 1)

                def open_gates(i):
                    dve.wait_ge(s.gsig, 2 * i + 2)
                    for b in range(2):
                        dve.tensor_tensor(g_all[:, bass.ds(2 * i + b, 1)], k.z[2 + b][:, None, 0:T], gsig[:, b:b + 1],
                                          ALU.mult).then_inc(s.zcopied, 1)

                def scan(i):
                    def step(n):
                        dve.wait_ge(s.dsteps, DSTEPS * i + n + 1)
                    dve.wait_ge(s.decay, 9 * i + 9)
                    dve.scalar_tensor_tensor(out=tau[:], in0=decay[:], scalar=1.0, in1=tau[:], op0=ALU.add,
                                             op1=ALU.mult).then_inc(s.dsteps, 1)
                    step(1)
                    dve.wait_ge(s.gated, 2 * i + 2)
                    dve.tensor_tensor(tau[:], tau[:], gate_i[:], ALU.mult).then_inc(s.dsteps, 1)
                    step(2)
                    for b in range(2):
                        dve.tensor_tensor_scan(gate_r[:, b, 0], decay[:, b, 0], tau[:, b, 0], 0.0, ALU.mult,
                                               ALU.add).then_inc(s.dsteps, 1)
                        dve.tensor_tensor_scan(gate_r[:, b, 1, ::-1], decay[:, b, 1, ::-1], tau[:, b, 1, ::-1], 0.0,
                                               ALU.mult, ALU.add).then_inc(s.dsteps, 1)

                def outputs(i):
                    dve.wait_ge(s.dsteps, DSTEPS * i + 7)
                    dve.tensor_tensor(gate_r[:, :, 0], gate_r[:, :, 0], gate_r[:, :, 1], ALU.add).then_inc(s.dsteps, 1)
                    dve.wait_ge(s.dsteps, DSTEPS * i + 8)
                    dve.tensor_tensor(y[:], gate_r[:, :, 0], g_all[:, bass.ds(2 * i, 2)], ALU.mult).then_inc(s.dsteps, 1)

                def split_y(i):
                    dve.wait_ge(s.rounded_y, i + 1)
                    dve.tensor_tensor(k.y_lo[:, bass.ds(2 * i, 2)], y[:], k.y_hi[:, bass.ds(2 * i, 2)].bitcast(F32),
                                      ALU.subtract).then_inc(s.ydone, 1)
                    dve.wait_ge(s.ydone, i + 1)

                def body(i, prev):
                    if prev:
                        open_gates(i - 1)
                    stream.residual(dve, i + 1, 0)
                    stream.residual(dve, i + 1, 1)
                    convolve(i)
                    if prev:
                        scan(i - 1)
                    stream.residual(dve, i + 1, 2)
                    if prev:
                        outputs(i - 1)
                    stream.residual(dve, i + 1, 3)
                    if prev:
                        split_y(i - 1)

                def tail(i):
                    open_gates(i)
                    scan(i)
                    outputs(i)
                    split_y(i)
                run_passes(dve, LRU_PASSES, body, tail)

            @block.tensor
            def _(pe):
                stream.open_pe(pe)
                pe.sem_inc(s.gates, 1)
                pe.sem_inc(s.ucopied, 2)
                pe.sem_inc(s.zcopied, 2)
                pe.sem_inc(s.taken, 1)

                def products(i):
                    pe.wait_ge(s.ucopied, 2 * i + 2)
                    for sl in (0, 1):
                        stream.multiply(pe, i, sl, k.xn_hi, k.xn_lo)
                    pe.wait_ge(s.zcopied, 2 * i + 2)
                    for sl in (2, 3):
                        stream.multiply(pe, i, sl, k.xn_hi, k.xn_lo)

                def gates(i):
                    pe.wait_ge(s.conv, CONV * i + 1 + CONV)
                    pe.wait_ge(s.weights, 16 * i + 16)
                    pe.wait_ge(s.taken, 8 * i + 1)
                    for b in range(2):
                        for d in range(2):
                            for g in range(2):
                                ins = pe.matmul(k.aux[2 * b + d][:, g * T:g * T + T], gate_w[:, b, 2 * d + g],
                                                k.feat[:, bass.ds(2 * i + b, 1)], start=True, stop=True)
                    ins.then_inc(s.gates, 1)

                def body(i, prev):
                    products(i)
                    gates(i)
                run_passes(pe, LRU_PASSES, body)


ROPE = "rope_in counted chain looked "


class RopeTables:

    def __init__(self, k, s, positions, freq):
        self.k, self.s, self.positions, self.freq = k, s, positions, freq
        self.pos_i = s.sbuf("pos_i", [P, T], I32)
        self.angle, self.turns, self.rest = (s.sbuf(n, [P, T]) for n in ("angle", "turns", "rest"))
        self.f = s.sbuf("f", [P, 2])

    def load(self, sp):
        sp.dma_start(self.f[:], constant(self.k, self.freq)).then_inc(self.s.rope_in, 16)
        if self.positions is not None:
            sp.dma_start(self.pos_i[:], self.positions.to_broadcast([P, T])).then_inc(self.s.rope_in, 16)

    def count(self, pool):
        if self.positions is None:
            pool.iota(self.pos_i[:], [[1, T]], base=0, channel_multiplier=0).then_inc(self.s.counted, 1)

    def reduce(self, dve):
        s, angle, turns, rest = self.s, self.angle, self.turns, self.rest
        turn_parts = (6.28125, 0.0019350051879882812)
        turn_parts = turn_parts + (2 * math.pi - sum(turn_parts),)
        magic = 1.5 * 2.0 ** 23
        link = chain(dve, s.chain)
        if self.positions is None:
            dve.wait_ge(s.counted, 1)
            dve.wait_ge(s.rope_in, 16)
        else:
            dve.wait_ge(s.rope_in, 32)
        link(lambda: dve.tensor_copy(angle[:], self.pos_i[:]))
        link(lambda: dve.tensor_scalar(angle[:], angle[:], self.f[:, 0:1], None, ALU.mult))
        for n, quarter in enumerate((0.0, 0.25)):
            if n:
                dve.wait_ge(s.looked, 1)
            link(lambda: dve.tensor_scalar(turns[:], angle[:], 0.5 / math.pi, quarter, ALU.mult, ALU.add))
            link(lambda: dve.tensor_scalar(turns[:], turns[:], magic, None, ALU.add))
            link(lambda: dve.tensor_scalar(turns[:], turns[:], -magic, None, ALU.add))
            for m, part in enumerate(turn_parts):
                link(lambda: dve.scalar_tensor_tensor(out=rest[:], in0=turns[:], scalar=-part,
                                                      in1=rest[:] if m else angle[:], op0=ALU.mult, op1=ALU.add))
            link(lambda: dve.tensor_scalar(rest[:], rest[:], quarter * 2 * math.pi, 3.1415925, ALU.add, ALU.min))
            link(lambda: dve.tensor_scalar(rest[:], rest[:], -3.1415925, None, ALU.max))

    def look_up(self, act):
        for n, table in enumerate((self.k.sin_t, self.k.cos_t)):
            act.wait_ge(self.s.chain, 2 + 8 * (n + 1))
            act.activation(table[:], self.rest[:], ACT.Sin).then_inc(self.s.looked, 1)


def merge_phase(k, name, first_slot, y_first, positions, freq):
    nc = k.nc
    with phase(nc, name, STREAM + ROPE + "gsig taken steps") as s:
        stream = Stream(k, s, first_slot)
        rope = RopeTables(k, s, positions, freq)
        gate, part = s.sbuf("gate", [P, 2, T]), s.sbuf("part", [P, 2, T])
        with nc.Block() as block:
            @block.sync
            def _(sp):
                rope.load(sp)
                stream.loads(sp, KT // 2)

            @block.gpsimd
            def _(pool):
                rope.count(pool)

            @block.scalar
            def _(act):
                stream.open_act(act)
                rope.look_up(act)

                def body(i, prev):
                    stream.round(act, i + 1, 0)
                    stream.round(act, i + 1, 1)
                    act.wait_ge(s.used, stream.done(i, 1))
                    act.wait_ge(s.taken, 2 * i + 2)
                    for b in range(2):
                        act.activation(gate[:, b], k.z[b][:, 0:T], ACT.Sigmoid).then_inc(s.gsig, 1)
                    stream.round(act, i + 1, 2)
                    stream.round(act, i + 1, 3)
                run_passes(act, KT // 2, body)

            @block.vector
            def _(dve):
                stream.open_dve(dve)
                dve.sem_inc(s.taken, 2)
                rope.reduce(dve)

                def merge(i):
                    dve.wait_ge(s.gsig, 2 * i + 4)
                    dve.wait_ge(s.used, stream.done(i, 3))
                    out = k.feat[:, bass.ds(2 * i, 2)] if y_first else part[:]
                    for b in range(2):
                        o = k.feat[:, bass.ds(2 * i + b, 1)] if y_first else part[:, b:b + 1]
                        dve.tensor_tensor(o, k.z[2 + b][:, None, 0:T], gate[:, b:b + 1], ALU.mult).then_inc(s.taken, 1)
                    if not y_first:
                        dve.wait_ge(s.taken, 2 * i + 4)
                        f = k.feat[:, bass.ds(2 * i, 2)]
                        dve.tensor_tensor(f, f, part[:], ALU.add).then_inc(s.steps, 1)
                        dve.wait_ge(s.steps, i + 1)

                def body(i, prev):
                    if prev:
                        merge(i - 1)
                    for n in range(SLOTS):
                        stream.residual(dve, i + 1, n)
                run_passes(dve, KT // 2, body, merge)

            @block.tensor
            def _(pe):
                stream.open_pe(pe)
                pe.sem_inc(s.gsig, 2)

                def products(i):
                    pe.wait_ge(s.gsig, 2 * i + 2)
                    for sl in (0, 1):
                        stream.multiply(pe, i, sl, k.xn_hi, k.xn_lo)
                    pe.wait_ge(s.taken, 2 * i + 2)
                    for sl in (2, 3):
                        stream.multiply(pe, i, sl, k.y_hi, k.y_lo)
                run_passes(pe, KT // 2, lambda i, prev: products(i))


def attention_phase(k, name, a):
    nc = k.nc
    heads = a.heads_per_tile
    pairs = heads
    M = 12
    R = 4 if heads == 2 else 3
    C = 4 if heads == 2 else 2
    KV_PASSES = 2 // heads
    G0 = 2 if heads == 1 else 1
    K_STEPS = 6 if heads == 1 else R + 8
    MIXED = 1 if heads == 1 else 0
    with phase(nc, name, STREAM + "consts ready kcopied kturned ksteps vcopied vcur qcopied turned rope "
               "rstd gated scores soft exped flipped fcopied mixed ysteps yrounded") as s:
        stream = Stream(k, s, a.first_slot)
        turn = s.sbuf("turn", [P, P])
        mask = s.sbuf("mask", [P, 2, T])
        sinks, sink_row = s.sbuf("sinks", [P, a.n_heads, 2]), s.sbuf("sink_row", [P, a.n_heads])
        norms = s.sbuf("norms", [P, 2])
        keys = s.sbuf("keys", [P, 4, T])
        values = s.sbuf("values", [P, 2, a.kv_width])
        values_now = s.sbuf("values_now", [P, 2, P]) if heads == 1 else None
        q_raw, q_sq, q_rot, part = (s.sbuf(n, [P, 2, T]) for n in ("q_raw", "q_sq", "q_rot", "part"))
        k_raw = s.sbuf("k_raw", [P, 4, T]) if heads == 1 else q_raw
        rstd = s.sbuf("rstd", [P, 2, T]) if heads == 2 else None
        gate = s.sbuf("gate", [P, 2, T])
        if heads == 1:
            S, W = [s.sbuf("S0", [P, 2, 2, T])[:]], [s.sbuf("W0", [P, 2, 2, T])[:]]
        else:
            part4 = [k.feat[:, 4 * n:4 * n + 4].rearrange("p (h b) t -> p h b t", h=2) for n in range(4)]
            S, W = part4[0:2], part4[2:4]
        small = [s.sbuf(f"small{p}", [P, 6, 4]) for p in range(pairs)]
        y = s.sbuf("y", [P, 2, T])
        cos_b = k.cos_t[:, None, :].to_broadcast([P, 2, T])
        sin_b = k.sin_t[:, None, :].to_broadcast([P, 2, T])

        def both(bank):
            return bank[:, 0:2 * T].rearrange("p (b t) -> p b t", b=2)

        def kv_of(i, p, h):
            return i // 2 if heads == 1 else (4 * i + 2 * p + h) // 3

        with nc.Block() as block:
            @block.sync
            def _(sp):
                sp.dma_start(turn[:], constant(k, a.turn)).then_inc(s.consts, 16)
                sp.dma_start(mask[:].rearrange("p b t -> p (b t)"), constant(k, a.mask)).then_inc(s.consts, 16)
                sp.dma_start(sink_row[:], a.sinks.to_broadcast([P, a.n_heads])).then_inc(s.consts, 16)
                if a.norms is not None:
                    sp.dma_start(norms[:], a.norms).then_inc(s.consts, 16)
                stream.loads(sp, G0 + a.passes)

            consts_in = 48 if a.norms is None else 64

            @block.gpsimd
            def _(pool):
                if heads == 1:
                    pool.wait_ge(s.vcopied, 4)

                    def values_here(i, prev):
                        pool.wait_ge(s.mixed, i + 1)
                        pool.tensor_copy(values_now[:], values[:, :, bass.ds((i // 2) * P, P)]).then_inc(s.vcur, 1)
                    run_passes(pool, a.passes, values_here)

            @block.scalar
            def _(act):
                stream.open_act(act)
                stream.round(act, 1, 0)
                stream.round(act, 1, 1)
                if heads == 1:
                    for t in range(4):
                        if t == 2:
                            stream.round(act, 1, 2)
                            stream.round(act, 1, 3)
                        act.wait_ge(s.used, stream.done(0, 2 * (t // 2) + 1))
                        act.activation(k_raw[:, t], k.z[t][:, 0:T], ACT.Copy).then_inc(s.kcopied, 1)
                    for n in range(4):
                        if n % 2 == 0:
                            stream.round(act, 2, n)
                            stream.round(act, 2, n + 1)
                        act.wait_ge(s.used, stream.done(1, 2 * (n // 2) + 1))
                        act.activation(values[:, n % 2, T * (n // 2):T * (n // 2) + T], k.z[n][:, 0:T], ACT.Copy)\
                           .then_inc(s.vcopied, 1)
                else:
                    act.wait_ge(s.consts, consts_in)
                    act.wait_ge(s.used, stream.done(0, 1))
                    for t in range(2):
                        act.activation(k_raw[:, t], k.z[t][:, 0:T], ACT.Copy, scale=norms[:, 1:2]).then_inc(s.kcopied, 1)
                        act.activation(q_sq[:, t], k.z[t][:, 0:T], ACT.Square).then_inc(s.kcopied, 1)
                    stream.round(act, 1, 2)
                    stream.round(act, 1, 3)
                    act.wait_ge(s.used, stream.done(0, 3))
                    for n in range(2):
                        act.activation(values[:, n, 0:T], k.z[2 + n][:, 0:T], ACT.Copy).then_inc(s.vcopied, 1)
                    act.wait_ge(s.kturned, 2)
                    inverse_root(act, k, rstd[:], both(k.aux[1]), 1.0 / HEAD_DIM_2, s.rstd, 0)

                def exps(i, p):
                    u = pairs * i + p
                    act.wait_ge(s.soft, M * u + 5)
                    for h in range(2):
                        for b in range(2):
                            c = 2 * h + b
                            act.activation(S[p][:, h, b], S[p][:, h, b], ACT.Exp, bias=small[p][:, 1, c:c + 1],
                                           accum_out=small[p][:, 3, c:c + 1]).then_inc(s.exped, 1)
                    act.wait_ge(s.soft, M * u + 6)
                    act.activation(small[p][:, 4], small[p][:, 2], ACT.Exp).then_inc(s.exped, 1)

                def copy_weights(i, p):
                    u = pairs * i + p
                    act.wait_ge(s.flipped, u + 1)
                    for h in range(2):
                        act.activation(W[p][:, h], both(k.aux[2 * p + h]), ACT.Copy).then_inc(s.fcopied, 1)

                def round_y(i, p):
                    u = pairs * i + p
                    act.wait_ge(s.ysteps, 2 * u + 1)
                    if heads == 1:
                        act.activation(k.y_hi[:, bass.ds(2 * i, 2)], y[:], ACT.Copy).then_inc(s.yrounded, 1)
                    else:
                        act.activation(k.y_hi[:, 2 * i + p], y[:, 0], ACT.Copy).then_inc(s.yrounded, 1)

                def body(i, prev):
                    g = i + G0
                    if prev:
                        act.wait_ge(s.used, stream.done(g - 1, 3))
                        for b in range(2):
                            act.activation(gate[:, b], k.z[2 + b][:, 0:T], ACT.Silu).then_inc(s.gated, 1)
                        exps(i - 1, 0)
                    stream.round(act, g + 1, 0)
                    stream.round(act, g + 1, 1)
                    act.wait_ge(s.used, stream.done(g, 1))
                    if prev:
                        act.wait_ge(s.rope, R * i)
                    elif heads == 2:
                        act.wait_ge(s.ksteps, K_STEPS)
                    for t in range(2):
                        if heads == 2:
                            act.activation(q_raw[:, t], k.z[t][:, 0:T], ACT.Copy, scale=norms[:, 0:1]).then_inc(s.qcopied, 1)
                            act.activation(q_sq[:, t], k.z[t][:, 0:T], ACT.Square).then_inc(s.qcopied, 1)
                        else:
                            act.activation(q_raw[:, t], k.z[t][:, 0:T], ACT.Copy).then_inc(s.qcopied, 1)
                    if prev:
                        copy_weights(i - 1, 0)
                    if prev and pairs == 2:
                        exps(i - 1, 1)
                    if heads == 2:
                        act.wait_ge(s.turned, i + 1)
                        inverse_root(act, k, rstd[:], both(k.z[1]), 1.0 / HEAD_DIM_2, s.rstd, 2 * i + 2)
                    stream.round(act, g + 1, 2)
                    if prev:
                        round_y(i - 1, 0)
                    if prev and pairs == 2:
                        copy_weights(i - 1, 1)
                    stream.round(act, g + 1, 3)
                    if prev and pairs == 2:
                        round_y(i - 1, 1)

                def tail(i):
                    act.wait_ge(s.used, stream.done(i + G0, 3))
                    for b in range(2):
                        act.activation(gate[:, b], k.z[2 + b][:, 0:T], ACT.Silu).then_inc(s.gated, 1)
                    for p in range(pairs):
                        exps(i, p)
                    for p in range(pairs):
                        copy_weights(i, p)
                        round_y(i, p)
                run_passes(act, a.passes, body, tail)

            @block.vector
            def _(dve):
                stream.open_dve(dve)
                for n in range(SLOTS):
                    stream.residual(dve, 1, n)
                dve.wait_ge(s.consts, consts_in)
                for b in range(2):
                    dve.tensor_copy(sinks[:, :, b], sink_row[:]).then_inc(s.ready, 1)

                def rotate(bank, turned, rooted, sem, base, raw, out):
                    dve.wait_ge(*turned)
                    after(dve, sem, base)
                    dve.tensor_tensor(part[:], raw, cos_b, ALU.mult).then_inc(sem, 1)
                    dve.tensor_tensor(out, both(bank), sin_b, ALU.mult).then_inc(sem, 1)
                    dve.wait_ge(sem, base + 2)
                    dve.tensor_tensor(out, out, part[:], ALU.add).then_inc(sem, 1)
                    if heads == 2:
                        dve.wait_ge(*rooted)
                        dve.wait_ge(sem, base + 3)
                        dve.tensor_tensor(out, out, rstd[:], ALU.mult).then_inc(sem, 1)

                if heads == 1:
                    for h in range(2):
                        rotate(k.aux[h], (s.kturned, h + 1), None, s.ksteps, R * h,
                               k_raw[:, 2 * h:2 * h + 2], keys[:, 2 * h:2 * h + 2])
                else:
                    rotate(k.aux[0], (s.kturned, 1), (s.rstd, 2), s.ksteps, 0, k_raw[:], q_rot[:])
                    dve.wait_ge(s.ksteps, R)
                    for kv in range(4):
                        half = (kv % 2) * 64
                        for to in (0, 64):
                            dve.tensor_copy(keys[to:to + 64, kv], q_rot[half:half + 64, kv // 2]).then_inc(s.ksteps, 1)
                if heads == 1:
                    for n in range(SLOTS):
                        stream.residual(dve, 2, n)

                def soften(i, p):
                    u = pairs * i + p
                    dve.wait_ge(s.scores, u + 1)
                    for h in range(2):
                        dve.scalar_tensor_tensor(out=S[p][:, h], in0=both(k.aux[2 * p + h]), scalar=a.scale, in1=mask[:],
                                                 op0=ALU.mult, op1=ALU.add).then_inc(s.soft, 1)
                    dve.wait_ge(s.soft, M * u + 2)
                    m = small[p]
                    dve.tensor_reduce(m[:, 0], S[p].rearrange("p h b t -> p (h b) t"), AX_X, ALU.max).then_inc(s.soft, 1)
                    dve.wait_ge(s.soft, M * u + 3)
                    sink = sinks[:, bass.ds(2 * u, 2)].rearrange("p h b -> p (h b)")
                    dve.tensor_tensor(m[:, 0], m[:, 0], sink, ALU.max).then_inc(s.soft, 1)
                    dve.wait_ge(s.soft, M * u + 4)
                    dve.tensor_scalar(m[:, 1], m[:, 0], -1.0, None, ALU.mult).then_inc(s.soft, 1)
                    dve.wait_ge(s.soft, M * u + 5)
                    dve.tensor_tensor(m[:, 2], m[:, 1], sink, ALU.add).then_inc(s.soft, 1)

                def normalise(i, p):
                    u = pairs * i + p
                    m = small[p]
                    dve.wait_ge(s.exped, 5 * u + 5)
                    dve.tensor_tensor(m[:, 5], m[:, 3], m[:, 4], ALU.add).then_inc(s.soft, 1)
                    dve.wait_ge(s.soft, M * u + 7)
                    dve.reciprocal(m[:, 0], m[:, 5]).then_inc(s.soft, 1)
                    dve.wait_ge(s.soft, M * u + 8)
                    for h in range(2):
                        for b in range(2):
                            c = 2 * h + b
                            dve.tensor_scalar(S[p][:, h, b], S[p][:, h, b], m[:, 0, c:c + 1], None, ALU.mult)\
                               .then_inc(s.soft, 1)

                def outputs(i, p):
                    u = pairs * i + p
                    dve.wait_ge(s.mixed, u + 1 + MIXED)
                    dve.wait_ge(s.gated, 2 * i + 2)
                    if heads == 1:
                        dve.tensor_tensor(y[:], both(k.aux[0]), gate[:], ALU.mult).then_inc(s.ysteps, 1)
                    else:
                        dve.tensor_tensor(y[:, 0], k.aux[2 * p][:, 0:T], gate[:, p], ALU.mult).then_inc(s.ysteps, 1)

                def split_outputs(i, p):
                    u = pairs * i + p
                    if heads == 1:
                        hi, lo, v = k.y_hi[:, bass.ds(2 * i, 2)], k.y_lo[:, bass.ds(2 * i, 2)], y[:]
                    else:
                        hi, lo, v = k.y_hi[:, 2 * i + p], k.y_lo[:, 2 * i + p], y[:, 0]
                    dve.wait_ge(s.yrounded, u + 1)
                    dve.tensor_tensor(lo, v, hi.bitcast(F32), ALU.subtract).then_inc(s.ysteps, 1)
                    dve.wait_ge(s.ysteps, 2 * u + 2)

                def body(i, prev):
                    g = i + G0
                    if prev:
                        soften(i - 1, 0)
                        normalise(i - 1, 0)
                    stream.residual(dve, g + 1, 0)
                    if prev and pairs == 2:
                        soften(i - 1, 1)
                    stream.residual(dve, g + 1, 1)
                    if prev and pairs == 2:
                        normalise(i - 1, 1)
                    if not prev:
                        dve.wait_ge(s.ksteps, K_STEPS)
                    rotate(k.z[0], (s.turned, i + 1), (s.rstd, 2 * i + 4), s.rope, R * i,
                           q_raw[:], q_rot[:])
                    if prev:
                        outputs(i - 1, 0)
                    stream.residual(dve, g + 1, 2)
                    if prev:
                        split_outputs(i - 1, 0)
                    stream.residual(dve, g + 1, 3)
                    if prev and pairs == 2:
                        outputs(i - 1, 1)
                        split_outputs(i - 1, 1)

                def tail(i):
                    for p in range(pairs):
                        soften(i, p)
                        normalise(i, p)
                    for p in range(pairs):
                        outputs(i, p)
                        split_outputs(i, p)
                run_passes(dve, a.passes, body, tail)

            @block.tensor
            def _(pe):
                stream.open_pe(pe)
                if heads == 1:
                    pe.sem_inc(s.mixed, 1)
                for sl in range(4):
                    stream.multiply(pe, 0, sl, k.xn_hi, k.xn_lo, tokens_out=heads == 2 and sl >= 2)
                pe.wait_ge(s.consts, consts_in)
                if heads == 1:
                    for h in range(2):
                        pe.wait_ge(s.kcopied, 2 * h + 2)
                        pe.matmul(k.aux[h][:, 0:2 * T], turn[:], k_raw[:, 2 * h:2 * h + 2], start=True, stop=True)\
                          .then_inc(s.kturned, 1)
                    pe.wait_ge(s.kcopied, 4)
                    for sl in range(4):
                        stream.multiply(pe, 1, sl, k.xn_hi, k.xn_lo, tokens_out=True)
                else:
                    pe.wait_ge(s.kcopied, 4)
                    pe.matmul(k.aux[0][:, 0:2 * T], turn[:], k_raw[:], start=True, stop=True).then_inc(s.kturned, 1)
                    pe.matmul(k.aux[1][:, 0:2 * T], k.blocks[:], q_sq[:], start=True, stop=True).then_inc(s.kturned, 1)

                def scores(i, p):
                    for h in range(2):
                        kv = kv_of(i, p, h)
                        for b in range(2):
                            out = k.aux[2 * p + h][:, b * T:b * T + T]
                            if heads == 1:
                                q, key = q_rot[:, h, P * b:P * b + P], keys[:, bass.ds(kv, 1)]
                            else:
                                lo = 64 * h
                                q, key = q_rot[lo:lo + 64, p, P * b:P * b + P], keys[lo:lo + 64, kv]
                            ins = pe.matmul(out, q, key, start=True, stop=True)
                    ins.then_inc(s.scores, 1)

                def flip(i, p):
                    u = pairs * i + p
                    pe.wait_ge(s.soft, M * u + 12)
                    for h in range(2):
                        for b in range(2):
                            for kb in range(2):
                                ins = pe.transpose(k.aux[2 * p + h][:, kb * T + b * P:kb * T + b * P + P],
                                                   S[p][:, h, b, kb * P:kb * P + P], k.ident[:])
                    ins.then_inc(s.flipped, 1)

                def mix(i, p):
                    u = pairs * i + p
                    pe.wait_ge(s.fcopied, 2 * u + 2)
                    if heads == 1:
                        pe.wait_ge(s.vcur, i + 1)
                    for h in range(2):
                        for kb in range(2):
                            if heads == 1:
                                out, v = k.aux[0][:, h * T:h * T + T], values_now[:, kb]
                            else:
                                at = 64 * kv_of(i, p, h)
                                out, v = k.aux[2 * p][64 * h:64 * h + 64, 0:T], values[:, kb, at:at + 64]
                            ins = pe.matmul(out, v, W[p][:, h, kb], start=kb == 0, stop=kb == 1)
                    ins.then_inc(s.mixed, 1)

                def body(i, prev):
                    g = i + G0
                    if prev:
                        pe.wait_ge(s.rope, R * i)
                    elif heads == 1:
                        pe.wait_ge(s.vcopied, 2)
                    stream.multiply(pe, g, 0, k.xn_hi, k.xn_lo)
                    if prev and pairs == 2:
                        if i >= 2:
                            pe.wait_ge(s.ysteps, 2 * pairs * (i - 1))
                        scores(i - 1, 1)
                    stream.multiply(pe, g, 1, k.xn_hi, k.xn_lo)
                    if prev:
                        flip(i - 1, 0)
                        pe.wait_ge(s.gated, 2 * i)
                    else:
                        pe.wait_ge(s.vcopied, 4 // heads)
                    stream.multiply(pe, g, 2, k.xn_hi, k.xn_lo)
                    if prev:
                        mix(i - 1, 0)
                        if pairs == 2:
                            flip(i - 1, 1)
                    pe.wait_ge(s.qcopied, C * i + C)
                    ins = pe.matmul(k.z[0][:, 0:2 * T], turn[:], q_raw[:], start=True, stop=True)
                    if heads == 2:
                        ins = pe.matmul(k.z[1][:, 0:2 * T], k.blocks[:], q_sq[:], start=True, stop=True)
                    ins.then_inc(s.turned, 1)
                    stream.multiply(pe, g, 3, k.xn_hi, k.xn_lo)
                    if prev and pairs == 2:
                        mix(i - 1, 1)
                    if prev:
                        pe.wait_ge(s.ysteps, 2 * pairs * (i - 1) + 1)
                    else:
                        pe.wait_ge(s.ksteps, K_STEPS)
                    pe.wait_ge(s.rope, R * i + R)
                    scores(i, 0)

                def tail(i):
                    if pairs == 2:
                        pe.wait_ge(s.ysteps, 2 * pairs * i)
                        scores(i, 1)
                    for p in range(pairs):
                        flip(i, p)
                    for p in range(pairs):
                        mix(i, p)
                run_passes(pe, a.passes, body, tail)


def tap_steps(dve, taps, start, params, padded, acc, first, last):
    for n in range(first, last):
        for b in range(2):
            tile = start + b
            w = P2_BCONV + B_TILES * n + tile
            if n == 0:
                dve.tensor_scalar(acc[:, tile], padded[:, tile, 0:T], params[:, w:w + 1],
                                  params[:, P2_BCONVB + tile:P2_BCONVB + tile + 1], ALU.mult, ALU.add).then_inc(taps, 1)
            else:
                dve.wait_ge(taps, 2 * n + b - 1)
                dve.scalar_tensor_tensor(out=acc[:, tile], in0=padded[:, tile, n:n + T], scalar=params[:, w:w + 1],
                                         in1=acc[:, tile], op0=ALU.mult, op1=ALU.add).then_inc(taps, 1)


def conv_phase(k, layer, conv):
    nc = k.nc
    B = B_TILES
    with phase(nc, "conv", STREAM + "params cleared acopied gsig gated zgated taps") as s:
        stream = Stream(k, s, layer * SLOTS_2 + SLOTS_1 + SLOT_CONV_2)
        params = s.sbuf("params", [P, P2_COLS])
        a_now, gsig = s.sbuf("a_now", [P, 2, T]), s.sbuf("gsig", [P, 2, T])
        padded, zgate, acc = conv.padded, conv.zgate, k.feat[:, KT - B:KT]

        with nc.Block() as block:
            @block.sync
            def _(sp):
                sp.dma_start(params[:], k.p2[bass.ds(layer, 1)].rearrange("a p n -> p (a n)")).then_inc(s.params, 16)
                stream.loads(sp, 3)

            @block.scalar
            def _(act):
                stream.open_act(act)
                for i in range(3):
                    stream.round(act, i + 1, 0)
                    stream.round(act, i + 1, 1)
                    act.wait_ge(s.used, stream.done(i, 1))
                    for b in range(2):
                        if i < 2:
                            if i:
                                act.wait_ge(s.gated, 2)
                            act.activation(a_now[:, b], k.z[b][:, 0:T], ACT.Copy).then_inc(s.acopied, 1)
                        else:
                            act.activation(zgate[:, b], k.z[b][:, 0:T], ACT.Silu).then_inc(s.zgated, 1)
                    stream.round(act, i + 1, 2)
                    stream.round(act, i + 1, 3)
                    act.wait_ge(s.used, stream.done(i, 3))
                    for b in range(2):
                        if i < 2:
                            act.activation(gsig[:, b], k.z[2 + b][:, 0:T], ACT.Sigmoid).then_inc(s.gsig, 1)
                        else:
                            act.activation(zgate[:, 2 + b], k.z[2 + b][:, 0:T], ACT.Silu).then_inc(s.zgated, 1)

            @block.vector
            def _(dve):
                stream.open_dve(dve)
                dve.memset(padded[:], 0.0).then_inc(s.cleared, 1)
                dve.wait_ge(s.cleared, 1)
                dve.wait_ge(s.params, 16)
                for i in range(3):
                    if i >= 1:
                        dve.wait_ge(s.acopied, 2 * i)
                        dve.wait_ge(s.gsig, 2 * i)
                        for b in range(2):
                            dve.tensor_tensor(padded[:, 2 * i - 2 + b, TAPS_B - 1:TAPS_B - 1 + T], a_now[:, b], gsig[:, b],
                                              ALU.mult).then_inc(s.gated, 1)
                    for n in range(SLOTS):
                        stream.residual(dve, i + 1, n)
                        if i >= 1:
                            m = SLOTS * (i - 1) + n
                            if m == 0:
                                dve.wait_ge(s.gated, 2)
                            tap_steps(dve, s.taps, 0, params, padded, acc, 4 * m, min(4 * m + 4, TAPS_B))

            @block.tensor
            def _(pe):
                stream.open_pe(pe)
                for i in range(3):
                    for sl in range(4):
                        if i and sl == 0:
                            pe.wait_ge(s.acopied, 2 * i)
                        if i and sl == 2:
                            pe.wait_ge(s.gsig, 2 * i)
                        stream.multiply(pe, i, sl, k.xn_hi, k.xn_lo)


def delta_inputs_phase(k, layer, keep, branch):
    nc = k.nc
    H = C_HEADS
    PAD = TAPS_C - 1
    with phase(nc, "din", STREAM + "params w12 rows cleared copied conv qkv squared summed std norm split12 rounded12 "
               "bg chain exped negexp taps pw bsummed centred bsquared bsquares bstd bln lsig hid mixed bsteps byrounded bylo") as s:
        stream = Stream(k, s, layer * SLOTS_2 + SLOTS_1 + SLOT_DELTA_2)
        params = s.sbuf("params", [P, P2_COLS])
        w12_lo = s.sbuf("w12_lo", [P, KT, 2 * H], F32R)
        w12_hi = s.sbuf("w12_hi", [P, KT, 2 * H], F32R)
        rows = s.sbuf("rows", [P, 2, H])
        padded = s.sbuf("padded", [P, 3, PAD + T])
        conv, sig = s.sbuf("conv", [P, 3, T]), s.sbuf("sig", [P, 3, T])
        std = s.sbuf("std", [P, 2, T])
        sq = sig[:, 0:2]
        B = B_TILES
        pw = s.sbuf("pw", [P, B, B * P])
        acc = k.feat[:, KT - B:KT]
        bstd = s.sbuf("bstd", [P, T])
        wide = branch.padded[:, :, 0:T]
        TAP_PASSES = H - 1
        TAPS = (TAPS_B - 1) // TAP_PASSES

        def bcol(at):
            return params[:, at:at + 1]
        w12 = std[:].rearrange("p a t -> p (a t)")[:, 0:KT * 2 * H].rearrange("p (k n) -> p k n", k=KT)
        x, t0, t1 = (conv[:, n, 0:2 * H].rearrange("p (b h) -> p b h", b=2) for n in range(3))
        t2 = conv[:, 0, 2 * H:4 * H].rearrange("p (b h) -> p b h", b=2)

        with nc.Block() as block:
            @block.sync
            def _(sp):
                sp.dma_start(params[:], k.p2[bass.ds(layer, 1)].rearrange("a p n -> p (a n)")).then_inc(s.params, 16)
                sp.dma_start(w12.rearrange("p k n -> p (k n)"), k.w12[bass.ds(layer, 1)].rearrange("a p n -> p (a n)"))\
                  .then_inc(s.w12, 16)
                sp.dma_start(rows[:].rearrange("p a n -> p (a n)"), k.rows_c[bass.ds(layer, 1)].to_broadcast([P, 2 * H]))\
                  .then_inc(s.rows, 16)
                sp.dma_start(pw[:].rearrange("p a n -> p (a n)"), k.pw[bass.ds(layer, 1)].rearrange("a p n -> p (a n)"))\
                  .then_inc(s.pw, 16)
                stream.loads(sp, H)

            @block.scalar
            def _(act):
                stream.open_act(act)
                act.wait_ge(s.w12, 16)
                act.activation(w12_hi[:], w12, ACT.Copy).then_inc(s.rounded12, 1)
                act.wait_ge(s.rows, 16)
                act.activation(rows[:, 0], rows[:, 0], ACT.Exp).then_inc(s.negexp, 1)
                act.wait_ge(s.cleared, 1)

                def gates():
                    act.wait_ge(s.bg, 1)
                    for b in range(2):
                        act.activation(keep.beta[:, b], k.aux[1][:, 16 * b:16 * b + H], ACT.Sigmoid).then_inc(s.exped, 1)
                    act.wait_ge(s.chain, 4)
                    act.activation(t1, t0, ACT.Exp).then_inc(s.exped, 1)

                def inputs(i):
                    act.wait_ge(s.used, stream.done(i, 1))
                    act.wait_ge(s.conv, 12 * i + 1)
                    for t in range(2):
                        act.activation(padded[:, t, PAD:PAD + T], k.z[t][:, 0:T], ACT.Copy).then_inc(s.copied, 1)

                def inputs_2(i):
                    act.wait_ge(s.used, stream.done(i, 3))
                    act.activation(padded[:, 2, PAD:PAD + T], k.z[2][:, 0:T], ACT.Copy).then_inc(s.copied, 1)
                    act.activation(keep.z_all[:, bass.ds(i, 1)], k.z[3][:, None, 0:T], ACT.Silu).then_inc(s.copied, 1)

                def await_convolution(i):
                    act.wait_ge(s.conv, 12 * i + 13)

                def silu(i):
                    act.activation(k.feat[:, bass.ds(2 * i, 2)], conv[:, 0:2], ACT.Silu).then_inc(s.qkv, 1)
                    act.activation(keep.v_all[:, bass.ds(i, 1)], conv[:, 2:3], ACT.Silu).then_inc(s.qkv, 1)

                def square(i):
                    act.activation(sq, k.feat[:, bass.ds(2 * i, 2)], ACT.Square).then_inc(s.squared, 1)

                def root(i):
                    act.wait_ge(s.summed, i + 1)
                    after(act, s.norm, 2 * i)
                    inverse_root(act, k, std[:], k.aux[0][:, 0:2 * T].rearrange("p (b t) -> p b t", b=2), 1.0, s.std, 2 * i)

                def branch_squares():
                    for n in range(B):
                        act.wait_ge(s.centred, n + 1)
                        act.activation(wide[:, n], acc[:, n], ACT.Square).then_inc(s.bsquared, 1)

                def branch_root():
                    act.wait_ge(s.bsquares, 1)
                    inverse_root(act, k, bstd[:], k.aux[3][:, 0:T], 1.0 / (B * P), s.bstd, 0)

                def branch_sigmoids():
                    for n in range(B):
                        act.wait_ge(s.bln, n + 1)
                        act.activation(wide[:, n], acc[:, n], ACT.Sigmoid, bias=bcol(P2_LNB + n)).then_inc(s.lsig, 1)

                def branch_round():
                    for n in range(B):
                        act.wait_ge(s.bsteps, n + 1)
                        act.activation(k.y_hi[:, 6 + n], acc[:, n], ACT.Copy).then_inc(s.byrounded, 1)

                def body(i, prev, last=False):
                    if prev:
                        inputs_2(i - 1)
                    if last:
                        branch_squares()
                    stream.round(act, i + 1, 0)
                    if prev:
                        await_convolution(i - 1)
                    stream.round(act, i + 1, 1)
                    if prev:
                        silu(i - 1)
                        act.wait_ge(s.qkv, 2 * i)
                    inputs(i)
                    if prev:
                        square(i - 1)
                    if last:
                        branch_root()
                    stream.round(act, i + 1, 2)
                    if prev:
                        root(i - 1)
                    if last:
                        branch_sigmoids()
                    stream.round(act, i + 1, 3)

                def tail(i):
                    inputs_2(i)
                    await_convolution(i)
                    silu(i)
                    act.wait_ge(s.qkv, 2 * i + 2)
                    square(i)
                    root(i)
                    branch_round()
                last_apart(act, H, body, tail, gates)

            @block.vector
            def _(dve):
                stream.open_dve(dve)
                dve.sem_inc(s.conv, 1)
                dve.memset(padded[:], 0.0).then_inc(s.cleared, 1)
                dve.wait_ge(s.rounded12, 1)
                dve.tensor_tensor(w12_lo[:], w12, w12_hi[:].bitcast(F32), ALU.subtract).then_inc(s.split12, 1)
                def gates():
                    link = chain(dve, s.chain)
                    dve.wait_ge(s.bg, 1)
                    dve.wait_ge(s.negexp, 1)
                    dve.wait_ge(s.exped, 2)
                    for b in range(2):
                        link(lambda: dve.tensor_tensor(x[:, b], k.aux[1][:, 16 * b + H:16 * b + 2 * H], rows[:, 1], ALU.add))
                    link(lambda: dve.tensor_scalar(t0, x, -1.0, None, ALU.mult))
                    link(lambda: dve.tensor_tensor(t0, t0, x, ALU.min))
                    dve.wait_ge(s.exped, 3)
                    softplus_tail(link, dve, x, t1, t0, t2)
                    for b in range(2):
                        link(lambda: dve.scalar_tensor_tensor(out=keep.g[:, b], in0=x[:, b], scalar=-1.0, in1=rows[:, 0],
                                                              op0=ALU.mult, op1=ALU.mult))

                dve.wait_ge(s.params, 16)

                def convolve(i):
                    dve.wait_ge(s.copied, 4 * i + 7)
                    after(dve, s.qkv, 2 * i)
                    for tap in range(TAPS_C):
                        for t in range(3):
                            c, src = conv[:, t], padded[:, t, tap:tap + T]
                            w = params[:, bass.ds(P2_CCONV + 3 * C_HEADS * tap + t + 3 * i, 1)]
                            if tap:
                                dve.wait_ge(s.conv, 12 * i + 1 + 3 * (tap - 1) + t + 1)
                                ins = dve.scalar_tensor_tensor(out=c, in0=src, scalar=w, in1=c, op0=ALU.mult, op1=ALU.add)
                            else:
                                ins = dve.tensor_scalar(c, src, w, None, ALU.mult)
                            ins.then_inc(s.conv, 1)

                def norm(i):
                    dve.wait_ge(s.std, 2 * i + 2)
                    q, key = k.feat[:, bass.ds(2 * i, 1)], k.feat[:, bass.ds(2 * i + 1, 1)]
                    dve.scalar_tensor_tensor(out=q, in0=q, scalar=C_DIM ** -0.5, in1=std[:, 0:1], op0=ALU.mult,
                                             op1=ALU.mult).then_inc(s.norm, 1)
                    dve.tensor_tensor(key, key, std[:, 1:2], ALU.mult).then_inc(s.norm, 1)

                def tap(i, n):
                    at = TAPS * i + n
                    for b in range(2):
                        dve.wait_ge(s.taps, 2 * at + b - 1)
                        dve.scalar_tensor_tensor(out=acc[:, 2 + b:3 + b], in0=branch.padded[:, 2 + b:3 + b, bass.ds(at, T)],
                                                 scalar=params[:, bass.ds(B * at + P2_BCONV + 2 + b, 1)],
                                                 in1=acc[:, 2 + b:3 + b], op0=ALU.mult, op1=ALU.add).then_inc(s.taps, 1)

                def branch_centre():
                    dve.wait_ge(s.bsummed, 1)
                    for n in range(B):
                        dve.scalar_tensor_tensor(out=acc[:, n], in0=k.aux[2][:, 0:T], scalar=-1.0 / (B * P), in1=acc[:, n],
                                                 op0=ALU.mult, op1=ALU.add).then_inc(s.centred, 1)

                def branch_norm():
                    dve.wait_ge(s.bstd, 2)
                    for n in range(B):
                        dve.scalar_tensor_tensor(out=acc[:, n], in0=acc[:, n], scalar=bcol(P2_LNW + n), in1=bstd[:],
                                                 op0=ALU.mult, op1=ALU.mult).then_inc(s.bln, 1)

                def branch_silu():
                    for n in range(B):
                        dve.wait_ge(s.lsig, n + 1)
                        dve.scalar_tensor_tensor(out=wide[:, n], in0=acc[:, n], scalar=bcol(P2_LNB + n), in1=wide[:, n],
                                                 op0=ALU.add, op1=ALU.mult).then_inc(s.hid, 1)

                def branch_gate():
                    for n in range(B):
                        dve.wait_ge(s.mixed, 2 * (n // 2) + 2)
                        dve.scalar_tensor_tensor(out=acc[:, n], in0=k.aux[2 + n // 2][:, T * (n % 2):T * (n % 2) + T],
                                                 scalar=bcol(P2_PWB + n), in1=branch.zgate[:, n], op0=ALU.add,
                                                 op1=ALU.mult).then_inc(s.bsteps, 1)

                def branch_split():
                    for n in range(B):
                        dve.wait_ge(s.byrounded, n + 1)
                        dve.tensor_tensor(k.y_lo[:, 6 + n], acc[:, n], k.y_hi[:, 6 + n].bitcast(F32), ALU.subtract)\
                           .then_inc(s.bylo, 1)

                tap_steps(dve, s.taps, 2, params, branch.padded, acc, 0, 1)

                def body(i, prev, last=False):
                    if last:
                        branch_centre()
                    if prev:
                        convolve(i - 1)
                    stream.residual(dve, i + 1, 0)
                    if not last:
                        tap(i, 1)
                        tap(i, 2)
                    stream.residual(dve, i + 1, 1)
                    if not last:
                        tap(i, 3)
                        tap(i, 4)
                    stream.residual(dve, i + 1, 2)
                    if last:
                        branch_norm()
                    else:
                        tap(i, 5)
                        tap(i, 6)
                    if last:
                        branch_silu()
                    stream.residual(dve, i + 1, 3)
                    if prev:
                        norm(i - 1)

                def tail(i):
                    convolve(i)
                    branch_gate()
                    norm(i)
                    branch_split()
                last_apart(dve, H, body, tail, gates)

            @block.tensor
            def _(pe):
                stream.open_pe(pe)
                pe.sem_inc(s.copied, 4)

                def gates():
                    pe.wait_ge(s.split12, 1)
                    for b in range(2):
                        n = 0
                        for kk in range(KT):
                            hi, lo = k.xn_hi[:, kk, P * b:P * b + P], k.xn_lo[:, kk, P * b:P * b + P]
                            for x_, w_ in ((hi, w12_hi[:, kk]), (hi, w12_lo[:, kk]), (lo, w12_hi[:, kk])):
                                ins = pe.matmul(k.aux[1][:, 16 * b:16 * b + 2 * H], x_, w_, start=n == 0, stop=n == 3 * KT - 1)
                                n += 1
                    ins.then_inc(s.bg, 1)

                def sums(i):
                    pe.wait_ge(s.squared, i + 1)
                    pe.matmul(k.aux[0][:, 0:2 * T], k.ones[:], sq, start=True, stop=True).then_inc(s.summed, 1)

                def branch_sum(bank, what):
                    for n in range(B):
                        ins = pe.matmul(bank[:, 0:T], k.ones[:], what[:, n], start=n == 0, stop=n == B - 1)
                    return ins

                def branch_product():
                    pe.wait_ge(s.pw, 16)
                    pe.wait_ge(s.hid, B)
                    for m in range(B):
                        for n in range(B):
                            ins = pe.matmul(k.aux[2 + m // 2][:, T * (m % 2):T * (m % 2) + T], pw[:, n, P * m:P * m + P],
                                            wide[:, n], start=n == 0, stop=n == B - 1)
                        ins.then_inc(s.mixed, 1)

                def body(i, prev, last=False):
                    if last:
                        pe.wait_ge(s.taps, 2 * TAPS_B)
                        branch_sum(k.aux[2], acc).then_inc(s.bsummed, 1)
                    pe.wait_ge(s.copied, 4 * i + 2)
                    stream.multiply(pe, i, 0, k.xn_hi, k.xn_lo)
                    if last:
                        pe.wait_ge(s.bsquared, B)
                        branch_sum(k.aux[3], wide).then_inc(s.bsquares, 1)
                    stream.multiply(pe, i, 1, k.xn_hi, k.xn_lo)
                    pe.wait_ge(s.copied, 4 * i + 4)
                    stream.multiply(pe, i, 2, k.xn_hi, k.xn_lo)
                    if prev:
                        sums(i - 1)
                    stream.multiply(pe, i, 3, k.xn_hi, k.xn_lo)
                    if last:
                        branch_product()
                last_apart(pe, H, body, sums, gates)


def delta_phase(k, layer, keep):
    nc = k.nc
    H, G = C_HEADS, C_HEADS // 2
    own = ("rows vturned kturned kk qk aturned decays grown masked vbeta kbeta amat intra acopied xstep bt ux ucopied xx uw wt "
           "zeroed ended ucopy gout vnew ws so sstate kvp sq osum rstd ysteps yrounded ylo")
    names = "consts cumulate_in sums scalars exps " + " ".join(f"{n}_{g}" for g in range(G) for n in own.split())
    with phase(nc, "delta", names) as s:
        group_sems = [dict(zip(own.split(), s.all[5 + g * len(own.split()):])) for g in range(G)]
        before, not_before = s.sbuf("before", [P, P]), s.sbuf("not_before", [P, P])
        cumulate = s.sbuf("cumulate", [P, P])
        levels, levels_t = s.sbuf("levels", [P, 6, P]), s.sbuf("levels_t", [P, 6, P])
        onorm = s.sbuf("onorm", [P, 2])
        cum = s.sbuf("cum", [P, 2, 2, H])
        sc = s.sbuf("sc", [P, 5, 2, H])
        ends = s.sbuf("ends", [P, G, 4, 2])
        CONSTS_IN = 5 * 16

        def quarters(x):
            x = x.rearrange("p a b -> p (a b)")
            return [x[:, 512 * n:512 * n + 512].rearrange("p (u t) -> p u t", u=4) for n in range(x.shape[1] // 512)]
        free = quarters(k.w_raw[:].rearrange("p a k n -> p (a k) n"))
        groups = []
        for g in range(G):
            mem = [free.pop() if free else s.sbuf(f"unit{g}_{n}", [P, 4, P])[:] for n in range(11)]
            A, AT, BT, X, XT, v_beta, k_end, k_beta, decay_t, grown, decay = mem
            heads = [2 * g, 2 * g + 1]
            groups.append(record(
                **group_sems[g], n=g, heads=heads, A=A, AT=AT, BT=BT, X=X, XT=XT, v_beta=v_beta, k_end=k_end, k_beta=k_beta,
                decay_t=decay_t, decay=decay, grown_=grown, UX=A, O=A, WT=AT, S=BT[:, 0:2], vn=BT[:, 2:4],
                R=XT, Y=X, intra_=decay_t, U=decay, b0=(k.z[0], k.z[2], k.aux[0])[g], b1=(k.z[1], k.z[3], k.aux[1])[g]))
        C = k.aux[3]

        def bank4(bank):
            return bank[:, 0:512].rearrange("p (u t) -> p u t", u=4)

        def flat(x):
            return x.rearrange("p u t -> p (u t)")

        def by_head(x):
            return flat(x).rearrange("p (h t) -> p h t", h=2)

        def masks(m):
            return m[:, None, :].to_broadcast([P, 4, P])

        def units(g):
            return [(u, u // 2, g.heads[u % 2], slice(P * (u // 2), P * (u // 2) + P)) for u in range(4)]

        def part(bank, u):
            return bank[:, P * u:P * u + P]

        with nc.Block() as block:
            @block.sync
            def _(sp):
                sp.dma_start(cumulate[:], constant(k, "cumulate")).then_inc(s.cumulate_in, 16)
                for t, name in ((before, "before"), (not_before, "not_before")):
                    sp.dma_start(t[:], constant(k, name)).then_inc(s.consts, 16)
                sp.dma_start(levels[:].rearrange("p l t -> p (l t)"), constant(k, "levels")).then_inc(s.consts, 16)
                sp.dma_start(levels_t[:].rearrange("p l t -> p (l t)"), constant(k, "levels_t")).then_inc(s.consts, 16)
                sp.dma_start(onorm[:], k.p2[bass.ds(layer, 1), :, P2_ONORM:P2_ONORM + 2].rearrange("a p n -> p (a n)"))\
                  .then_inc(s.consts, 16)
                sp.wait_ge(s.consts, CONSTS_IN)
                sp.wait_ge(s.cumulate_in, 16)

            @block.scalar
            def _(act):
                act.wait_ge(s.scalars, 3)
                act.activation(sc[:, 0], cum[:, 0], ACT.Exp).then_inc(s.exps, 1)
                act.activation(sc[:, 1], sc[:, 4], ACT.Exp).then_inc(s.exps, 1)
                for g in groups:
                    act.wait_ge(g.rows, 1)
                    act.activation(g.grown_, bank4(g.b0), ACT.Exp).then_inc(g.grown, 1)
                for g in groups:
                    act.wait_ge(g.masked, 1)
                    for u, r, h, _ in units(g):
                        act.activation(g.decay[:, u], g.decay[:, u], ACT.Exp, bias=cum[:, 0, r, h:h + 1]).then_inc(g.decays, 1)
                for g in groups:
                    act.wait_ge(g.masked, 2)
                    for u, r, h, _ in units(g):
                        act.activation(g.decay_t[:, u], g.decay_t[:, u], ACT.Exp, bias=sc[:, 3, r, h:h + 1]).then_inc(g.decays, 1)
                for g in groups:
                    act.wait_ge(g.aturned, 1)
                    act.activation(g.AT, bank4(g.b1), ACT.Copy).then_inc(g.acopied, 1)
                for level in range(1, 6):
                    for g in groups:
                        act.wait_ge(g.ux, level)
                        act.activation(g.UX, bank4(g.b0), ACT.Copy).then_inc(g.ucopied, 1)
                for g in groups:
                    act.wait_ge(g.uw, 1)
                    act.activation(g.U, bank4(g.b0), ACT.Copy).then_inc(g.ucopy, 1)
                for g in groups:
                    act.wait_ge(g.so, 8)
                    act.activation(g.UX, bank4(g.b1), ACT.Square).then_inc(g.sq, 1)
                for g in groups:
                    act.wait_ge(g.osum, 1)
                    act.activation(g.R, bank4(g.b0), ACT.Ln, bias=k.eps[:], scale=1.0 / C_DIM).then_inc(g.rstd, 1)
                for g in groups:
                    act.wait_ge(g.rstd, 1)
                    act.activation(g.R, g.R, ACT.Exp, scale=-0.5).then_inc(g.rstd, 1)
                for g in groups:
                    act.wait_ge(g.ysteps, 2)
                    act.activation(k.y_hi[:, 10 + 2 * g.n:12 + 2 * g.n], by_head(g.Y), ACT.Copy).then_inc(g.yrounded, 1)

            @block.tensor
            def _(pe):
                pe.wait_ge(s.cumulate_in, 16)
                pe.matmul(C[:, 0:2 * H], cumulate[:], keep.g[:].rearrange("p r h -> p (r h)"), start=True, stop=True)\
                  .then_inc(s.sums, 1)
                pe.matmul(C[:, 2 * H:4 * H], k.blocks[:], keep.g[:].rearrange("p r h -> p (r h)"), start=True, stop=True)\
                  .then_inc(s.sums, 1)
                for g in groups:
                    for u, r, h, _ in units(g):
                        ins = pe.matmul(part(g.b0, u), keep.g[:, r, h:h + 1].to_broadcast([P, P]), cumulate[:], start=True,
                                        stop=True)
                    ins.then_inc(g.rows, 1)
                    for u, r, h, t in units(g):
                        ins = pe.transpose(part(g.b1, u), keep.v_all[:, h, t], k.ident[:])
                    ins.then_inc(g.vturned, 1)
                for g in groups:
                    pe.wait_ge(g.masked, 2)
                    for u, r, h, t in units(g):
                        ins = pe.transpose(part(g.b0, u), k.feat[:, 2 * h + 1, t], k.ident[:])
                    ins.then_inc(g.kturned, 1)
                for g in groups:
                    pe.wait_ge(g.vbeta, 4)
                    for u, r, h, t in units(g):
                        ins = pe.matmul(part(g.b1, u), k.feat[:, 2 * h + 1, t], k.feat[:, 2 * h + 1, t], start=True, stop=True)
                    ins.then_inc(g.kk, 1)
                for g in groups:
                    pe.wait_ge(g.kbeta, 8)
                    for u, r, h, t in units(g):
                        ins = pe.matmul(part(g.b0, u), k.feat[:, 2 * h + 1, t], k.feat[:, 2 * h, t], start=True, stop=True)
                    ins.then_inc(g.qk, 1)
                for g in groups:
                    pe.wait_ge(g.amat, 4)
                    for u in range(4):
                        ins = pe.transpose(part(g.b1, u), g.A[:, u], k.ident[:])
                    ins.then_inc(g.aturned, 1)
                for level in range(1, 6):
                    for g in groups:
                        if level == 1:
                            pe.wait_ge(g.intra, 1)
                        pe.wait_ge(g.bt, level)
                        pe.wait_ge(g.xstep, 2 * level + 2)
                        for u in range(4):
                            ins = pe.matmul(part(g.b0, u), g.BT[:, u], g.X[:, u], start=True, stop=True)
                        ins.then_inc(g.ux, 1)
                    for g in groups:
                        pe.wait_ge(g.ucopied, level)
                        for u in range(4):
                            ins = pe.matmul(part(g.b1, u), g.XT[:, u], g.UX[:, u], start=True, stop=True)
                        ins.then_inc(g.xx, 1)
                        for u in range(4):
                            ins = pe.matmul(part(g.b0, u), g.UX[:, u], g.XT[:, u], start=True, stop=True)
                        ins.then_inc(g.xx, 1)
                for g in groups:
                    pe.wait_ge(g.xstep, 14)
                    for u in range(4):
                        ins = pe.matmul(part(g.b0, u), g.XT[:, u], g.v_beta[:, u], start=True, stop=True)
                    ins.then_inc(g.uw, 1)
                    for u in range(4):
                        ins = pe.matmul(part(g.b1, u), g.k_beta[:, u], g.XT[:, u], start=True, stop=True)
                    ins.then_inc(g.uw, 1)
                for c in range(4):
                    r, off = c // 2, (c % 2) * CHUNK
                    rows = slice(off, off + CHUNK)
                    for g in groups:
                        if c == 0:
                            pe.wait_ge(g.zeroed, 2)
                            pe.wait_ge(g.wt, 1)
                            pe.wait_ge(g.ucopy, 1)
                        else:
                            pe.wait_ge(g.sstate, 2 * c)
                        for h in range(2):
                            ins = pe.matmul(g.b0[rows, P * h:P * h + P], g.WT[:, 2 * r + h, rows], g.S[:, h], start=True, stop=True)
                        ins.then_inc(g.ws, 1)
                    for g in groups:
                        if c == 0:
                            pe.wait_ge(g.gout, 2)
                        pe.wait_ge(g.vnew, c + 1)
                        for h in range(2):
                            ins = pe.matmul(g.b0[:, T + P * h:T + P * h + P], g.k_end[rows, 2 * r + h], g.vn[rows, h], start=True,
                                            stop=True)
                        ins.then_inc(g.kvp, 1)
                        for h in range(2):
                            u = 2 * r + h
                            out = g.b1[:, T * h + CHUNK * c:T * h + CHUNK * c + CHUNK]
                            pe.matmul(out, g.S[:, h], g.grown_[:, u, rows], start=True, stop=False)
                            pe.matmul(out, g.vn[:, h], g.intra_[:, u, rows], start=False, stop=True).then_inc(g.so, 1)
                for g in groups:
                    pe.wait_ge(g.sq, 1)
                    pe.wait_ge(g.sstate, 8)
                    pe.matmul(g.b0[:, 0:2 * T], k.ones[:], flat(g.UX), start=True, stop=True).then_inc(g.osum, 1)

            @block.vector
            def _(dve):
                dve.wait_ge(s.sums, 2)
                dve.tensor_copy(cum[:].rearrange("p a r h -> p (a r h)"), C[:, 0:4 * H]).then_inc(s.scalars, 1)
                dve.wait_ge(s.scalars, 1)
                dve.tensor_scalar(sc[:, 3], cum[:, 0], -1.0, None, ALU.mult).then_inc(s.scalars, 1)
                dve.tensor_tensor(sc[:, 4], cum[:, 1], cum[:, 0], ALU.subtract).then_inc(s.scalars, 1)
                dve.wait_ge(s.exps, 1)
                dve.tensor_tensor(sc[:, 2], sc[:, 0], keep.beta[:], ALU.mult).then_inc(s.scalars, 1)
                dve.wait_ge(s.consts, CONSTS_IN)
                for g in groups:
                    dve.wait_ge(g.grown, 1)
                    dve.scalar_tensor_tensor(out=g.decay, in0=bank4(g.b0), scalar=-1.0, in1=masks(before), op0=ALU.mult,
                                             op1=ALU.add).then_inc(g.masked, 1)
                    dve.tensor_tensor(g.decay_t, bank4(g.b0), masks(not_before), ALU.add).then_inc(g.masked, 1)
                for g in groups:
                    dve.wait_ge(g.vturned, 1)
                    for u, r, h, _ in units(g):
                        dve.tensor_scalar(g.v_beta[:, u], part(g.b1, u), keep.beta[:, r, h:h + 1], None, ALU.mult)\
                           .then_inc(g.vbeta, 1)
                dve.wait_ge(s.scalars, 4)
                dve.wait_ge(s.exps, 2)
                for g in groups:
                    dve.wait_ge(g.kturned, 1)
                    for u, r, h, _ in units(g):
                        dve.tensor_scalar(g.k_beta[:, u], part(g.b0, u), sc[:, 2, r, h:h + 1], None, ALU.mult).then_inc(g.kbeta, 1)
                        dve.tensor_scalar(g.k_end[:, u], part(g.b0, u), sc[:, 1, r, h:h + 1], None, ALU.mult).then_inc(g.kbeta, 1)
                for g in groups:
                    dve.wait_ge(g.kk, 1)
                    dve.wait_ge(g.decays, 4)
                    for u, r, h, _ in units(g):
                        dve.scalar_tensor_tensor(out=g.A[:, u], in0=part(g.b1, u), scalar=keep.beta[:, r, h:h + 1],
                                                 in1=g.decay[:, u], op0=ALU.mult, op1=ALU.mult).then_inc(g.amat, 1)
                for g in groups:
                    dve.wait_ge(g.qk, 1)
                    dve.wait_ge(g.decays, 8)
                    dve.tensor_tensor(g.intra_, bank4(g.b0), g.decay_t, ALU.mult).then_inc(g.intra, 1)
                for g in groups:
                    dve.wait_ge(g.amat, 4)
                    dve.tensor_tensor(g.X, g.A, masks(levels[:, 0]), ALU.mult).then_inc(g.xstep, 1)
                    dve.wait_ge(g.xstep, 1)
                    dve.tensor_tensor(g.X, g.X, masks(k.ident), ALU.add).then_inc(g.xstep, 1)
                for g in groups:
                    dve.wait_ge(g.acopied, 1)
                    dve.tensor_tensor(g.BT, g.AT, masks(levels_t[:, 1]), ALU.mult).then_inc(g.bt, 1)
                    dve.tensor_tensor(g.XT, g.AT, masks(levels_t[:, 0]), ALU.mult).then_inc(g.xstep, 1)
                    dve.wait_ge(g.xstep, 3)
                    dve.tensor_tensor(g.XT, g.XT, masks(k.ident), ALU.add).then_inc(g.xstep, 1)
                for level in range(1, 6):
                    for g in groups:
                        if level < 5:
                            dve.wait_ge(g.ux, level)
                            dve.tensor_tensor(g.BT, g.AT, masks(levels_t[:, level + 1]), ALU.mult).then_inc(g.bt, 1)
                    for g in groups:
                        dve.wait_ge(g.xx, 2 * level - 1)
                        dve.wait_ge(g.xstep, 2 * level + 2)
                        dve.tensor_tensor(g.X, bank4(g.b1), g.X, ALU.add).then_inc(g.xstep, 1)
                        dve.wait_ge(g.xx, 2 * level)
                        dve.tensor_tensor(g.XT, bank4(g.b0), g.XT, ALU.add).then_inc(g.xstep, 1)
                for g in groups:
                    dve.memset(g.S, 0.0).then_inc(g.zeroed, 1)
                    dve.memset(g.vn, 0.0).then_inc(g.zeroed, 1)
                    dve.wait_ge(g.grown, 1)
                    dve.tensor_copy(ends[:, g.n], g.grown_[:, :, CHUNK - 1::CHUNK]).then_inc(g.ended, 1)
                    dve.wait_ge(g.ended, 1)
                    for h in range(2):
                        q = k.feat[:, 2 * g.heads[h]].rearrange("p (r t) -> p r t", r=2)
                        grown = g.grown_.rearrange("p (r h) t -> p r h t", r=2)[:, :, h]
                        dve.tensor_tensor(grown, q, grown, ALU.mult).then_inc(g.gout, 1)
                for g in groups:
                    dve.wait_ge(g.uw, 2)
                    dve.tensor_copy(g.WT, bank4(g.b1)).then_inc(g.wt, 1)
                for c in range(4):
                    r, off = c // 2, (c % 2) * CHUNK
                    rows = slice(off, off + CHUNK)
                    for g in groups:
                        dve.wait_ge(g.ws, c + 1)
                        if c:
                            dve.wait_ge(g.so, 2 * c)
                        else:
                            dve.wait_ge(g.zeroed, 2)
                            dve.wait_ge(g.ucopy, 1)
                        dve.tensor_tensor(g.vn[rows], g.U[rows, 2 * r:2 * r + 2],
                                          g.b0[rows, 0:2 * P].rearrange("p (h t) -> p h t", h=2), ALU.subtract).then_inc(g.vnew, 1)
                    for g in groups:
                        dve.wait_ge(g.kvp, c + 1)
                        dve.wait_ge(g.so, 2 * c + 2)
                        for h in range(2):
                            dve.scalar_tensor_tensor(out=g.S[:, h], in0=g.S[:, h], scalar=ends[:, g.n, 2 * r + h, c % 2:c % 2 + 1],
                                                     in1=g.b0[:, T + P * h:T + P * h + P], op0=ALU.mult, op1=ALU.add)\
                               .then_inc(g.sstate, 1)
                for g in groups:
                    dve.wait_ge(g.rstd, 2)
                    dve.scalar_tensor_tensor(out=flat(g.O), in0=g.b1[:, 0:512], scalar=onorm[:, 0:1], in1=flat(g.R), op0=ALU.mult,
                                             op1=ALU.mult).then_inc(g.ysteps, 1)
                    dve.wait_ge(g.ysteps, 1)
                    dve.tensor_tensor(by_head(g.Y), by_head(g.O), keep.z_all[:, 2 * g.n:2 * g.n + 2], ALU.mult).then_inc(g.ysteps, 1)
                for g in groups:
                    dve.wait_ge(g.yrounded, 1)
                    dve.tensor_tensor(k.y_lo[:, 10 + 2 * g.n:12 + 2 * g.n], by_head(g.Y),
                                      k.y_hi[:, 10 + 2 * g.n:12 + 2 * g.n].bitcast(F32), ALU.subtract).then_inc(g.ylo, 1)


def out_phase_1(k, x_dram):
    nc = k.nc
    with phase(nc, "out1", STREAM + "params xin merged_hi merged_lo copied acc sq summed rstd norm step cleared") as s:
        stream = Stream(k, s, SLOT_OUT_1)
        o = s.sbuf("o", [P, KT, T])
        acc, sq = s.sbuf("acc", [P, T]), s.sbuf("sq", [P, 4, T])
        rstd = s.sbuf("rstd", [P, T])
        w = s.sbuf("w", [P, KT])
        passes = KT // 4
        with nc.Block() as block:
            @block.sync
            def _(sp):
                sp.dma_start(w[:], k.p1[:, P1_POST:P1_POST + KT]).then_inc(s.params, 16)
                sp.wait_ge(s.merged_lo, 4)
                sp.dma_start(k.feat[:], x_dram).then_inc(s.xin, 16)
                stream.loads(sp, passes)

            @block.scalar
            def _(act):
                stream.open_act(act)
                for q in range(4):
                    act.activation(k.xn_hi[:, 4 * q:4 * q + 4], k.feat[:, 4 * q:4 * q + 4], ACT.Copy).then_inc(s.merged_hi, 1)

                def copies(i, half):
                    act.wait_ge(s.used, stream.done(i, 2 * half + 1))
                    act.wait_ge(s.acc, 4 * i + 2 * half + 2)
                    for b in (2 * half, 2 * half + 1):
                        act.activation(sq[:, b], k.z[b][:, 0:T], ACT.Square).then_inc(s.sq, 1)
                    for b in (2 * half, 2 * half + 1):
                        act.activation(o[:, bass.ds(4 * i + b, 1)], k.z[b][:, None, 0:T], ACT.Copy).then_inc(s.copied, 1)

                def body(i, prev):
                    if prev:
                        copies(i - 1, 1)
                    stream.round(act, i + 1, 0)
                    stream.round(act, i + 1, 1)
                    copies(i, 0)
                    stream.round(act, i + 1, 2)
                    stream.round(act, i + 1, 3)
                run_passes(act, passes, body, lambda i: copies(i, 1))
                act.wait_ge(s.summed, 1)
                inverse_root(act, k, rstd[:], k.aux[0][:, 0:T], 1.0 / D, s.rstd, 0)

            @block.vector
            def _(dve):
                stream.open_dve(dve)
                dve.sem_inc(s.acc, 4)
                dve.memset(acc[:], 0.0).then_inc(s.cleared, 1)
                dve.wait_ge(s.cleared, 1)
                for q in range(4):
                    dve.wait_ge(s.merged_hi, q + 1)
                    dve.tensor_tensor(k.xn_lo[:, 4 * q:4 * q + 4], k.feat[:, 4 * q:4 * q + 4],
                                      k.xn_hi[:, 4 * q:4 * q + 4].bitcast(F32), ALU.subtract).then_inc(s.merged_lo, 1)

                def sums(i, half):
                    dve.wait_ge(s.sq, 4 * i + 2 * half + 2)
                    for b in (2 * half, 2 * half + 1):
                        dve.tensor_tensor(acc[:], acc[:], sq[:, b], ALU.add).then_inc(s.acc, 1)
                        dve.wait_ge(s.acc, 4 * i + 5 + b)

                def body(i, prev):
                    if prev:
                        sums(i - 1, 1)
                    stream.residual(dve, i + 1, 0)
                    stream.residual(dve, i + 1, 1)
                    sums(i, 0)
                    stream.residual(dve, i + 1, 2)
                    stream.residual(dve, i + 1, 3)
                run_passes(dve, passes, body, lambda i: sums(i, 1))
                dve.wait_ge(s.rstd, 2)
                dve.wait_ge(s.params, 16)
                dve.wait_ge(s.xin, 16)
                for t in range(KT):
                    dve.scalar_tensor_tensor(out=o[:, t], in0=o[:, t], scalar=w[:, t:t + 1], in1=rstd[:], op0=ALU.mult,
                                             op1=ALU.mult).then_inc(s.norm, 1)
                for q in range(4):
                    dve.wait_ge(s.norm, 4 * q + 4)
                    f = k.feat[:, 4 * q:4 * q + 4]
                    dve.tensor_tensor(f, f, o[:, 4 * q:4 * q + 4], ALU.add).then_inc(s.step, 1)

            @block.tensor
            def _(pe):
                stream.open_pe(pe)
                pe.sem_inc(s.copied, 4)

                def products(i, prev):
                    for sl in range(SLOTS):
                        if not prev and sl < 2:
                            pe.wait_ge(s.merged_lo, 2 * sl + 2)
                        if sl % 2 == 0:
                            pe.wait_ge(s.copied, 4 * i + 2 + sl)
                        stream.multiply(pe, i, sl, k.xn_hi, k.xn_lo)
                run_passes(pe, passes, products)
                pe.wait_ge(s.acc, 4 * passes + 4)
                pe.matmul(k.aux[0][:, 0:T], k.ones[:], acc[:], start=True, stop=True).then_inc(s.summed, 1)


def out_phase_2(k, layer, state, out):
    nc = k.nc
    with phase(nc, "out2", STREAM + "xin added stored") as s:
        stream = Stream(k, s, layer * SLOTS_2 + SLOTS_1 + SLOT_OUT_2)
        passes = KT // 4
        with nc.Block() as block:
            @block.sync
            def _(sp):
                sp.dma_start(k.feat[:], state).then_inc(s.xin, 16)

                def store(i):
                    sp.wait_ge(s.added, 4 * i + 8)
                    sp.dma_start(out[:, bass.ds(4 * i, 4)], k.feat[:, bass.ds(4 * i, 4)]).then_inc(s.stored, 16)

                def body(i, prev):
                    stream.load(sp, i + 1, 0)
                    stream.load(sp, i + 1, 1)
                    if prev:
                        store(i - 1)
                    stream.load(sp, i + 1, 2)
                    stream.load(sp, i + 1, 3)
                run_passes(sp, passes, body, store)
                sp.wait_ge(s.stored, 16 * passes)

            @block.scalar
            def _(act):
                stream.open_act(act)
                with act.Fori(1, passes + 1) as i:
                    for n in range(SLOTS):
                        stream.round(act, i, n)

            @block.vector
            def _(dve):
                stream.open_dve(dve)

                def add(i, half):
                    for b in (2 * half, 2 * half + 1):
                        dve.wait_ge(s.used, stream.done(i, 2 * half + 1))
                        f = k.feat[:, bass.ds(4 * i + b, 1)]
                        dve.tensor_tensor(f, k.z[b][:, None, 0:T], f, ALU.add).then_inc(s.added, 1)

                def body(i, prev):
                    if prev:
                        add(i - 1, 1)
                    stream.residual(dve, i + 1, 0)
                    stream.residual(dve, i + 1, 1)
                    if not prev:
                        dve.wait_ge(s.xin, 16)
                    add(i, 0)
                    stream.residual(dve, i + 1, 2)
                    stream.residual(dve, i + 1, 3)
                run_passes(dve, passes, body, lambda i: add(i, 1))

            @block.tensor
            def _(pe):
                stream.open_pe(pe)
                pe.sem_inc(s.added, 4)

                def products(i, prev):
                    for sl in range(SLOTS):
                        if sl % 2 == 0:
                            pe.wait_ge(s.added, 4 * i + 2 + sl)
                        stream.multiply(pe, i, sl, k.y_hi, k.y_lo)
                run_passes(pe, passes, products)


class Kernel:
    pass


def build(nc, t):
    with ExitStack() as stack:
        def sbuf(name, shape, dt=F32):
            return stack.enter_context(nc.sbuf_tensor(name, shape, dt))
        k = Kernel()
        k.nc = nc
        k.constants, k.w, k.p1, k.p2 = t["constants"], t["w"], t["p1"], t["p2"]
        k.lru_w, k.pw, k.w12, k.rows_c = t["lru_w"], t["pw"], t["w12"], t["rows_c"]
        k.w_raw = sbuf("w_raw", [P, RAW, SLOT_K, CHUNK_COLS])
        k.w_hi = sbuf("w_hi", [P, SLOTS, SLOT_K, CHUNK_COLS], F32R)
        k.w_lo = sbuf("w_lo", [P, SLOTS, SLOT_K, CHUNK_COLS], F32R)
        k.y_hi, k.y_lo = sbuf("y_hi", [P, KT, T], F32R), sbuf("y_lo", [P, KT, T], F32R)
        k.feat = sbuf("feat", [P, KT, T])
        k.ident, k.ones, k.blocks = sbuf("ident", [P, P]), sbuf("ones", [P, P]), sbuf("blocks", [P, P])
        k.eps = sbuf("eps", [P, 1])
        k.cos_t, k.sin_t = sbuf("cos_t", [P, T]), sbuf("sin_t", [P, T])
        k.z = [stack.enter_context(nc.psum_tensor(f"z{n}", [P, 2 * T], F32)) for n in range(4)]
        k.aux = [stack.enter_context(nc.psum_tensor(f"aux{n}", [P, 2 * T], F32)) for n in range(4)]

        def normed(name, scope):
            k.xn_hi, k.xn_lo = (scope.enter_context(nc.sbuf_tensor(f"{name}_{part}", [P, KT, T], F32R)) for part in ("hi", "lo"))

        first = stack.enter_context(ExitStack())
        normed("xn_1", first)
        norm_phase(k, "norm1", t["p1"][:, P1_NORM:P1_NORM + KT], t["x"], None, True)
        lru_phase(k)
        merge_phase(k, "merge_a", SLOT_MERGE_A, True, None, "freq_1")
        attention_phase(k, "att1", record(
            heads_per_tile=1, n_heads=16, passes=8, first_slot=SLOT_ATT_1, kv_width=512, turn="turn_1",
            mask="window_1", sinks=t["sinks_1"], norms=None, scale=HEAD_DIM_1 ** -0.5))
        merge_phase(k, "merge_b", SLOT_MERGE_B, False, t["positions"], "freq_2")
        out_phase_1(k, t["x"])
        first.close()
        with nc.Fori(0, LAYERS) as layer:
            with ExitStack() as kept:
                keep = record(**{n: kept.enter_context(nc.sbuf_tensor(f"keep_{n}", shape, F32)) for n, shape in (
                    ("v_all", [P, C_HEADS, T]), ("z_all", [P, C_HEADS, T]), ("beta", [P, 2, C_HEADS]), ("g", [P, 2, C_HEADS]))})
                with ExitStack() as second:
                    normed("xn_2", second)
                    norm_phase(k, "norm2", t["p2"][bass.ds(layer, 1), :, P2_NORM:P2_NORM + KT].rearrange("a p n -> p (a n)"),
                               None, t["state"])
                    attention_phase(k, "att2", record(
                        heads_per_tile=2, n_heads=HEADS_2, passes=3, first_slot=layer * SLOTS_2 + SLOTS_1 + SLOT_ATT_2,
                        kv_width=256, turn="turn_2", mask="window_2", sinks=t["sinks_2"][bass.ds(layer, 1)],
                        norms=t["p2"][bass.ds(layer, 1), :, P2_QN:P2_KN + 1].rearrange("a p n -> p (a n)"),
                        scale=HEAD_DIM_2 ** -0.5))
                    branch = record(**{n: second.enter_context(nc.sbuf_tensor(f"branch_{n}", [P, B_TILES, width], F32))
                                       for n, width in (("padded", TAPS_B - 1 + T), ("zgate", T))})
                    conv_phase(k, layer, branch)
                    delta_inputs_phase(k, layer, keep, branch)
                delta_phase(k, layer, keep)
            out_phase_2(k, layer, t["state"], t["out"])


def slots_of(matrix, column_tiles):
    out = []
    for a, b in zip(column_tiles[0::2], column_tiles[1::2]):
        chunk = np.concatenate([matrix[:, a:a + P], matrix[:, b:b + P]], 1)
        halves = chunk.reshape(2, SLOT_K, P, CHUNK_COLS).transpose(0, 2, 1, 3)
        out.append(halves.reshape(2, P, SLOT_K * CHUNK_COLS))
    return np.concatenate(out, 0)


def tiles(start, n):
    return [start + P * j for j in range(n)]


def by_partition(v):
    v = np.asarray(v)
    return v.reshape(-1, P).T


def lay_out(x, norm_pre_w, w_in, conv_w, conv_b, lru_w_r, lru_b_r, lru_w_i, lru_b_i, lru_lambda, attn_sink, w_proj_a,
            w_proj_b, w_out, norm_post_w, positions_2, norm_w_2, w_in_2, q_norm_w_2, k_norm_w_2, sinks_2, b_conv_w_2,
            b_conv_b_2, b_ln_w_2, b_ln_b_2, b_pw_w_2, b_pw_b_2, c_conv_w_2, c_a_log_2, c_dt_bias_2, c_onorm_w_2, w_out_2):
    a = {"x": x[0].T.reshape(KT, P, T).transpose(1, 0, 2)}
    u0, g0, q0 = 0, D, 2 * D
    k0, v0 = 3 * D, 3 * D + 512
    ga0, ml0, ma0 = 3 * D + 1024, 4 * D + 1024, 5 * D + 1024
    w = w_in[0]
    lru = [c for i in range(8) for s in (u0, g0) for c in tiles(s + 256 * i, 2)]
    att = tiles(k0, 4) + tiles(v0, 4) + [c for i in range(8) for s in (q0, ga0) for c in tiles(s + 256 * i, 2)]

    def merged(m0, proj):
        m, p_ = slots_of(w, tiles(m0, KT)), slots_of(proj, tiles(0, KT))
        return np.stack([m.reshape(8, 2, P, -1), p_.reshape(8, 2, P, -1)], 1).reshape(32, P, -1)
    w_1 = np.concatenate([slots_of(w, lru), merged(ml0, w_proj_a[0]), slots_of(w, att), merged(ma0, w_proj_b[0]),
                              slots_of(w_out[0], tiles(0, KT))], 0)
    a["p1"] = np.concatenate([by_partition(v) for v in (norm_pre_w, conv_w, conv_b, lru_b_r, lru_b_i, lru_lambda, norm_post_w)], 1)
    lw = np.stack([lru_w_r[0], lru_w_i[0]], 0)
    a["lru_w"] = lw.transpose(2, 3, 1, 0, 4).reshape(8, 2, P, 4, P).transpose(0, 2, 1, 3, 4).reshape(8, P, 8 * P)
    a["sinks_1"] = attn_sink
    a["sinks_2"] = sinks_2
    a["positions"] = positions_2
    widths = (768, 256, 256, 768, 512, 512, 512, 768, 768, 768, 6, 6, 768)
    q_, k_, v_, za, ba, bg, zb, cq, ck, cv, b_, a_, zc = np.cumsum((0,) + widths[:-1]).tolist()
    order = tiles(k_, 2) + tiles(v_, 2) + [c for i in range(3) for s in (q_, za) for c in tiles(s + 256 * i, 2)]
    order += tiles(ba, 2) + tiles(bg, 2) + tiles(ba + 256, 2) + tiles(bg + 256, 2) + tiles(zb, 4)
    order += [s + P * h for h in range(C_HEADS) for s in (cq, ck, cv, zc)]
    w_2 = [np.concatenate([slots_of(w_in_2[l], order), slots_of(w_out_2[l], tiles(0, KT))], 0) for l in range(LAYERS)]
    a["w"] = np.concatenate([w_1] + w_2 + [w_1[:SLOTS]], 0)
    a["w12"] = w_in_2[:, :, b_:b_ + 12].reshape(LAYERS, KT, P, 12).transpose(0, 2, 1, 3).reshape(LAYERS, P, KT * 12)
    rows = []
    for l in range(LAYERS):
        qn, kn = (np.concatenate([v[l], v[l]])[:, None] for v in (q_norm_w_2, k_norm_w_2))
        cc = c_conv_w_2[l].reshape(TAPS_C, 3, C_HEADS, P).transpose(3, 0, 2, 1).reshape(P, -1)
        rows.append(np.concatenate([by_partition(norm_w_2[l]), qn, kn, c_onorm_w_2[l][:, None], by_partition(b_conv_w_2[l]),
                                    by_partition(b_conv_b_2[l]), by_partition(b_ln_w_2[l]), by_partition(b_ln_b_2[l]),
                                    by_partition(b_pw_b_2[l]), cc], 1))
    a["p2"] = np.stack(rows, 0)
    a["pw"] = b_pw_w_2.reshape(LAYERS, B_TILES, P, B_TILES * P).transpose(0, 2, 1, 3).reshape(LAYERS, P, -1)
    a["rows_c"] = np.concatenate([c_a_log_2, c_dt_bias_2], 1)
    a["constants"] = CONSTANTS
    return {n: np.ascontiguousarray(v) for n, v in a.items()}


def kernel(**inputs):
    import concourse.bacc as bacc
    from concourse.bass_utils import run_bass_kernel_spmd

    arrays = lay_out(**{n: np.asarray(v) for n, v in inputs.items()})
    nc = bacc.Bacc("TRN2", target_bir_lowering=False, num_devices=1)
    t = {n: nc.dram_tensor(f"in_{n}_dram", v.shape, mybir.dt.from_np(v.dtype), kind="ExternalInput").ap()
         for n, v in arrays.items()}
    t["out"] = nc.dram_tensor("out_0_dram", (P, KT, T), F32, kind="ExternalOutput").ap()
    t["state"] = nc.dram_tensor("state_dram", (P, KT, T), F32, kind="Internal").ap()
    build(nc, t)
    r = run_bass_kernel_spmd(nc, [{f"in_{n}_dram": v for n, v in arrays.items()}], core_ids=[0])
    y = r.results[0]["out_0_dram"]
    return np.ascontiguousarray(y.transpose(2, 1, 0).reshape(1, T, D))
```
